# Optimizing a Trainium2 kernel written in Bass

```python
import jax, jax.numpy as jnp
from jax import lax
import numpy as np
import math

D_MODEL = 1024
BATCH = 1
SEQ = 256
DEPTH = 1

FOURIER_GROUPS = 4
FOURIER_GROUP_DIM = 128
D_FOURIER = FOURIER_GROUPS * FOURIER_GROUP_DIM
D_CONV = D_MODEL
CONV_WIDTH = 3
N_BRANCHES = 2
D_IN_PROJ = D_FOURIER + 3 * D_CONV + N_BRANCHES * D_MODEL
N_EXPERTS = 16
EC_CAPACITY = 2
D_EXPERT = 2048
N_MOD = 6
RMS_EPS = 1e-6


def rms_norm(x, g):
    xf = x.astype(jnp.float32)
    y = xf * lax.rsqrt(jnp.mean(xf * xf, axis=-1, keepdims=True) + RMS_EPS)
    return (y * g.astype(jnp.float32)).astype(x.dtype)

def modulate(h, shift, scale):
    return h * (1 + scale[:, None, :]) + shift[:, None, :]

def fourier_mix(u):
    b, s, _ = u.shape
    ug = u.reshape(b, s, FOURIER_GROUPS, FOURIER_GROUP_DIM).astype(jnp.float32)
    f = jnp.fft.fftn(ug, axes=(1, 3), norm="ortho")
    return jnp.real(f).reshape(b, s, D_FOURIER).astype(u.dtype)

def centred_conv3(u, w):
    s = u.shape[1]
    up = jnp.pad(u, ((0, 0), (1, 1), (0, 0)))
    return up[:, 0:s] * w[0] + up[:, 1:s + 1] * w[1] + up[:, 2:s + 2] * w[2]

def expert_choice_moe(h, w_router, b_router, w_gate_e, w_up_e, w_down_e):
    b, s, d = h.shape
    cap = EC_CAPACITY * s // N_EXPERTS
    logits = jnp.einsum('bsd,de->bse', h, w_router).astype(jnp.float32) + b_router.astype(jnp.float32)
    probs = jax.nn.softmax(logits, axis=-1)
    vals, idx = lax.top_k(jnp.swapaxes(probs, 1, 2), cap)
    xe = jax.vmap(lambda hb, ib: hb[ib])(h, idx)
    a = jnp.einsum('becd,edf->becf', xe, w_gate_e)
    u = jnp.einsum('becd,edf->becf', xe, w_up_e)
    y = jnp.einsum('becf,efd->becd', jax.nn.silu(a) * u, w_down_e)
    y = y * vals[..., None].astype(y.dtype)
    return jax.vmap(lambda yb, ib: jnp.zeros((s, d), yb.dtype).at[ib.reshape(-1)].add(yb.reshape(-1, d)))(y, idx)

def first_inputs(seed: int = 0) -> dict:
    key = jax.random.key(seed)
    ks = jax.random.split(key, 20)
    f32 = jnp.float32
    nrm = lambda k, shape, scale: (jax.random.normal(k, shape, f32) * scale).astype(f32)
    D = D_MODEL
    return {
        "x": nrm(ks[0], (BATCH, SEQ, D), 1.0),
        "c": nrm(ks[1], (BATCH, D), 1.0),
        "w_ada": nrm(ks[2], (DEPTH, D, N_MOD * D), 0.5 * D ** -0.5),
        "b_ada": nrm(ks[3], (DEPTH, N_MOD * D), 0.02),
        "g_norm_mix": 1.0 + nrm(ks[4], (DEPTH, D), 0.02),
        "w_in": nrm(ks[5], (DEPTH, D, D_IN_PROJ), D ** -0.5),
        "b_gate": nrm(ks[6], (DEPTH, N_BRANCHES * D), 0.02),
        "w_fourier": nrm(ks[7], (DEPTH, D_FOURIER, D), D_FOURIER ** -0.5),
        "w_conv": nrm(ks[8], (DEPTH, CONV_WIDTH, D_CONV), CONV_WIDTH ** -0.5),
        "w_conv_out": nrm(ks[9], (DEPTH, D_CONV, D), D_CONV ** -0.5),
        "w_o": nrm(ks[10], (DEPTH, D, D), D ** -0.5),
        "g_norm_moe": 1.0 + nrm(ks[11], (DEPTH, D), 0.02),
        "w_router": nrm(ks[12], (DEPTH, D, N_EXPERTS), D ** -0.5),
        "b_router": nrm(ks[13], (DEPTH, N_EXPERTS), 0.01),
        "w_gate_e": nrm(ks[14], (DEPTH, N_EXPERTS, D, D_EXPERT), D ** -0.5),
        "w_up_e": nrm(ks[15], (DEPTH, N_EXPERTS, D, D_EXPERT), D ** -0.5),
        "w_down_e": nrm(ks[16], (DEPTH, N_EXPERTS, D_EXPERT, D), D_EXPERT ** -0.5),
        "g_final": 1.0 + nrm(ks[17], (D,), 0.02),
    }

def first_block(x, c, w_ada, b_ada, g_norm_mix, w_in, b_gate, w_fourier, w_conv, w_conv_out, w_o,
              g_norm_moe, w_router, b_router, w_gate_e, w_up_e, w_down_e, g_final):
    D = D_MODEL
    c_act = jax.nn.silu(c)
    for l in range(DEPTH):
        mod = jnp.einsum('bd,dm->bm', c_act, w_ada[l]) + b_ada[l]
        shift_m, scale_m, gate_m, shift_f, scale_f, gate_f = jnp.split(mod, N_MOD, axis=-1)

        h = modulate(rms_norm(x, g_norm_mix[l]), shift_m, scale_m)
        p = jnp.einsum('bsd,dk->bsk', h, w_in[l])
        o1 = D_FOURIER
        o2 = o1 + D_CONV
        o3 = o2 + D_CONV
        o4 = o3 + D_CONV
        u_f = p[..., :o1]
        v, b_g, c_g = p[..., o1:o2], p[..., o2:o3], p[..., o3:o4]
        g_logits = p[..., o4:] + b_gate[l]
        gate_a = jax.nn.sigmoid(g_logits[..., :D])
        gate_b = jax.nn.sigmoid(g_logits[..., D:])
        y_a = jnp.einsum('bsk,kd->bsd', fourier_mix(u_f), w_fourier[l])
        y_b = jnp.einsum('bsk,kd->bsd', b_g * centred_conv3(c_g * v, w_conv[l]), w_conv_out[l])
        z = gate_a * y_a + gate_b * y_b
        mix_out = jnp.einsum('bsd,de->bse', z, w_o[l])
        x = x + gate_m[:, None, :] * mix_out

        h2 = modulate(rms_norm(x, g_norm_moe[l]), shift_f, scale_f)
        moe_out = expert_choice_moe(h2, w_router[l], b_router[l], w_gate_e[l], w_up_e[l], w_down_e[l])
        x = x + gate_f[:, None, :] * moe_out
    return rms_norm(x, g_final)


HEAD_DIM = 64
NSA_HEADS = 8
NSA_KV_GROUPS = 2
NSA_HPG = NSA_HEADS // NSA_KV_GROUPS
NSA_WIDTH = NSA_HEADS * HEAD_DIM
NSA_KV_WIDTH = NSA_KV_GROUPS * HEAD_DIM
CMP_LEN = 32
CMP_STRIDE = 16
CMP_HIDDEN = 2 * HEAD_DIM
SLC_BLOCK = 64
SLC_TOPN = 16
WINDOW = 512
MOBA_HEADS = 8
MOBA_WIDTH = MOBA_HEADS * HEAD_DIM
MOBA_BLOCK = 256
MOBA_TOPK = 3
TOTAL_HEADS = NSA_HEADS + MOBA_HEADS
Q_CHUNK = 32
COL_WIDTHS = (NSA_WIDTH, 6 * NSA_KV_WIDTH, 3 * NSA_HEADS, NSA_WIDTH, 3 * MOBA_WIDTH, MOBA_WIDTH, 2 * D_MODEL)
IN_COLS = NSA_WIDTH + 6 * NSA_KV_WIDTH + 3 * NSA_HEADS + NSA_WIDTH + 3 * MOBA_WIDTH + MOBA_WIDTH + 2 * D_MODEL


def rms_norm_2(x, g):
    xf = x.astype(jnp.float32)
    y = xf * lax.rsqrt(jnp.mean(xf * xf, axis=-1, keepdims=True) + RMS_EPS)
    return (y * g.astype(jnp.float32)).astype(x.dtype)

def alibi_slopes(n):
    return jnp.asarray((2.0 ** (-8.0 * np.arange(1, n + 1) / n)).astype(np.float32))

def masked_softmax(s, mask):
    s = jnp.where(mask, s, -jnp.inf)
    m = jnp.max(s, axis=-1, keepdims=True)
    m = jnp.where(jnp.isfinite(m), m, 0.0)
    p = jnp.where(mask, jnp.exp(s - m), 0.0)
    return p / jnp.maximum(jnp.sum(p, axis=-1, keepdims=True), 1e-30)

def cmp_to_slc_matrix(n_cmp, n_slc):
    cs = np.arange(n_cmp) * CMP_STRIDE
    ce = cs + CMP_LEN - 1
    ss = np.arange(n_slc) * SLC_BLOCK
    se = ss + SLC_BLOCK - 1
    return ((cs[:, None] <= se[None, :]) & (ce[:, None] >= ss[None, :])).astype(np.float32)

def compress(k, pe, w1, w2):
    S = k.shape[2]
    n_cmp = (S - CMP_LEN) // CMP_STRIDE + 1
    idx = np.arange(n_cmp)[:, None] * CMP_STRIDE + np.arange(CMP_LEN)[None, :]
    blocks = k[:, :, idx] + pe
    h = jax.nn.silu(jnp.einsum('bgnld,lde->bgne', blocks, w1))
    return jnp.einsum('bgne,ef->bgnf', h, w2)

def nsa_attention(q, kc, vc, ks, vs, kw, vw, gates, slopes):
    B, G, P, S, hd = q.shape
    n_cmp = kc.shape[2]
    n_slc = S // SLC_BLOCK
    k_sel = min(SLC_TOPN, n_slc)
    scale = hd ** -0.5
    cmp_end = jnp.asarray(np.arange(n_cmp) * CMP_STRIDE + CMP_LEN - 1, jnp.int32)
    overlap = jnp.asarray(cmp_to_slc_matrix(n_cmp, n_slc))
    ks_b = ks.reshape(B, G, n_slc, SLC_BLOCK, hd)
    vs_b = vs.reshape(B, G, n_slc, SLC_BLOCK, hd)
    kw_p = jnp.pad(kw, ((0, 0), (0, 0), (WINDOW, 0), (0, 0)))
    vw_p = jnp.pad(vw, ((0, 0), (0, 0), (WINDOW, 0), (0, 0)))
    bi = jnp.arange(B)[:, None, None, None]
    gi = jnp.arange(G)[None, :, None, None]
    blk = jnp.arange(n_slc)
    in_blk = jnp.arange(SLC_BLOCK)
    win_off = jnp.arange(WINDOW + Q_CHUNK) - WINDOW
    sl = slopes.astype(jnp.float32)[None, :, :, None, None]

    def chunk(ci):
        c0 = ci * Q_CHUNK
        t = c0 + jnp.arange(Q_CHUNK)
        qc = lax.dynamic_slice_in_dim(q, c0, Q_CHUNK, axis=3)
        g = lax.dynamic_slice_in_dim(gates, c0, Q_CHUNK, axis=4)
        dist = t[:, None] - cmp_end[None, :]
        s = jnp.einsum('bgpqd,bgnd->bgpqn', qc, kc).astype(jnp.float32) * scale - sl * dist.astype(jnp.float32)
        p_cmp = masked_softmax(s, dist >= 0)
        o_cmp = jnp.einsum('bgpqn,bgnd->bgpqd', p_cmp.astype(vc.dtype), vc)
        imp = jnp.einsum('bgpqn,nj->bgqj', p_cmp, overlap)
        cur = t // SLC_BLOCK
        causal_blk = blk[None, :] <= cur[:, None]
        forced = (blk[None, :] == 0) | (blk[None, :] == cur[:, None]) | (blk[None, :] == cur[:, None] - 1)
        imp = jnp.where(forced, jnp.inf, imp)
        imp = jnp.where(causal_blk, imp, -jnp.inf)
        _, sel = lax.top_k(imp, k_sel)
        kg = ks_b[bi, gi, sel]
        vg = vs_b[bi, gi, sel]
        pos = (sel[..., None] * SLC_BLOCK + in_blk).reshape(B, G, 1, Q_CHUNK, k_sel * SLC_BLOCK)
        dist = t[:, None] - pos
        s = jnp.einsum('bgpqd,bgqkld->bgpqkl', qc, kg).reshape(B, G, P, Q_CHUNK, k_sel * SLC_BLOCK)
        s = s.astype(jnp.float32) * scale - sl * dist.astype(jnp.float32)
        p = masked_softmax(s, dist >= 0).astype(vg.dtype).reshape(B, G, P, Q_CHUNK, k_sel, SLC_BLOCK)
        o_slc = jnp.einsum('bgpqkl,bgqkld->bgpqd', p, vg)
        kwin = lax.dynamic_slice_in_dim(kw_p, c0, WINDOW + Q_CHUNK, axis=2)
        vwin = lax.dynamic_slice_in_dim(vw_p, c0, WINDOW + Q_CHUNK, axis=2)
        posw = c0 + win_off
        dist = t[:, None] - posw[None, :]
        mask = (posw[None, :] >= 0) & (dist >= 0) & (dist < WINDOW)
        s = jnp.einsum('bgpqd,bgkd->bgpqk', qc, kwin).astype(jnp.float32) * scale - sl * dist.astype(jnp.float32)
        p = masked_softmax(s, mask).astype(vwin.dtype)
        o_win = jnp.einsum('bgpqk,bgkd->bgpqd', p, vwin)
        return g[0][..., None] * o_cmp + g[1][..., None] * o_slc + g[2][..., None] * o_win

    out = lax.map(chunk, jnp.arange(S // Q_CHUNK))
    return out.transpose(1, 0, 4, 2, 3, 5).reshape(B, S, G * P * hd)

def moba_attention(q, k, v, slopes):
    B, H, S, hd = q.shape
    nb = -(-S // MOBA_BLOCK)
    pad = nb * MOBA_BLOCK - S
    kb = jnp.pad(k, ((0, 0), (0, 0), (0, pad), (0, 0))).reshape(B, H, nb, MOBA_BLOCK, hd)
    vb = jnp.pad(v, ((0, 0), (0, 0), (0, pad), (0, 0))).reshape(B, H, nb, MOBA_BLOCK, hd)
    kbar = jnp.mean(kb.astype(jnp.float32), axis=3)
    k_sel = min(MOBA_TOPK, nb)
    scale = hd ** -0.5
    bi = jnp.arange(B)[:, None, None, None]
    hi = jnp.arange(H)[None, :, None, None]
    offs = jnp.arange(MOBA_BLOCK)
    blocks = jnp.arange(nb)
    sl = slopes.astype(jnp.float32)[None, :, None, None]

    def chunk(ci):
        c0 = ci * Q_CHUNK
        t = c0 + jnp.arange(Q_CHUNK)
        cur = c0 // MOBA_BLOCK
        qc = lax.dynamic_slice_in_dim(q, c0, Q_CHUNK, axis=2)
        gate = jnp.einsum('bhqd,bhnd->bhqn', qc.astype(jnp.float32), kbar)
        gate = jnp.where(blocks < cur, gate, -jnp.inf)
        _, sel = lax.top_k(gate, k_sel)
        valid = sel < cur
        kg = kb[bi, hi, sel]
        vg = vb[bi, hi, sel]
        ko = lax.dynamic_index_in_dim(kb, cur, axis=2, keepdims=False)
        vo = lax.dynamic_index_in_dim(vb, cur, axis=2, keepdims=False)
        n_sel = k_sel * MOBA_BLOCK
        s_sel = jnp.einsum('bhqd,bhqkld->bhqkl', qc, kg).reshape(B, H, Q_CHUNK, n_sel)
        s_own = jnp.einsum('bhqd,bhld->bhql', qc, ko)
        s = jnp.concatenate([s_sel, s_own], axis=-1).astype(jnp.float32) * scale
        pos_sel = (sel[..., None] * MOBA_BLOCK + offs).reshape(B, H, Q_CHUNK, n_sel)
        pos_own = jnp.broadcast_to(cur * MOBA_BLOCK + offs, (B, H, Q_CHUNK, MOBA_BLOCK))
        pos = jnp.concatenate([pos_sel, pos_own], axis=-1)
        dist = t[:, None] - pos
        mask_sel = jnp.broadcast_to(valid[..., None], (B, H, Q_CHUNK, k_sel, MOBA_BLOCK)).reshape(B, H, Q_CHUNK, n_sel)
        mask = jnp.concatenate([mask_sel, dist[..., n_sel:] >= 0], axis=-1)
        s = s - sl * dist.astype(jnp.float32)
        p = masked_softmax(s, mask).astype(v.dtype)
        p_sel = p[..., :n_sel].reshape(B, H, Q_CHUNK, k_sel, MOBA_BLOCK)
        p_own = p[..., n_sel:]
        return jnp.einsum('bhqkl,bhqkld->bhqd', p_sel, vg) + jnp.einsum('bhql,bhld->bhqd', p_own, vo)

    out = lax.map(chunk, jnp.arange(S // Q_CHUNK))
    return out.transpose(1, 0, 3, 2, 4).reshape(B, S, H * hd)

def hybrid_layer(x, norm_pre, w_in, pe_k, w1_k, w2_k, pe_v, w1_v, w2_v, w_a, w_b, w_o, norm_post):
    B, S, _ = x.shape
    G, P, hd = NSA_KV_GROUPS, NSA_HPG, HEAD_DIM
    u = rms_norm_2(x, norm_pre)
    proj = u @ w_in
    splits = [int(c) for c in np.cumsum(COL_WIDTHS)[:-1]]
    q_a, kv_a, g_a, z_a, qkv_b, z_b, merge = jnp.split(proj, splits, axis=-1)
    slopes = alibi_slopes(TOTAL_HEADS)
    q_a = q_a.reshape(B, S, G, P, hd).transpose(0, 2, 3, 1, 4)
    kv_a = kv_a.reshape(B, S, 6, G, hd).transpose(2, 0, 3, 1, 4)
    kc = compress(kv_a[0], pe_k, w1_k, w2_k)
    vc = compress(kv_a[1], pe_v, w1_v, w2_v)
    gates_a = jax.nn.sigmoid(g_a).reshape(B, S, 3, G, P).transpose(2, 0, 3, 4, 1)
    o_a = nsa_attention(q_a, kc, vc, kv_a[2], kv_a[3], kv_a[4], kv_a[5], gates_a,
                        slopes[0::2].reshape(G, P))
    y_a = o_a * jax.nn.silu(z_a)
    qkv_b = qkv_b.reshape(B, S, 3, MOBA_HEADS, hd).transpose(2, 0, 3, 1, 4)
    o_b = moba_attention(qkv_b[0], qkv_b[1], qkv_b[2], slopes[1::2])
    y_b = o_b * jax.nn.silu(z_b)
    gate_a, gate_b = jnp.split(merge, 2, axis=-1)
    m = jax.nn.sigmoid(gate_a) * (y_a @ w_a) + jax.nn.sigmoid(gate_b) * (y_b @ w_b)
    return x + rms_norm_2(m @ w_o, norm_post)

def second_inputs(seed: int = 0) -> dict:
    key = jax.random.key(seed)
    ks = jax.random.split(key, 13)

    def nrm(k, shape, s):
        return jax.random.normal(k, shape, jnp.float32) * s

    return {
        'x': nrm(ks[0], (BATCH, SEQ, D_MODEL), 1.0),
        'norm_pre': 1.0 + nrm(ks[1], (DEPTH, D_MODEL), 0.1),
        'w_in': nrm(ks[2], (DEPTH, D_MODEL, IN_COLS), D_MODEL ** -0.5),
        'cmp_pe_k': nrm(ks[3], (DEPTH, CMP_LEN, HEAD_DIM), 0.1),
        'cmp_w1_k': nrm(ks[4], (DEPTH, CMP_LEN, HEAD_DIM, CMP_HIDDEN), (CMP_LEN * HEAD_DIM) ** -0.5),
        'cmp_w2_k': nrm(ks[5], (DEPTH, CMP_HIDDEN, HEAD_DIM), CMP_HIDDEN ** -0.5),
        'cmp_pe_v': nrm(ks[6], (DEPTH, CMP_LEN, HEAD_DIM), 0.1),
        'cmp_w1_v': nrm(ks[7], (DEPTH, CMP_LEN, HEAD_DIM, CMP_HIDDEN), (CMP_LEN * HEAD_DIM) ** -0.5),
        'cmp_w2_v': nrm(ks[8], (DEPTH, CMP_HIDDEN, HEAD_DIM), CMP_HIDDEN ** -0.5),
        'w_branch_a': nrm(ks[9], (DEPTH, NSA_WIDTH, D_MODEL), NSA_WIDTH ** -0.5),
        'w_branch_b': nrm(ks[10], (DEPTH, MOBA_WIDTH, D_MODEL), MOBA_WIDTH ** -0.5),
        'w_o': nrm(ks[11], (DEPTH, D_MODEL, D_MODEL), D_MODEL ** -0.5),
        'norm_post': 1.0 + nrm(ks[12], (DEPTH, D_MODEL), 0.1),
    }

def second_block(x, norm_pre, w_in, cmp_pe_k, cmp_w1_k, cmp_w2_k, cmp_pe_v, cmp_w1_v, cmp_w2_v,
              w_branch_a, w_branch_b, w_o, norm_post):
    h = x
    for l in range(DEPTH):
        h = hybrid_layer(h, norm_pre[l], w_in[l], cmp_pe_k[l], cmp_w1_k[l], cmp_w2_k[l],
                         cmp_pe_v[l], cmp_w1_v[l], cmp_w2_v[l], w_branch_a[l], w_branch_b[l],
                         w_o[l], norm_post[l])
    return h


DEPTH_3 = 2

N_MIXERS = 4
N_HEADS_GROUP = D_MODEL // (N_MIXERS * HEAD_DIM)
GROUP_WIDTH = N_HEADS_GROUP * HEAD_DIM
MIX_WIDTH = N_MIXERS * GROUP_WIDTH
Q_BLK = 128
GRID_W = 64
NA_ROWS = 8
NA_COLS = 16
DIFF_QK_DIM = HEAD_DIM // 2
DIL_PATTERNS = ((128, 1), (512, 4), (2048, 16))
MLA_Q_RANK = D_MODEL // 4
MLA_KV_RANK = D_MODEL // 8
MLA_NOPE = HEAD_DIM
MLA_ROPE = HEAD_DIM // 2
MLA_V = HEAD_DIM
ROPE_THETA = 10000.0
T5_BUCKETS = 32
T5_MAX_DIST = 1024
T5_HEADS = 2 * N_HEADS_GROUP
D_FF = ((8 * D_MODEL + 3 * 256 - 1) // (3 * 256)) * 256
IN_WIDTH = 9 * GROUP_WIDTH + MLA_Q_RANK + MLA_KV_RANK + MLA_ROPE
EPS = 1e-6


def rms_norm_3(x, g):
    xf = x.astype(jnp.float32)
    y = xf * lax.rsqrt(jnp.mean(xf * xf, axis=-1, keepdims=True) + EPS)
    return (y * g.astype(jnp.float32)).astype(x.dtype)

def t5_bucket(rel):
    nb = T5_BUCKETS // 2
    max_exact = nb // 2
    side = jnp.where(rel > 0, nb, 0)
    n = jnp.abs(rel)
    large = max_exact + (jnp.log(jnp.maximum(n, 1).astype(jnp.float32) / max_exact)
                         / math.log(T5_MAX_DIST / max_exact) * (nb - max_exact)).astype(jnp.int32)
    large = jnp.minimum(large, nb - 1)
    return side + jnp.where(n < max_exact, n, large)

def rope_tables(pos):
    half = MLA_ROPE // 2
    inv_freq = ROPE_THETA ** (-jnp.arange(half, dtype=jnp.float32) / half)
    ang = pos.astype(jnp.float32)[:, None] * inv_freq[None, :]
    return jnp.cos(ang), jnp.sin(ang)

def apply_rope(x, cos, sin):
    half = x.shape[-1] // 2
    x1 = x[..., :half].astype(jnp.float32)
    x2 = x[..., half:].astype(jnp.float32)
    return jnp.concatenate([x1 * cos - x2 * sin, x1 * sin + x2 * cos], axis=-1).astype(x.dtype)

def neighborhood_attention(q, k, v, rpb):
    B, S, H, D = q.shape
    rows = S // GRID_W
    wr = min(NA_ROWS, rows)
    scale = D ** -0.5
    kg = k.reshape(B, rows, GRID_W, H, D)
    vg = v.reshape(B, rows, GRID_W, H, D)
    qg = q.reshape(B, rows, GRID_W, H, D).swapaxes(0, 1)
    col = jnp.arange(GRID_W)
    col_idx = jnp.clip(col - NA_COLS // 2, 0, GRID_W - NA_COLS)[:, None] + jnp.arange(NA_COLS)[None, :]
    col_bias_idx = col_idx - col[:, None] + NA_COLS - 1

    def one_row(args):
        q_row, r = args
        r0 = jnp.clip(r - wr // 2, 0, rows - wr)
        k_rows = lax.dynamic_slice_in_dim(kg, r0, wr, axis=1)
        v_rows = lax.dynamic_slice_in_dim(vg, r0, wr, axis=1)
        k_nb = k_rows[:, :, col_idx]
        v_nb = v_rows[:, :, col_idx]
        row_bias_idx = r0 + jnp.arange(wr) - r + NA_ROWS - 1
        bias = rpb[:, row_bias_idx[None, :, None], col_bias_idx[:, None, :]]
        s = jnp.einsum('bqhd,brqchd->bhqrc', q_row, k_nb).astype(jnp.float32) * scale + bias.astype(jnp.float32)
        p = jax.nn.softmax(s.reshape(B, H, GRID_W, wr * NA_COLS), axis=-1).reshape(s.shape)
        return jnp.einsum('bhqrc,brqchd->bqhd', p.astype(v.dtype), v_nb)

    out = lax.map(one_row, (qg, jnp.arange(rows)))
    return out.swapaxes(0, 1).reshape(B, S, H * D)

def diff_attention(q, k, v, lam, lam_init, subln_g, table):
    B, S, H, _, dk = q.shape
    nblk = S // Q_BLK
    scale = dk ** -0.5
    qb = q.reshape(B, nblk, Q_BLK, H, 2, dk).swapaxes(0, 1)
    kpos = jnp.arange(S)

    def one_block(args):
        q_blk, i = args
        qpos = i * Q_BLK + jnp.arange(Q_BLK)
        bias = table[t5_bucket(kpos[None, :] - qpos[:, None])].transpose(2, 0, 1).astype(jnp.float32)
        s = jnp.einsum('bqhcd,bkhcd->bchqk', q_blk, k).astype(jnp.float32) * scale + bias[None, None]
        p = jax.nn.softmax(s, axis=-1)
        a = p[:, 0] - lam * p[:, 1]
        return jnp.einsum('bhqk,bkhd->bqhd', a.astype(v.dtype), v)

    o = lax.map(one_block, (qb, jnp.arange(nblk))).swapaxes(0, 1).reshape(B, S, H, -1)
    o = rms_norm_3(o, subln_g) * (1.0 - lam_init)
    return o.reshape(B, S, -1)

def dilated_attention(q, k, v, table):
    B, S, H, D = q.shape
    nblk = S // Q_BLK
    scale = D ** -0.5
    qb = q.reshape(B, nblk, Q_BLK, H, D).swapaxes(0, 1)

    def one_block(args):
        q_blk, i = args
        qpos = i * Q_BLK + jnp.arange(Q_BLK)
        outs, lses = [], []
        for window, dil in DIL_PATTERNS:
            m = window // (2 * dil)
            offs = dil * jnp.arange(-m, m + 1)
            kpos = qpos[:, None] + offs[None, :]
            valid = (kpos >= 0) & (kpos < S)
            kidx = jnp.clip(kpos, 0, S - 1)
            k_g = k[:, kidx]
            v_g = v[:, kidx]
            bias = table[t5_bucket(offs)].T.astype(jnp.float32)
            s = jnp.einsum('bqhd,bqkhd->bhqk', q_blk, k_g).astype(jnp.float32) * scale + bias[None, :, None, :]
            s = jnp.where(valid[None, None], s, -jnp.inf)
            s_max = jnp.max(s, axis=-1, keepdims=True)
            e = jnp.exp(s - s_max)
            den = jnp.sum(e, axis=-1)
            o = jnp.einsum('bhqk,bqkhd->bqhd', e, v_g.astype(jnp.float32)) / den.transpose(0, 2, 1)[..., None]
            outs.append(o)
            lses.append(s_max[..., 0] + jnp.log(den))
        wts = jax.nn.softmax(jnp.stack(lses), axis=0)
        out = jnp.sum(jnp.stack(outs) * wts.transpose(0, 1, 3, 2)[..., None], axis=0)
        return out.astype(q.dtype)

    out = lax.map(one_block, (qb, jnp.arange(nblk)))
    return out.swapaxes(0, 1).reshape(B, S, H * D)

def mla_attention(q_nope, q_rope, k_nope, k_rope, v):
    B, S, H, _ = q_nope.shape
    nblk = S // Q_BLK
    scale = (MLA_NOPE + MLA_ROPE) ** -0.5

    def blocks(t):
        return t.reshape(B, nblk, Q_BLK, *t.shape[2:]).swapaxes(0, 1)

    def one_block(args):
        qn, qr = args
        s = jnp.einsum('bqhd,bkhd->bhqk', qn, k_nope) + jnp.einsum('bqhd,bkd->bhqk', qr, k_rope)
        p = jax.nn.softmax(s.astype(jnp.float32) * scale, axis=-1)
        return jnp.einsum('bhqk,bkhd->bqhd', p.astype(v.dtype), v)

    out = lax.map(one_block, (blocks(q_nope), blocks(q_rope)))
    return out.swapaxes(0, 1).reshape(B, S, -1)

def third_inputs(seed: int = 0) -> dict:
    key = jax.random.key(seed)
    ks = jax.random.split(key, 17)
    H = N_HEADS_GROUP

    def nrm(k, shape, scale):
        return jax.random.normal(k, shape, jnp.float32) * scale

    return {
        'x': nrm(ks[0], (BATCH, SEQ, D_MODEL), 1.0),
        'attn_norm': 1.0 + nrm(ks[1], (DEPTH_3, D_MODEL), 0.05),
        'w_in': nrm(ks[2], (DEPTH_3, D_MODEL, IN_WIDTH), D_MODEL ** -0.5),
        'na_rpb': nrm(ks[3], (DEPTH_3, H, 2 * NA_ROWS - 1, 2 * NA_COLS - 1), 0.1),
        'diff_lambda': nrm(ks[4], (DEPTH_3, 4, DIFF_QK_DIM), 0.1),
        'diff_subln': 1.0 + nrm(ks[5], (DEPTH_3, HEAD_DIM), 0.05),
        'mla_q_norm': 1.0 + nrm(ks[6], (DEPTH_3, MLA_Q_RANK), 0.05),
        'w_uq': nrm(ks[7], (DEPTH_3, MLA_Q_RANK, H * (MLA_NOPE + MLA_ROPE)), MLA_Q_RANK ** -0.5),
        'mla_kv_norm': 1.0 + nrm(ks[8], (DEPTH_3, MLA_KV_RANK), 0.05),
        'w_ukv': nrm(ks[9], (DEPTH_3, MLA_KV_RANK, H * (MLA_NOPE + MLA_V)), MLA_KV_RANK ** -0.5),
        't5_table': nrm(ks[10], (T5_BUCKETS, T5_HEADS), 0.1),
        'w_o': nrm(ks[11], (DEPTH_3, MIX_WIDTH, D_MODEL), MIX_WIDTH ** -0.5),
        'ffn_norm': 1.0 + nrm(ks[12], (DEPTH_3, D_MODEL), 0.05),
        'w_gate': nrm(ks[13], (DEPTH_3, D_MODEL, D_FF), D_MODEL ** -0.5),
        'w_up': nrm(ks[14], (DEPTH_3, D_MODEL, D_FF), D_MODEL ** -0.5),
        'w_down': nrm(ks[15], (DEPTH_3, D_FF, D_MODEL), D_FF ** -0.5),
        'final_norm': 1.0 + nrm(ks[16], (D_MODEL,), 0.05),
    }

def third_block(x, attn_norm, w_in, na_rpb, diff_lambda, diff_subln, mla_q_norm, w_uq,
              mla_kv_norm, w_ukv, t5_table, w_o, ffn_norm, w_gate, w_up, w_down, final_norm):
    B, S, _ = x.shape
    H, G = N_HEADS_GROUP, GROUP_WIDTH
    cos, sin = rope_tables(jnp.arange(S))
    t5_diff = t5_table[:, :H]
    t5_dil = t5_table[:, H:]
    split_points = np.cumsum([G] * 9 + [MLA_Q_RANK, MLA_KV_RANK]).tolist()
    for l in range(DEPTH_3):
        h = rms_norm_3(x, attn_norm[l])
        proj = h @ w_in[l]
        qa, ka, va, qb, kb, vb, qc, kc, vc, cq, ckv, kr = jnp.split(proj, split_points, axis=-1)

        o_a = neighborhood_attention(qa.reshape(B, S, H, HEAD_DIM), ka.reshape(B, S, H, HEAD_DIM),
                                     va.reshape(B, S, H, HEAD_DIM), na_rpb[l])

        lam_init = 0.8 - 0.6 * math.exp(-0.3 * l)
        lq1, lk1, lq2, lk2 = [diff_lambda[l, j].astype(jnp.float32) for j in range(4)]
        lam = jnp.exp(jnp.sum(lq1 * lk1)) - jnp.exp(jnp.sum(lq2 * lk2)) + lam_init
        o_b = diff_attention(qb.reshape(B, S, H, 2, DIFF_QK_DIM), kb.reshape(B, S, H, 2, DIFF_QK_DIM),
                             vb.reshape(B, S, H, HEAD_DIM), lam, lam_init, diff_subln[l], t5_diff)

        o_c = dilated_attention(qc.reshape(B, S, H, HEAD_DIM), kc.reshape(B, S, H, HEAD_DIM),
                                vc.reshape(B, S, H, HEAD_DIM), t5_dil)

        cq = rms_norm_3(cq, mla_q_norm[l])
        qd = (cq @ w_uq[l]).reshape(B, S, H, MLA_NOPE + MLA_ROPE)
        q_nope = qd[..., :MLA_NOPE]
        q_rope = apply_rope(qd[..., MLA_NOPE:], cos[:, None, :], sin[:, None, :])
        ckv = rms_norm_3(ckv, mla_kv_norm[l])
        kvd = (ckv @ w_ukv[l]).reshape(B, S, H, MLA_NOPE + MLA_V)
        k_nope = kvd[..., :MLA_NOPE]
        v_d = kvd[..., MLA_NOPE:]
        k_rope = apply_rope(kr, cos, sin)
        o_d = mla_attention(q_nope, q_rope, k_nope, k_rope, v_d)

        mix = jnp.concatenate([o_a, o_b, o_c, o_d], axis=-1)
        x = x + mix @ w_o[l]

        h = rms_norm_3(x, ffn_norm[l])
        x = x + (jax.nn.silu(h @ w_gate[l]) * (h @ w_up[l])) @ w_down[l]
    return rms_norm_3(x, final_norm)


def setup_inputs(seed=0):
    out = dict(first_inputs(seed))
    for name, value in second_inputs(seed + 1).items():
        if name != "x":
            out[name + "_2"] = value
    for name, value in third_inputs(seed + 2).items():
        if name != "x":
            out[name + "_3"] = value
    return out


def reference(
    x, c, w_ada, b_ada, g_norm_mix, w_in, b_gate, w_fourier, w_conv, w_conv_out, w_o,
    g_norm_moe, w_router, b_router, w_gate_e, w_up_e, w_down_e, g_final, norm_pre_2, w_in_2,
    cmp_pe_k_2, cmp_w1_k_2, cmp_w2_k_2, cmp_pe_v_2, cmp_w1_v_2, cmp_w2_v_2, w_branch_a_2,
    w_branch_b_2, w_o_2, norm_post_2, attn_norm_3, w_in_3, na_rpb_3, diff_lambda_3,
    diff_subln_3, mla_q_norm_3, w_uq_3, mla_kv_norm_3, w_ukv_3, t5_table_3, w_o_3, ffn_norm_3,
    w_gate_3, w_up_3, w_down_3, final_norm_3,
):
    x = first_block(
        x, c, w_ada, b_ada, g_norm_mix, w_in, b_gate, w_fourier, w_conv, w_conv_out, w_o,
        g_norm_moe, w_router, b_router, w_gate_e, w_up_e, w_down_e, g_final,
    )
    x = second_block(
        x, norm_pre_2, w_in_2, cmp_pe_k_2, cmp_w1_k_2, cmp_w2_k_2, cmp_pe_v_2, cmp_w1_v_2,
        cmp_w2_v_2, w_branch_a_2, w_branch_b_2, w_o_2, norm_post_2,
    )
    return third_block(
        x, attn_norm_3, w_in_3, na_rpb_3, diff_lambda_3, diff_subln_3, mla_q_norm_3, w_uq_3,
        mla_kv_norm_3, w_ukv_3, t5_table_3, w_o_3, ffn_norm_3, w_gate_3, w_up_3, w_down_3,
        final_norm_3,
    )


_drawn_inputs = setup_inputs


def setup_inputs(seed=0):
    import zlib

    import numpy as np

    out = dict(_drawn_inputs(seed))
    spreads = {}
    factors = {'g_norm_mix': 3.807,
     'b_gate': 8.0,
     'g_norm_moe': 5.534,
     'b_router': 8.0,
     'cmp_pe_k_2': 8.0,
     'na_rpb_3': 6.211,
     'diff_lambda_3': 6.296,
     'diff_subln_3': 2.78,
     'mla_q_norm_3': 8.0,
     'mla_kv_norm_3': 8.0}
    for name, (base, spread) in spreads.items():
        noise = np.random.default_rng([zlib.crc32(name.encode()), seed]).standard_normal(out[name].shape)
        drawn = base * np.exp(spread * noise) if base else spread * noise
        out[name] = __import__('jax').numpy.asarray(drawn.astype(out[name].dtype))
    for name, factor in factors.items():
        out[name] = (out[name] * factor).astype(out[name].dtype)
    return out
```

```python
import math
from contextlib import ExitStack

import numpy as np

import concourse.bass as bass
from concourse import mybir

ALU = mybir.AluOpType
ACT = mybir.ActivationFunctionType
AX_X = mybir.AxisListType.X
F32 = mybir.dt.float32

P = 128
T = 256
TT = T // P
D = 1024
KT = D // P
EPS = 1e-6
NE = 16
CAP = 2 * T // NE
FE = 2048
SLOT = 4096
RING = 6
RING3 = 5
BIG = 1e30
NHEAD = 16
HD = 64
NCMP = (T - 32) // 16 + 1
DFF = ((8 * D + 3 * 256 - 1) // (3 * 256)) * 256
FT = DFF // P
LAYERS = 2
ARENA = 19776
GATE_UNITS = (4, 5, 10, 11)
NDIL = ((128, 1), (512, 4), (2048, 16))
GRID_W, NA_ROWS, NA_COLS = 64, 8, 16
NA_SPAN = T // GRID_W
REL = 2 * T
NAREL = 2 * GRID_W


def t5_bucket(rel):
    nb, exact = 16, 8
    side = np.where(rel > 0, nb, 0)
    n = np.abs(rel)
    q = np.maximum(n, 1).astype(np.float32) / np.float32(exact)
    large = exact + (np.log(q) / np.float32(math.log(1024 / exact)) * np.float32(nb - exact)).astype(np.int32)
    return side + np.where(n < exact, n, np.minimum(large, nb - 1))


def build_constants():
    c = {}
    tok = np.arange(T)
    c["ident"] = np.eye(P)
    c["ones"] = np.ones((P, P))
    q, k = tok[:, None], tok[None, :]
    causal = np.where(q >= k, (q - k).astype(np.float64), BIG)
    c["dist"] = np.concatenate([causal[:P, :P], causal[P:, :]], axis=1)
    end = np.arange(16) * 16 + 31
    dc = np.where((q >= end[None, :]) & (np.arange(16)[None, :] < NCMP), (q - end[None, :]).astype(np.float64), BIG)
    c["cmpdist"] = dc.reshape(TT, P, 16).transpose(1, 0, 2).reshape(P, 32)
    c["cmpvalid"] = (tok >= 31).astype(np.float64).reshape(TT, P).T
    col = np.arange(GRID_W)
    start = np.clip(col - NA_COLS // 2, 0, GRID_W - NA_COLS)
    out = ~((col[None, :] >= start[:, None]) & (col[None, :] < start[:, None] + NA_COLS))
    c["nawin"] = np.tile(np.where(out, BIG, 0.0), (2, NA_SPAN))
    half = 16
    freq = np.float32(10000.0) ** (-np.arange(half, dtype=np.float32) / np.float32(half))
    ang = (tok.astype(np.float32)[:, None] * freq[None, :]).astype(np.float32)
    for n, f in (("cos", np.cos), ("sin", np.sin)):
        c[n] = f(ang.astype(np.float64)).reshape(TT, P, half).transpose(1, 0, 2).reshape(P, TT * half)
    rel = np.arange(REL) - (T - 1)
    hot = np.zeros((P, REL))
    hot[t5_bucket(rel), np.arange(REL)] = 1.0
    c["t5hot"] = hot
    mult = sum(((np.abs(rel) <= w // 2) & (rel % d == 0)).astype(np.int64) for w, d in NDIL)
    add = np.zeros((P, REL))
    add[4:8] = np.where(mult > 0, -np.log(np.maximum(mult, 1)), BIG)
    c["diladd"] = add
    names = list(c)
    kept = np.concatenate([c[n] for n in names], axis=1).astype(np.float32)
    at, pos = {}, 0
    for n in names:
        at[n] = (pos, c[n].shape[1])
        pos += c[n].shape[1]
    a = 2 * np.pi * (np.outer(tok, tok) % T) / T
    s = 1.0 / math.sqrt(T * P)
    dft_s = np.concatenate([np.cos(a) * s, np.sin(a) * s], axis=1).reshape(TT, P, 2 * T).transpose(1, 0, 2)
    b = 2 * np.pi * (np.outer(np.arange(P), np.arange(P)) % P) / P
    dft = np.concatenate([dft_s.reshape(P, TT * 2 * T), np.cos(b), -np.sin(b)], axis=1).astype(np.float32)
    tri = (tok[:, None] < tok[None, :]).astype(np.float32).reshape(TT, P, T).transpose(1, 0, 2).reshape(P, TT * T)
    slots = np.tile(np.arange(CAP), (P, NE)).astype(np.float32)
    return kept, at, dft, np.concatenate([tri, slots], axis=1).astype(np.float32)


def slope(i):
    return float(np.float32(2.0 ** (-8.0 * (i + 1) / NHEAD)))


def names(prefix, n):
    return [f"{prefix}{i}" for i in range(n)]


PIECES = (names("ada", 12) + names("n1_", 4) + names("uf", 2) + names("dfta", 4) + names("dftb", 2)
          + names("v", 4) + names("b", 4) + names("c", 4) + names("ga", 4) + names("gb", 4)
          + names("wf", 4) + names("wc", 4) + names("wo", 4) + names("n2_", 4) + names("h2n", 4)
          + ["rt", "pt", "mk", "pos"]
          + names("n3_", 4) + names("qa", 2) + ["kc", "ks", "vs", "kw", "vw", "gnsa", "hk", "kcT", "vcn"]
          + names("za", 2) + names("qb", 2) + names("kb", 2) + names("vb", 2) + names("zb", 2)
          + names("mA", 4) + names("mB", 4) + names("yt", 4)
          + ["wa0", "wa1", "wb0", "wb1", "wa2", "wa3", "wb2", "wb3"] + names("wo2_", 4))
AT = {n: i for i, n in enumerate(PIECES)}
LP = (names("n4_", 4) + ["qa0", "ka0", "va0", "qb0", "kb0", "vb0", "qc0", "kc0", "vc0", "cq", "ckv", "kr", "cqT", "ckvT"]
      + names("uq", 2) + names("ukv", 2) + names("qm", 2) + names("km", 2) + names("mix", 4) + names("wo3_", 4)
      + names("n5_", 4) + names("gu", 22) + names("down", 4))
assert len(AT) == len(PIECES) 
LAT = {n: i for i, n in enumerate(LP)}
LPN = len(LP)
assert LPN % 4 == 0

UNITS = (names("ada", 12) + names("win", 11) + names("wf", 2) + names("wc", 2) + names("wo", 2))
N_MOE = len(UNITS)
UPE = 12
UNITS2 = ["qa", "kv", "kvwg", "w1", "za", "qb", "kb", "vb", "zb"] + names("mg", 4) + names("ab", 2) + names("wo2_", 2)
UAT = {n: i for i, n in enumerate(UNITS)}
U2AT = {n: N_MOE + UPE * NE + i for i, n in enumerate(UNITS2)}
N_U12 = N_MOE + UPE * NE + len(UNITS2)
L3 = names("win", 6) + names("wo", 2) + names("gu", 11) + names("dn", 6)
L3AT = {n: i for i, n in enumerate(L3)}
assert len(L3) % RING3 == 0

JOBS3 = ([("na", h, 0, t) for h in range(4) for t in range(TT)]
         + [("diff", h, c, t) for h in range(4) for t in range(TT) for c in range(2)]
         + [("dil", h, 0, t) for h in range(4) for t in range(TT)]
         + [("mla", h, 0, t) for h in range(4) for t in range(TT)])
NJ3 = len(JOBS3)
_first = ["qa0", "ka0", "va0", "qb0", "kb0", "vb0"]
_rest = ["qc0", "kc0", "vc0", "cq", "ckv", "kr", "cqT", "ckvT", "uq0", "uq1", "ukv0", "ukv1", "qm0", "qm1", "km0", "km1"]
PLAN3 = [("piece", n) for n in _first]
for _i, _n in enumerate(_rest):
    PLAN3.append(("piece", _n))
    PLAN3 += [("job", j) for j in range(2 * _i, 2 * _i + 2)]
PLAN3 += [("job", j) for j in range(2 * len(_rest), NJ3)]
PARTS3 = {L3AT["win5"]: 3}
PARTS3.update({L3AT[f"gu{i}"]: 2 for i in range(11)})
LAST3 = {L3AT[u]: LAT[p] for u, p in (("win0", "ka0"), ("win1", "qb0"), ("win2", "vb0"), ("win3", "kc0"),
                                      ("win4", "cq"), ("win5", "ukv1"), ("wo0", "wo3_1"), ("wo1", "wo3_3"),
                                      ("dn5", "down3"))}
LAST3.update({L3AT[f"gu{i}"]: LAT[f"gu{2 * i + 1}"] for i in range(11)})
LAM_INIT = [0.8 - 0.6 * math.exp(-0.3 * l) for l in range(LAYERS)]
LAST = {UAT[f"ada{i}"]: AT[f"ada{i}"] for i in range(12)}
LAST[UAT["win0"]] = AT["uf1"]
for _i in range(10):
    LAST[UAT[f"win{_i + 1}"]] = AT[("v", "b", "c", "ga", "gb")[_i // 2] + str(2 * (_i % 2) + 1)]
for _n in ("wf", "wc", "wo"):
    for _i in range(2):
        LAST[UAT[f"{_n}{_i}"]] = AT[f"{_n}{2 * _i + 1}"]
LAST.update({U2AT[u]: AT[p] for u, p in (("qa", "qa1"), ("kv", "vs"), ("kvwg", "vcn"), ("w1", "hk"), ("za", "za1"),
                                         ("qb", "qb1"), ("kb", "kb1"), ("vb", "vb1"), ("zb", "zb1"),
                                         ("mg0", "mA1"), ("mg1", "mA3"), ("mg2", "mB1"), ("mg3", "mB3"),
                                         ("ab0", "wb1"), ("ab1", "wb3"), ("wo2_0", "wo2_1"), ("wo2_1", "wo2_3"))})

NSA_JOBS = [(br, h, t) for h in range(8) for t in range(TT) for br in ("cmp", "slc", "win")]
MOBA_JOBS = [("moba", h, t) for h in range(8) for t in range(TT)]
JOBS2 = NSA_JOBS + MOBA_JOBS
_tail = (names("za", 2) + names("qb", 2) + names("kb", 2) + names("vb", 2) + names("zb", 2) + names("mA", 4)
         + names("mB", 4))
PLAN2 = []
NJ2 = len(JOBS2)
for _i, _n in enumerate(_tail):
    PLAN2.append(("piece", _n))
    PLAN2 += [("job", j) for j in range(len(JOBS2) * _i // len(_tail), len(JOBS2) * (_i + 1) // len(_tail))]


def program(nc, a, cst_at, out):
    with ExitStack() as ctx:
        def sb(name, cols, parts=P):
            return ctx.enter_context(nc.sbuf_tensor(name, [parts, cols], F32))[:, :]

        def sem(name):
            return ctx.enter_context(nc.semaphore(name))

        def dram(name, shape):
            return nc.dram_tensor(name, shape, F32, kind="Internal").ap()

        ring = sb("ring", RING * SLOT)
        x = sb("x", TT * D).rearrange("p (t d) -> p t d", t=TT)
        xT = sb("xT", KT * T).rearrange("p (k t) -> p k t", k=KT)
        cst = sb("cst", a["c_kept"].shape[1])
        vec1 = sb("vec1", 112)
        vec2 = sb("vec2", 78)
        stat = sb("stat", 512)
        arena = sb("arena", ARENA)
        psum = ctx.enter_context(nc.psum_tensor("psum", [P, 8, 512], F32))[:, :, :]

        def K(name):
            o, n = cst_at[name]
            return cst[:, o:o + n]

        ident, ones = K("ident"), K("ones")

        class Place:

            def __init__(self, at):
                self.at = at

            def __call__(self, n):
                self.at += n
                assert self.at <= ARENA, self.at
                return arena[:, self.at - n:self.at]

        pl = Place(0)
        gate_m, gate_f, gbc = pl(D), pl(D), pl(D)
        tri = pl(TT * T).rearrange("p (k t) -> p k t", k=TT)
        slot_id = pl(NE * CAP).rearrange("p (e c) -> p e c", e=NE)
        base1 = pl.at
        uf = pl(TT * 512).rearrange("p (t n) -> p t n", t=TT)
        part = uf
        vT = pl(KT * T).rearrange("p (k t) -> p k t", k=KT)
        cv = pl(KT * (T + 2)).rearrange("p (k t) -> p k t", k=KT)
        bT = pl(KT * T).rearrange("p (k t) -> p k t", k=KT)
        gaT = pl(KT * T).rearrange("p (k t) -> p k t", k=KT)
        gbT = pl(KT * T).rearrange("p (k t) -> p k t", k=KT)
        Bcs = gbT.rearrange("p (g h) t -> p g (h t)", g=4)
        fmT = pl(4 * T).rearrange("p (k t) -> p k t", k=4)
        dfts = pl(TT * 2 * T).rearrange("p (k n) -> p k n", k=TT)
        dftg = pl(2 * P).rearrange("p (c n) -> p c n", c=2)
        vrow = pl(2 * P).rearrange("p (c n) -> p c n", c=2)
        csil = pl(KT * 32).rearrange("p (k n) -> p k n", k=KT)
        t5tab = pl(8)
        t5vec = pl(REL)
        narow = pl(NAREL)
        lamraw = pl(LAYERS * P).rearrange("p (l n) -> p l n", l=LAYERS)
        lamprod = pl(LAYERS * 2 * 32).rearrange("p (l c n) -> p l c n", l=LAYERS, c=2)
        xn1 = vT.rearrange("p k t -> p (k t)").rearrange("p (t d) -> p t d", t=TT)
        mtmp = uf.rearrange("p t n -> p (t n)")

        pm = Place(base1)
        h2n = pm(TT * D).rearrange("p (t d) -> p t d", t=TT)
        acc = pm(TT * D).rearrange("p (t d) -> p t d", t=TT)
        sel = pm(TT * NE * CAP).rearrange("p (t n) -> p t n", t=TT)
        selw = pm(TT * NE * CAP).rearrange("p (t n) -> p t n", t=TT)
        rep = pm(TT * P).rearrange("p (t j c) -> p t j c", t=TT, j=4)
        selT = pm(T)
        xeT = pm(KT * CAP).rearrange("p (k c) -> p k c", k=KT)
        hT = pm(4 * P).rearrange("p (s n) -> p s n", s=4)
        sil = pm(512)
        gu = pm(512)
        ysb = pm(T)
        wr = pm(KT * NE).rearrange("p (k e) -> p k e", k=KT)
        brow = pm(NE)
        lg = pm(TT * NE).rearrange("p (t e) -> p t e", t=TT)
        ex = pm(TT * NE).rearrange("p (t e) -> p t e", t=TT)
        prob = pm(TT * NE).rearrange("p (t e) -> p t e", t=TT)
        pT = pm(T)
        work = pm(T)
        mk = pm(T)
        top8 = pm(8)
        maskn = pm(TT * NE).rearrange("p (t e) -> p t e", t=TT)
        posm = pm(TT * NE).rearrange("p (t e) -> p t e", t=TT)
        xn2 = h2n

        p2 = Place(D)
        zA = p2(D).rearrange("p (t n) -> p t n", t=TT)
        p2.at = 3 * D
        qaT = p2(4 * T).rearrange("p (k t) -> p k t", k=4)
        ksT = p2(2 * T).rearrange("p (g t) -> p g t", g=2)
        kwT = p2(2 * T).rearrange("p (g t) -> p g t", g=2)
        yT = arena[:, 3 * D:5 * D].rearrange("p (k t) -> p k t", k=KT)
        k2 = p2(2 * 2 * T).rearrange("p (c g t) -> p c g t", c=2, g=2)
        kb2 = p2(2 * 16 * 32).rearrange("p (c l n) -> p c l n", c=2, l=16)
        hk = p2(64).rearrange("p (c n) -> p c n", c=2)
        kcT = p2(32)
        vcn = p2(2 * HD).rearrange("p (g n) -> p g n", g=2)
        vs = p2(TT * P).rearrange("p (t n) -> p t n", t=TT)
        vw = p2(TT * P).rearrange("p (t n) -> p t n", t=TT)
        gn = p2(TT * 24).rearrange("p (t n) -> p t n", t=TT)
        qbT = p2(4 * T).rearrange("p (k t) -> p k t", k=4)
        kbT = p2(4 * T).rearrange("p (k t) -> p k t", k=4)
        vbn = p2(TT * 512).rearrange("p (t n) -> p t n", t=TT)
        zB = p2(TT * 512).rearrange("p (t n) -> p t n", t=TT)
        oA = p2(TT * 512).rearrange("p (t n) -> p t n", t=TT)
        oB = p2(TT * 512).rearrange("p (t n) -> p t n", t=TT)
        mAT = p2(KT * T).rearrange("p (k t) -> p k t", k=KT)
        mBT = p2(KT * T).rearrange("p (k t) -> p k t", k=KT)
        xn3 = mAT.rearrange("p k t -> p (k t)").rearrange("p (t d) -> p t d", t=TT)
        mixn = mBT.rearrange("p k t -> p (k t)").rearrange("p (t d) -> p t d", t=TT)
        yjunk = yT.rearrange("p k t -> p (k t)").rearrange("p (t d) -> p t d", t=TT)
        pj = Place(p2.at)
        sbuf = pj(2 * T).rearrange("p (b n) -> p b n", b=2)
        ebuf = pj(2 * T).rearrange("p (b n) -> p b n", b=2)
        pbuf = pj(2 * T).rearrange("p (b n) -> p b n", b=2)

        p3 = Place(0)
        nab = p3(8 * T).rearrange("p (h t n) -> p h t n", h=4, t=TT)
        p3.at = 3 * D
        qk = p3(12 * T).rearrange("p (k t) -> p k t", k=12)
        mixT = arena[:, 3 * D:5 * D].rearrange("p (k t) -> p k t", k=KT)
        actT = arena[:, 3 * D:3 * D + FT * T].rearrange("p (k t) -> p k t", k=FT)
        v3 = p3(3 * TT * T).rearrange("p (c t n) -> p c t n", c=3, t=TT)
        cqn = p3(TT * 256).rearrange("p (t n) -> p t n", t=TT)
        ckvn = p3(TT * P).rearrange("p (t n) -> p t n", t=TT)
        krn = p3(TT * 32).rearrange("p (t n) -> p t n", t=TT)
        cqT = p3(2 * T).rearrange("p (k t) -> p k t", k=2)
        ckvT = p3(T).rearrange("p (k t) -> p k t", k=1)
        qdn = p3(TT * 4 * 96).rearrange("p (t h n) -> p t h n", t=TT, h=4)
        kcat = p3(TT * 4 * 96).rearrange("p (t h n) -> p t h n", t=TT, h=4)
        vd = p3(TT * T).rearrange("p (t n) -> p t n", t=TT)
        qmT = p3(4 * T).rearrange("p (k t) -> p k t", k=4)
        kmT = p3(4 * T).rearrange("p (k t) -> p k t", k=4)
        mix = p3(TT * D).rearrange("p (t d) -> p t d", t=TT)
        rp = p3(4 * TT * 4 * 16).rearrange("p (c t h n) -> p c t h n", c=4, t=TT, h=4)
        rk = p3(4 * TT * 16).rearrange("p (c t n) -> p c t n", c=4, t=TT)
        hsq = p3(TT * 256).rearrange("p (t h n) -> p t h n", t=TT, h=4)
        assert p3.at <= p2.at
        t5b = ring[:, RING3 * SLOT:RING * SLOT].rearrange("p (h t n) -> p h t n", h=8, t=TT)

        st = Place(0)
        st.at = 0

        def small(n, _p=[0]):
            _p[0] += n
            assert _p[0] <= 512
            return stat[:, _p[0] - n:_p[0]]

        neghalf = small(2)
        mod = small(48)
        Am, Bm, Af, Bf = small(8), small(8), small(8), small(8)
        ssq, rstd = small(2), small(2)
        rmax, rsum, rrec = small(2), small(2), small(2)
        negmax = small(2)
        jmin, jsum, jrec = small(2), small(2), small(2)
        lamneg = small(LAYERS)
        lamsum = small(4)
        lamexp = small(4)
        subg = small(LAYERS * HD).rearrange("p (l n) -> p l n", l=LAYERS)
        hstat = small(16)
        hrstd = small(8)
        halfs = small(8)
        subl = small(HD)
        spare = small(NJ3 + 5)

        t5_row = dram("t5_row", (8, REL))
        t5_rep = dram("t5_rep", (8, (P + 1) * REL))
        na_row = dram("na_row", (LAYERS * 4 * 7, NAREL))
        na_rep = dram("na_rep", (LAYERS * 4 * 7, GRID_W * NAREL))

        w_ready = [sem(f"w_ready{i}") for i in range(RING)]
        e_unit = sem("e_unit")
        w3_ready = [sem(f"w3_ready{i}") for i in range(RING3)]
        g_ready = sem("g_ready")
        g_free = [sem(f"g_free{i}") for i in range(4)]
        in_x, in_cst, in_vec, in_b1 = sem("in_x"), sem("in_cst"), sem("in_vec"), sem("in_b1")
        in_moe, in_route = sem("in_moe"), sem("in_route")
        consts_set = sem("consts_set")
        n_sq, n_ms, n_rstd, n_xn = sem("n_sq"), sem("n_ms"), sem("n_rstd"), sem("n_xn")
        v_used = sem("v_used")
        v_cols = sem("v_cols")
        c_act = sem("c_act")
        part_ready = sem("part_ready")
        mod_mm = sem("mod_mm")
        mod_done = sem("mod_done")
        cv_done, conv_done = sem("cv_done"), sem("conv_done")
        z_done = sem("z_done")
        x1_done = sem("x1_done")
        r_lg, r_exp, r_prob, r_sel = sem("r_lg"), sem("r_exp"), sem("r_prob"), sem("r_sel")
        e_rep, e_gath, e_xe, e_selTp, e_selT = (sem(n) for n in ("e_rep", "e_gath", "e_xe", "e_selTp", "e_selT"))
        e_sil, e_gu, e_hTp, e_hT = (sem(n) for n in ("e_sil", "e_gu", "e_hTp", "e_hT"))
        e_y, e_sc, e_acc = (sem(n) for n in ("e_y", "e_sc", "e_acc"))
        x2_done, x3_done = sem("x2_done"), sem("x3_done")
        g3_ready = sem("g3_ready")
        g3_free = [sem(f"g3_free{i}") for i in range(4)]
        w3_dn = sem("w3_dn")
        n3_sq, n3_ms, n3_rstd, n3_xn = (sem(n) for n in ("n3_sq", "n3_ms", "n3_rstd", "n3_xn"))
        h_sq, h_rstd, h_ms = sem("h_sq"), sem("h_rstd"), sem("h_ms")
        d_sq, d_rstd, d_ms = sem("d_sq"), sem("d_rstd"), sem("d_ms")
        lat_n, rope_q, rope_k, mix_done = (sem(n) for n in ("lat_n", "rope_q", "rope_k", "mix_done"))
        xm_done, nab_done = sem("xm_done"), sem("nab_done")
        in_t5, in_na, in_fin, in_lam = sem("in_t5"), sem("in_na"), sem("in_fin"), sem("in_lam")
        in_rel, rel_st, rel_rep, rel_na = sem("in_rel"), sem("rel_st"), sem("rel_rep"), sem("rel_na")
        lam_s, lam_e = sem("lam_s"), sem("lam_e")
        y_out = sem("y_out")
        k_s, k_min, k_exp, k_t, k_p, k_o, k_done = (sem(n) for n in ("k_s", "k_min", "k_exp", "k_t", "k_p", "k_o", "k_done"))
        in_post = sem("in_post")
        kb_done, gn_done, m_done, y_done, x4_done = (sem(n) for n in ("kb_done", "gn_done", "m_done", "y_done", "x4_done"))
        j_s, j_min, j_exp, j_t, j_p, j_o, j_done = (sem(n) for n in ("j_s", "j_min", "j_exp", "j_t", "j_p", "j_o", "j_done"))
        s_out = sem("s_out")
        rel_io = sem("rel_io")
        rel_src = sem("rel_src")

        def slot(n, m=RING):
            return ring[:, (n % m) * SLOT:(n % m + 1) * SLOT]

        PARTS = {U2AT["kvwg"]: 4, U2AT["w1"]: 2, U2AT["ab0"]: 2, U2AT["ab1"]: 2}

        def landed(n):
            return 16 * sum(PARTS.get(m, 1) for m in range(n % RING, n + 1, RING))

        landed2 = landed

        def landed3(n, l):
            per = 16 * sum(PARTS3.get(m, 1) for m in range(n % RING3, len(L3), RING3))
            return l * per + 16 * sum(PARTS3.get(m, 1) for m in range(n % RING3, n + 1, RING3))

        def piece(eng, i, l=None):
            if l is None:
                eng.wait_ge(g_ready, i + 1)
            else:
                eng.wait_ge(g3_ready, l * LPN + (i + 1))

        def bank_free(eng, i, l=None):
            if i >= 4:
                if l is None:
                    eng.wait_ge(g_free[i % 4], i // 4)
                else:
                    eng.wait_ge(g3_free[i % 4], l * (LPN // 4) + i // 4)

        def taken(eng, *idx, l=None):
            for i in idx:
                if l is None:
                    eng.wait_ge(g_free[i % 4], i // 4 + 1)
                else:
                    eng.wait_ge(g3_free[i % 4], l * (LPN // 4) + (i // 4 + 1))

        def G(i):
            return psum[:, i % 4, :]

        def job3(j, l):
            kind, h, c, t = JOBS3[j]
            qs = slice(t * P, t * P + P)
            if kind == "mla":
                return dict(q=qmT[0:96, h, qs], k=kmT[0:96, h, :], widths=[P] * TT, bias=None,
                            v=[vd[:, i, h * HD:h * HD + HD] for i in range(TT)],
                            out=mix[:, t, 768 + h * HD:832 + h * HD], coef=None, first=True)
            b = ("na", "diff", "dil").index(kind)
            lo, n = (HD * (h % 2), HD) if kind != "diff" else (HD * (h % 2) + 32 * c, 32)
            bias = nab[:, h, t, :] if kind == "na" else t5b[:, h + 4 * (kind == "dil"), t, :]
            return dict(q=qk[lo:lo + n, 4 * b + h // 2, qs], k=qk[lo:lo + n, 4 * b + 2 + h // 2, :], widths=[P] * TT,
                        bias=bias, v=[v3[:, b, i, h * HD:h * HD + HD] for i in range(TT)],
                        out=mix[:, t, 256 * b + h * HD:256 * b + h * HD + HD],
                        coef=lamneg[:, bass.ds(l, 1)] if c else None, first=c == 0)

        def job2(j):
            br, h, t = JOBS2[j]
            lo = HD * (h % 2)
            g = h // 4
            qs = slice(t * P, t * P + P)
            part_ = slice(lo, lo + HD)
            out_ = (oB if br == "moba" else oA)[:, t, h * HD:h * HD + HD]
            dist = K("dist")[:, 0:P] if t == 0 else K("dist")[:, P:P + T]
            nk = P * (t + 1)
            if br == "cmp":
                return dict(q=qaT[part_, h // 2, qs], k=kcT[part_, g * NCMP:(g + 1) * NCMP], widths=[NCMP],
                            dist=K("cmpdist")[:, 16 * t:16 * t + NCMP], slope=slope(2 * h),
                            v=[vcn[0:NCMP, g, :]], out=out_, coef=gn[:, t, h:h + 1], first=True)
            if br == "moba":
                return dict(q=qbT[part_, h // 2, qs], k=kbT[part_, h // 2, 0:nk], widths=[P] * (t + 1), dist=dist,
                            slope=slope(2 * h + 1), v=[vbn[:, i, h * HD:h * HD + HD] for i in range(t + 1)],
                            out=out_, coef=None, first=True)
            kk, vv, i = (ksT, vs, 1) if br == "slc" else (kwT, vw, 2)
            return dict(q=qaT[part_, h // 2, qs], k=kk[part_, g, 0:nk], widths=[P] * (t + 1), dist=dist,
                        slope=slope(2 * h), v=[vv[:, u, g * HD:g * HD + HD] for u in range(t + 1)],
                        out=out_, coef=gn[:, t, 8 * i + h:8 * i + h + 1], first=False)

        block = ctx.enter_context(nc.Block())

        @block.sync
        def _(sp):
            sp.dma_start(vrow[0:48, 0, :], a["b_ada"].rearrange("l (r n) -> (l r) n", n=P)).then_inc(in_vec, 16)
            for r0, n, t in ((48, 8, a["g_norm_mix"]), (56, 8, a["g_norm_moe"]), (64, 8, a["c"]),
                             (88, 8, None), (96, 16, a["b_gate"])):
                if t is not None:
                    sp.dma_start(vrow[r0:r0 + n, 0, :], t.rearrange("l (r n) -> (l r) n", n=P)).then_inc(in_vec, 16)
            sp.dma_start(vrow[72:96, 0, :], a["w_conv"].rearrange("l w (r n) -> (l w r) n", n=P)).then_inc(in_vec, 16)
            r0 = 0
            for t in ("norm_pre_2", "attn_norm_3", "ffn_norm_3", "mla_q_norm_3", "mla_kv_norm_3"):
                v = a[t].rearrange("l (r n) -> (l r) n", n=P)
                sp.dma_start(vrow[r0:r0 + v.shape[0], 1, :], v).then_inc(in_vec, 16)
                r0 += v.shape[0]
            for t in ("cmp_pe_k_2", "cmp_pe_v_2"):
                sp.dma_start(vrow[r0:r0 + 16, 1, :], a[t].rearrange("l (r c) d -> (l r) (c d)", c=2)).then_inc(in_vec, 16)
                r0 += 16
            sp.dma_start(t5tab[0:32, :], a["t5_table_3"]).then_inc(in_rel, 16)
            sp.dma_start(lamraw, a["diff_lambda_3"].rearrange("l c n -> l (c n)").partition_broadcast(P)).then_inc(in_lam, 16)
            sp.dma_start(subg, a["diff_subln_3"].partition_broadcast(P)).then_inc(in_lam, 16)
            sp.dma_start(cst, a["c_kept"]).then_inc(in_cst, 16)
            sp.dma_start(x, a["x"].rearrange("b (t p) d -> p (b t) d", p=P)).then_inc(in_x, 16)

            def unit(n, *moves):
                if n >= RING:
                    sp.wait_ge(g_ready, LAST[n - RING] + 1)
                for dst, src in moves:
                    sp.dma_start(dst, src).then_inc(w_ready[n % RING], 16)

            def cols(w, c0, n, kt=KT):
                return w.rearrange("l (k p) n -> p (l k) n", p=P)[:, 0:kt, c0:c0 + n]

            def dst(n, kt, c, at=0):
                return slot(n)[:, at:at + kt * c].rearrange("p (k c) -> p k c", k=kt)

            for i in range(12):
                n = UAT[f"ada{i}"]
                unit(n, (dst(n, KT, 512), cols(a["w_ada"], 512 * i, 512)))
                if i == 0:
                    sp.dma_start(gate_m, a["b_ada"][:, 2 * D:3 * D].partition_broadcast(P).squeeze(1)).then_inc(in_b1, 16)
                    sp.dma_start(gate_f, a["b_ada"][:, 5 * D:6 * D].partition_broadcast(P).squeeze(1)).then_inc(in_b1, 16)
                    sp.dma_start(dfts, a["c_dft"][:, 0:TT * 2 * T].rearrange("p (k n) -> p k n", k=TT)).then_inc(in_b1, 16)
                    sp.dma_start(dftg, a["c_dft"][:, TT * 2 * T:].rearrange("p (k n) -> p k n", k=2)).then_inc(in_b1, 16)
                    sp.dma_start(arena[:, 3 * D:3 * D + 1024], a["c_moe"]).then_inc(in_moe, 16)
                    sp.dma_start(gbc, a["g_final"].unsqueeze(0).partition_broadcast(P).squeeze(1)).then_inc(in_moe, 16)
            for i in range(11):
                n = UAT[f"win{i}"]
                unit(n, (dst(n, KT, 512), cols(a["w_in"], 512 * i, 512)))
            for i in range(2):
                n = UAT[f"wf{i}"]
                unit(n, (dst(n, 4, 512), cols(a["w_fourier"], 512 * i, 512, 4)))
            for nm, w in (("wc", "w_conv_out"), ("wo", "w_o")):
                for i in range(2):
                    n = UAT[f"{nm}{i}"]
                    unit(n, (dst(n, KT, 512), cols(a[w], 512 * i, 512)))
            wg = a["w_gate_e"].rearrange("l e (k p) f -> p (l e k) f", p=P)
            wu = a["w_up_e"].rearrange("l e (k p) f -> p (l e k) f", p=P)
            wd = a["w_down_e"].rearrange("l e (k p) d -> p (l e k) d", p=P)

            def expert_unit(e, i):
                n = N_MOE + i
                if i < 8:
                    w = wg if i < 4 else wu
                    src = w[:, bass.ds(e * KT + 2 * (i % 4), 2), :]
                    d = slot(n).rearrange("p (k c) -> p k c", k=2)
                else:
                    src = wd[:, bass.ds(e * (FE // P) + 4 * (i - 8), 4), :]
                    d = slot(n).rearrange("p (k c) -> p k c", k=4)
                sp.dma_start(d, src).then_inc(w_ready[n % RING], 16)

            for i in range(RING):
                sp.wait_ge(g_ready, LAST[N_MOE + i - RING] + 1)
                expert_unit(0, i)
            with sp.Fori(0, NE - 1) as e:
                for i in range(RING, UPE):
                    sp.wait_ge(e_unit, e * UPE + (i - RING + 1))
                    expert_unit(e, i)
                for i in range(RING):
                    sp.wait_ge(e_unit, e * UPE + (i + RING + 1))
                    expert_unit(e + 1, i)
            for i in range(RING, UPE):
                sp.wait_ge(e_unit, (NE - 1) * UPE + (i - RING + 1))
                expert_unit(NE - 1, i)
            def unit2(name, *moves):
                n = U2AT[name]
                if n - RING < N_MOE + NE * UPE:
                    sp.wait_ge(e_unit, n - RING - N_MOE + 1)
                else:
                    sp.wait_ge(g_ready, LAST[n - RING] + 1)
                for d, src in moves:
                    sp.dma_start(d, src).then_inc(w_ready[n % RING], 16)

            def w2cols(name, c0, n):
                unit2(name, (dst(U2AT[name], KT, n), cols(a["w_in_2"], c0, n)))

            w2cols("qa", 0, 512)
            w2cols("kv", 512, 512)
            n = U2AT["kvwg"]
            unit2("kvwg", (dst(n, KT, 280), cols(a["w_in_2"], 1024, 280)),
                  (dst(n, 1, HD, KT * 280), cols(a["cmp_w2_k_2"], 0, HD, 1)),
                  (dst(n, 1, HD, KT * 280 + HD), cols(a["cmp_w2_k_2"], 0, HD, 1)),
                  (dst(n, 1, HD, KT * 280 + P), cols(a["cmp_w2_v_2"], 0, HD, 1)))
            n = U2AT["w1"]
            unit2("w1", *[(dst(n, 16, P, 2048 * i), a[f"cmp_w1_{c}_2"].rearrange("o (l c) d e -> (c d) (o l) e", c=2))
                          for i, c in enumerate("kv")])
            for nm, c0 in (("za", 1304), ("qb", 1816), ("kb", 2328), ("vb", 2840), ("zb", 3352), ("mg0", 3864),
                           ("mg1", 4376), ("mg2", 4888), ("mg3", 5400)):
                w2cols(nm, c0, 512)
            for i in range(2):
                n = U2AT[f"ab{i}"]
                unit2(f"ab{i}", (dst(n, 4, 512), cols(a["w_branch_a_2"], 512 * i, 512, 4)),
                      (dst(n, 4, 512, 2048), cols(a["w_branch_b_2"], 512 * i, 512, 4)))
            for i in range(2):
                n = U2AT[f"wo2_{i}"]
                unit2(f"wo2_{i}", (dst(n, KT, 512), cols(a["w_o_2"], 512 * i, 512)))
            sp.wait_ge(g_ready, LAST[U2AT["mg3"]] + 1)
            sp.wait_ge(rel_rep, 16)
            for h in range(8):
                for t in range(TT):
                    o = T - 1 - t * P
                    src = t5_rep[h, o:o + P * (REL - 1)].rearrange("(q w) -> q w", w=REL - 1)[:, 0:T]
                    sp.dma_start(t5b[:, h, t, :], src).then_inc(in_t5, 16)

            for l in range(LAYERS):
                def unit3(name, *moves):
                    n = L3AT[name]
                    if n < RING3 and l == 0:
                        prev = max(m for m in range(N_U12) if m % RING == n)
                        sp.wait_ge(g_ready, LAST[prev] + 1)
                    else:
                        m, ll = (n - RING3, l) if n >= RING3 else (n + len(L3) - RING3, l - 1)
                        if m in LAST3:
                            sp.wait_ge(g3_ready, ll * LPN + LAST3[m] + 1)
                        else:
                            sp.wait_ge(w3_dn, ll * 5 + m - L3AT["dn0"] + 1)
                    for d, src in moves:
                        sp.dma_start(d, src).then_inc(w3_ready[n % RING3], 16)

                def dst3(n, kt, c, at=0):
                    return slot(n, RING3)[:, at:at + kt * c].rearrange("p (k c) -> p k c", k=kt)

                def kcols(w, c0, n, k0=0, kt=KT):
                    return w[l, k0 * P:(k0 + kt) * P, c0:c0 + n].rearrange("(k p) n -> p k n", p=P)

                for i in range(5):
                    unit3(f"win{i}", (dst3(L3AT[f"win{i}"], KT, 512), kcols(a["w_in_3"], 512 * i, 512)))
                n = L3AT["win5"]
                unit3("win5", (dst3(n, KT, 160), kcols(a["w_in_3"], 2560, 160)),
                      (dst3(n, 2, 384, KT * 160), kcols(a["w_uq_3"], 0, 384, 0, 2)),
                      (dst3(n, 1, 512, KT * 160 + 768), kcols(a["w_ukv_3"], 0, 512, 0, 1)))
                for i in range(2):
                    unit3(f"wo{i}", (dst3(L3AT[f"wo{i}"], KT, 512), kcols(a["w_o_3"], 512 * i, 512)))
                for i in range(11):
                    n = L3AT[f"gu{i}"]
                    d = dst3(n, KT, 512)
                    unit3(f"gu{i}", (d[:, :, 0:256], kcols(a["w_gate_3"], 256 * i, 256)),
                          (d[:, :, 256:512], kcols(a["w_up_3"], 256 * i, 256)))
                for i in range(6):
                    kt = min(4, FT - 4 * i)
                    unit3(f"dn{i}", (dst3(L3AT[f"dn{i}"], kt, D), kcols(a["w_down_3"], 0, D, 4 * i, kt)))
            sp.wait_ge(y_out, 2)
            sp.dma_start(out.rearrange("b (t p) d -> p (b t) d", p=P), x).then_inc(s_out, 16)
            sp.wait_ge(s_out, 16)

        @block.gpsimd
        def _(pool):
            nc.gpsimd.memset(neghalf, -0.5).then_inc(consts_set, 1)
            nc.gpsimd.memset(csil.rearrange("p k n -> p (k n)"), 0.0).then_inc(consts_set, 1)
            nc.gpsimd.memset(cv.rearrange("p k t -> p (k t)"), 0.0).then_inc(consts_set, 1)
            nc.gpsimd.memset(narow, 0.0).then_inc(consts_set, 1)
            nc.gpsimd.memset(halfs, -0.5).then_inc(consts_set, 1)

            def rstd_of(k):
                pool.wait_ge(n_sq, 2 * k + 2)
                nc.gpsimd.tensor_scalar(rstd, ssq, 1.0 / D, EPS, ALU.mult, ALU.add).then_inc(n_ms, 1)
                pool.wait_ge(n_ms, k + 1)
                if k == 0:
                    pool.wait_ge(consts_set, 1)
                nc.gpsimd.tensor_tensor(rstd, rstd, neghalf, ALU.pow).then_inc(n_rstd, 1)

            rstd_of(0)
            pool.wait_ge(consts_set, 4)
            for l in range(LAYERS):
                for h in range(4):
                    r = (l * 4 + h) * 7
                    pool.dma_start(narow[r:r + 7, 48:79], a["na_rpb_3"][l, h, 4:11, :]).then_inc(rel_na, 16)
            pool.wait_ge(rel_na, 16 * 8)
            pool.dma_start(na_row, narow[0:56, :]).then_inc(rel_na, 16)
            pool.wait_ge(rel_src, 1)
            pool.dma_start(t5_row, t5vec[0:8, :]).then_inc(rel_st, 16)
            pool.wait_ge(rel_na, 16 * 9)
            pool.dma_start(na_rep.rearrange("r (q n) -> r q n", q=GRID_W),
                           na_row.unsqueeze(1).broadcast_to([56, GRID_W, NAREL])).then_inc(rel_na, 16)
            pool.wait_ge(rel_st, 16)
            pool.dma_start(t5_rep[:, 0:P * REL].rearrange("r (q n) -> r q n", q=P),
                           t5_row.unsqueeze(1).broadcast_to([8, P, REL])).then_inc(rel_rep, 16)
            pool.wait_ge(rel_na, 16 * 10)
            pool.wait_ge(x1_done, 4)
            pool.dma_start(wr, a["w_router"].rearrange("l (k p) e -> p (l k) e", p=P)).then_inc(in_route, 16)
            pool.dma_start(brow, a["b_router"].partition_broadcast(P).squeeze(1)).then_inc(in_route, 16)
            rstd_of(1)
            nc.gpsimd.memset(acc.rearrange("p t d -> p (t d)"), 0.0).then_inc(e_acc, 1)
            rstd_of(2)
            pool.wait_ge(x3_done, 1)
            pool.dma_start(gbc, a["norm_post_2"].partition_broadcast(P).squeeze(1)).then_inc(in_post, 16)
            rstd_of(3)
            rstd_of(4)

            def roots(at_, dst_, src, widths, sq, ms, need, at):
                pool.wait_ge(sq, need)
                nc.gpsimd.tensor_tensor(spare[:, NJ3 + at_:NJ3 + at_ + 1], halfs[:, 0:1], halfs[:, 0:1], ALU.mult)
                for lo, hi, w in widths:
                    o = nc.gpsimd.tensor_scalar(dst_[:, lo:hi], src[:, lo:hi], 1.0 / w, EPS, ALU.mult, ALU.add)
                    o.then_inc(ms, 1)
                pool.wait_ge(ms, at)
                n = widths[-1][1]
                return nc.gpsimd.tensor_tensor(dst_[:, 0:n], dst_[:, 0:n], halfs[:, 0:n], ALU.pow)

            with pool.Fori(0, LAYERS) as l:
                pool.wait_ge(x4_done, l + 1)
                for h in range(4):
                    for t in range(TT):
                        for r in range(2):
                            qr = 2 * t + r
                            src = na_rep[bass.ds(l * 28 + (h * 7 + 3 - qr), 4), GRID_W - 1:GRID_W - 1 + GRID_W * (NAREL - 1)]
                            src = src.rearrange("r (q w) -> q r w", w=NAREL - 1)[:, :, 0:GRID_W]
                            pool.dma_start(nab[GRID_W * r:GRID_W * r + GRID_W, h, t, :].rearrange("p (r n) -> p r n", r=4),
                                           src).then_inc(in_na, 16)
                roots(0, rstd, ssq, [(0, 2, D)], n3_sq, n3_ms, l * 4 + 2, l * 2 + 1).then_inc(n3_rstd, 1)
                roots(1, hrstd, hstat, [(0, 2, 256), (2, 4, P)], h_sq, h_ms, l * 4 + 4, l * 2 + 2).then_inc(h_rstd, 1)
                roots(2, hrstd, hstat, [(0, 8, HD)], d_sq, d_ms, l + 1, l + 1).then_inc(d_rstd, 1)
                roots(3, rstd, ssq, [(0, 2, D)], n3_sq, n3_ms, l * 4 + 4, l * 2 + 2).then_inc(n3_rstd, 1)
            pool.dma_start(gbc, a["final_norm_3"].unsqueeze(0).partition_broadcast(P).squeeze(1)).then_inc(in_fin, 16)
            roots(4, rstd, ssq, [(0, 2, D)], n3_sq, n3_ms, LAYERS * 4 + 2, LAYERS * 2 + 1).then_inc(n3_rstd, 1)

        @block.scalar
        def _(act):
            def squares(xn, src=x, sq=n_sq):
                for t in range(TT):
                    nc.scalar.activation(xn[:, t, :], src[:, t, :], ACT.Square,
                                         accum_out=ssq[:, t:t + 1]).then_inc(sq, 1)

            act.wait_ge(v_cols, 1)
            act.wait_ge(consts_set, 2)
            nc.scalar.activation(csil[:, :, 0:1], vec1[:, 64:72].unsqueeze(2), ACT.Silu).then_inc(c_act, 1)
            act.wait_ge(in_x, 16)
            squares(xn1)
            act.wait_ge(lam_s, 1)
            nc.scalar.activation(lamexp, lamsum, ACT.Exp).then_inc(lam_e, 1)
            for u in range(12):
                i = AT[f"ada{u}"]
                piece(act, i)
                if u >= 2:
                    act.wait_ge(mod_mm, u - 1)
                nc.scalar.copy(part[:, u % 2, :], G(i)).then_inc(g_free[i % 4], 1)
            for i in (AT["uf0"], AT["uf1"]):
                piece(act, i)
                h = i - AT["uf0"]
                nc.scalar.copy(uf[:, :, 256 * h:256 * h + 256],
                               G(i).rearrange("p (t n) -> p t n", t=TT)).then_inc(g_free[i % 4], 1)
            for g in range(4):
                i = AT[f"dfta{g}"]
                piece(act, i)
                nc.scalar.copy(Bcs[:, g, :], G(i)).then_inc(g_free[i % 4], 1)
            for h in range(2):
                i = AT[f"dftb{h}"]
                piece(act, i)
                nc.scalar.copy(fmT[:, 2 * h:2 * h + 2, :],
                               G(i).rearrange("p (k t) -> p k t", k=2)).then_inc(g_free[i % 4], 1)
            for nm, dstT in (("v", vT), ("b", bT)):
                for h in range(4):
                    i = AT[f"{nm}{h}"]
                    piece(act, i)
                    nc.scalar.copy(dstT[:, 2 * h:2 * h + 2, :],
                                   G(i).rearrange("p (k t) -> p k t", k=2)).then_inc(g_free[i % 4], 1)
            for b, (nm, dstT) in enumerate((("ga", gaT), ("gb", gbT))):
                for h in range(4):
                    i = AT[f"{nm}{h}"]
                    piece(act, i)
                    for m in range(2):
                        k = 2 * h + m
                        o = nc.scalar.activation(dstT[:, k, :], G(i)[:, m * T:m * T + T], ACT.Sigmoid,
                                                 bias=vec1[:, 96 + 8 * b + k:97 + 8 * b + k])
                    o.then_inc(g_free[i % 4], 1)
            act.wait_ge(x1_done, 4)
            act.wait_ge(n_rstd, 1)
            act.wait_ge(n_xn, 1)
            squares(xn2)
            for h in range(4):
                i = AT[f"h2n{h}"]
                piece(act, i)
                nc.scalar.copy(h2n[:, h // 2, 512 * (h % 2):512 * (h % 2) + 512], G(i)).then_inc(g_free[i % 4], 1)
            act.wait_ge(r_lg, 1)
            for t in range(TT):
                nc.scalar.activation(ex[:, t, :], lg[:, t, :], ACT.Exp, bias=negmax[:, t:t + 1],
                                     accum_out=rsum[:, t:t + 1]).then_inc(r_exp, 1)
            with act.Fori(0, NE) as e:
                act.wait_ge(e_unit, e * UPE + 4)
                nc.scalar.activation(sil, psum[:, 0, :], ACT.Silu).then_inc(e_sil, 1)
                act.wait_ge(e_hTp, e + 1)
                nc.scalar.copy(hT.rearrange("p s n -> p (s n)"), psum[:, 3, :]).then_inc(e_hT, 1)
                act.wait_ge(e_unit, e * UPE + UPE)
                nc.scalar.copy(ysb, psum[:, 2, 0:T]).then_inc(e_y, 1)
            act.wait_ge(x2_done, 1)
            squares(xn2)

            act.wait_ge(x3_done, 1)
            squares(xn3)

            def take(name, d, func=ACT.Copy, scale=1.0, src=None, l=None):
                i = AT[name] if l is None else LAT[name]
                piece(act, i, l)
                src = G(i) if src is None else src(G(i))
                free = g_free if l is None else g3_free
                return nc.scalar.activation(d, src, func, scale=scale).then_inc(free[i % 4], 1)

            def two(g):
                return g.rearrange("p (k n) -> p k n", k=2)

            SC = HD ** -0.5
            for h in range(2):
                take(f"qa{h}", qaT[:, 2 * h:2 * h + 2, :], scale=-SC, src=two)
            take("vs", vs, src=lambda g: two(g[:, 0:2 * P]))
            take("vw", vw, src=lambda g: two(g[:, 0:2 * P]))
            take("gnsa", gn, ACT.Sigmoid, src=lambda g: two(g[:, 0:48]))
            take("hk", hk[:, :, 0:2 * NCMP], ACT.Silu, src=lambda g: two(g[:, 0:64])[:, :, 0:2 * NCMP])
            take("kcT", kcT[:, 0:2 * NCMP], src=lambda g: g[:, 0:2 * NCMP])
            take("vcn", vcn[0:NCMP, :, :], src=lambda g: two(g[0:NCMP, 0:2 * HD]))

            def exp_of(j, J, mins, exps, turned, ended, base=0):
                b = j % 2
                act.wait_ge(mins, base + (j + 1))
                nk = sum(J["widths"])
                if j >= 2:
                    act.wait_ge(turned, base + (j - 1))
                    act.wait_ge(ended, base + (j - 1))
                nc.scalar.activation(ebuf[:, b, 0:nk], sbuf[:, b, 0:nk], ACT.Exp, bias=jmin[:, b:b + 1], scale=-1.0,
                                     accum_out=jsum[:, b:b + 1]).then_inc(exps, 1)

            def probs_of(j, J, turned, used, probs, base=0):
                b = j % 2
                act.wait_ge(turned, base + (j + 1))
                if j >= 2:
                    act.wait_ge(used, base + (j - 1))
                w = J["widths"]
                d = pbuf[0:w[0], b, 0:len(w) * P]
                nc.scalar.copy(d, psum[0:w[0], 6, 0:len(w) * P]).then_inc(probs, 1)

            for kind, n in PLAN2:
                if kind == "job":
                    exp_of(n, job2(n), j_min, j_exp, j_t, j_done)
                    if n >= 1:
                        probs_of(n - 1, job2(n - 1), j_t, j_o, j_p)
                    continue
                h = int(n[-1])
                if n[:2] == "za":
                    take(n, zA[:, :, 256 * h:256 * h + 256], ACT.Silu, src=two)
                elif n[:2] == "zb":
                    take(n, zB[:, :, 256 * h:256 * h + 256], ACT.Silu, src=two)
                elif n[:2] == "qb":
                    take(n, qbT[:, 2 * h:2 * h + 2, :], scale=-SC, src=two)
                elif n[:2] == "kb":
                    take(n, kbT[:, 2 * h:2 * h + 2, :], src=two)
                elif n[:2] == "vb":
                    take(n, vbn[:, :, 256 * h:256 * h + 256], src=two)
                else:
                    take(n, (mAT if n[1] == "A" else mBT)[:, 2 * h:2 * h + 2, :], ACT.Sigmoid, src=two)
            probs_of(len(JOBS2) - 1, job2(len(JOBS2) - 1), j_t, j_o, j_p)
            for h in range(4):
                take(f"yt{h}", yT[:, 2 * h:2 * h + 2, :], src=two)
            for h in range(4):
                take(f"wo2_{h}", mixn[:, :, 256 * h:256 * h + 256], src=two)
            nc.scalar.drain()
            squares(yjunk, mixn)

            Q = {"qa0": (0, -SC), "ka0": (2, 1.0), "qb0": (4, -((HD // 2) ** -0.5)), "kb0": (6, 1.0), "qc0": (8, -SC),
                 "kc0": (10, 1.0)}
            with act.Fori(0, LAYERS) as l:
                act.wait_ge(x4_done, l + 1)
                squares(mix, sq=n3_sq)
                for kind, n in PLAN3:
                    if kind == "job":
                        exp_of(n, job3(n, l), k_min, k_exp, k_t, k_done, l * NJ3)
                        if n >= 1:
                            probs_of(n - 1, job3(n - 1, l), k_t, k_o, k_p, l * NJ3)
                        continue
                    if n in Q:
                        at, sc = Q[n]
                        take(n, qk[:, at:at + 2, :], scale=sc, src=two, l=l)
                    elif n in ("va0", "vb0", "vc0"):
                        take(n, v3[:, "abc".index(n[1]), :, :], src=two, l=l)
                    elif n == "cq":
                        take(n, cqn, src=two, l=l)
                    elif n == "ckv":
                        take(n, ckvn, src=lambda g: two(g[:, 0:2 * P]), l=l)
                    elif n == "kr":
                        take(n, krn, src=lambda g: two(g[:, 0:64]), l=l)
                        nc.scalar.drain()
                        for t in range(TT):
                            nc.scalar.activation(cqT[:, t, :], cqn[:, t, :], ACT.Square,
                                                 accum_out=hstat[:, t:t + 1]).then_inc(h_sq, 1)
                            nc.scalar.activation(ckvT[:, 0, t * P:t * P + P], ckvn[:, t, :], ACT.Square,
                                                 accum_out=hstat[:, 2 + t:3 + t]).then_inc(h_sq, 1)
                    elif n[:2] == "uq":
                        t = int(n[-1])
                        take(n, qdn[:, t, :, :], scale=-(96.0 ** -0.5),
                             src=lambda g: g[:, 0:384].rearrange("p (h n) -> p h n", h=4), l=l)
                    elif n[:3] == "ukv":
                        t = int(n[-1])
                        i = LAT[n]
                        piece(act, i, l)
                        g = G(i).rearrange("p (h c n) -> p h c n", h=4, c=2)
                        nc.scalar.copy(kcat[:, t, :, 0:HD], g[:, :, 0, :])
                        nc.scalar.copy(vd[:, t, :].rearrange("p (h n) -> p h n", h=4),
                                       g[:, :, 1, :]).then_inc(g3_free[i % 4], 1)
                    elif n[:2] in ("qm", "km"):
                        h = 2 * int(n[-1])
                        take(n, (qmT if n[0] == "q" else kmT)[0:96, h:h + 2, :], src=lambda g: two(g[0:96, :]), l=l)
                probs_of(NJ3 - 1, job3(NJ3 - 1, l), k_t, k_o, k_p, l * NJ3)
                for h in range(4):
                    take(f"mix{h}", mixT[:, 2 * h:2 * h + 2, :], src=two, l=l)
                act.wait_ge(xm_done, l * 4 + 4)
                squares(mix, sq=n3_sq)
                for i in range(11):
                    take(f"gu{2 * i}", actT[:, 2 * i:2 * i + 2, :], ACT.Silu, src=two, l=l)
            act.wait_ge(x4_done, LAYERS + 1)
            squares(mix, sq=n3_sq)

        @block.tensor
        def _(pe):
            def mm(o, l, r, s=True, e=True):
                return nc.tensor.matmul(o, l, r, start=s, stop=e)

            def unit(n):
                pe.wait_ge(w_ready[n % RING], landed(n))

            def ready(o, l):
                return o.then_inc(g_ready if l is None else g3_ready, 1)

            def rows(i, w, kt, c0, width, xs, l=None):
                bank_free(pe, i, l)
                for t in range(TT):
                    for k in range(kt):
                        o = mm(G(i)[:, t * width:(t + 1) * width], xs[:, k, t * P:t * P + P], w[:, k, c0:c0 + width],
                               k == 0, k == kt - 1)
                return ready(o, l)

            def colsT(i, w, kt, c0, xs, ms=2, k0=0, l=None):
                bank_free(pe, i, l)
                for m in range(ms):
                    for k in range(kt):
                        o = mm(G(i)[:, m * T:m * T + T], w[:, k, c0 + m * P:c0 + m * P + P], xs[:, k0 + k, :],
                               k == 0, k == kt - 1)
                return ready(o, l)

            def turn_x(first, src, l=None):
                for h in range(4):
                    i = first + h
                    bank_free(pe, i, l)
                    for m in range(2):
                        for t in range(TT):
                            k = 2 * h + m
                            o = nc.tensor.transpose(G(i)[:, m * T + t * P:m * T + t * P + P],
                                                    src[:, t, k * P:k * P + P], ident)
                    ready(o, l)

            pe.wait_ge(in_vec, 16 * 13)
            pe.wait_ge(in_cst, 16)
            nc.tensor.transpose(psum[:, 5, 0:112], vrow[0:112, 0, :], ident[0:112, 0:112])
            nc.tensor.transpose(psum[:, 5, 128:206], vrow[0:78, 1, :], ident[0:78, 0:78]).then_inc(v_used, 1)
            pe.wait_ge(in_rel, 16)
            mm(psum[0:8, 7, :], t5tab[0:32, :], K("t5hot")[0:32, :]).then_inc(v_used, 1)
            pe.wait_ge(rel_src, 1)
            pe.wait_ge(c_act, 1)

            def mod_second(u):
                taken(pe, AT[f"ada{u}"])
                if u not in GATE_UNITS:
                    for s in range(4):
                        o = mm(psum[:, 4, 4 * u + s:4 * u + s + 1], part[:, u % 2, s * P:s * P + P], ones[:, 0:1])
                    o.then_inc(mod_mm, 1)
                else:
                    r = GATE_UNITS.index(u)
                    if r >= 2:
                        pe.wait_ge(mod_done, r - 1)
                    mm(psum[:, 6 + r % 2, :], ones, part[:, u % 2, :]).then_inc(mod_mm, 1)

            for u in range(12):
                i, n = AT[f"ada{u}"], UAT[f"ada{u}"]
                unit(n)
                bank_free(pe, i)
                w = slot(n).rearrange("p (k c) -> p k c", k=KT)
                for k in range(2):
                    for j in range(4):
                        o = mm(G(i)[32 * j:32 * j + 32, :], csil[:, 2 * j + k, :], w[:, 2 * j + k, :], k == 0, k == 1)
                o.then_inc(g_ready, 1)
                if u >= 1:
                    mod_second(u - 1)
            mod_second(11)

            def W(n, kt, c, at=0):
                return slot(n)[:, at:at + kt * c].rearrange("p (k c) -> p k c", k=kt)

            pe.wait_ge(n_xn, 1)
            turn_x(AT["n1_0"], xn1)
            taken(pe, *range(AT["n1_0"], AT["n1_0"] + 4))
            unit(UAT["win0"])
            for h in range(2):
                rows(AT[f"uf{h}"], W(UAT["win0"], KT, 512), KT, 256 * h, 256, xT)
            taken(pe, AT["uf0"], AT["uf1"])
            pe.wait_ge(in_b1, 16 * 4)
            for g in range(4):
                i = AT[f"dfta{g}"]
                bank_free(pe, i)
                for k in range(TT):
                    o = mm(G(i), uf[:, k, g * P:g * P + P], dfts[:, k, :], k == 0, k == 1)
                o.then_inc(g_ready, 1)
            for h in range(2):
                i = AT[f"dftb{h}"]
                bank_free(pe, i)
                for m in range(2):
                    g = 2 * h + m
                    taken(pe, AT[f"dfta{g}"])
                    for c in range(2):
                        o = mm(G(i)[:, m * T:m * T + T], dftg[:, c, :], Bcs[:, g, c * T:c * T + T], c == 0, c == 1)
                o.then_inc(g_ready, 1)
            for b, nm in enumerate(("v", "b", "c", "ga", "gb")):
                for h in range(4):
                    n = UAT["win1"] + 2 * b + h // 2
                    unit(n)
                    colsT(AT[f"{nm}{h}"], W(n, KT, 512), KT, 256 * (h % 2), xT)
            taken(pe, AT["dftb0"], AT["dftb1"])
            for h in range(4):
                n = UAT["wf0"] + h // 2
                unit(n)
                colsT(AT[f"wf{h}"], W(n, 4, 512), 4, 256 * (h % 2), fmT)
            pe.wait_ge(conv_done, KT)
            for h in range(4):
                n = UAT["wc0"] + h // 2
                unit(n)
                colsT(AT[f"wc{h}"], W(n, KT, 512), KT, 256 * (h % 2), bT)
            pe.wait_ge(z_done, 4)
            for h in range(4):
                n = UAT["wo0"] + h // 2
                unit(n)
                rows(AT[f"wo{h}"], W(n, KT, 512), KT, 256 * (h % 2), 256, gaT)

            pe.wait_ge(n_xn, 2)
            turn_x(AT["n2_0"], xn2)
            taken(pe, *range(AT["n2_0"], AT["n2_0"] + 4))
            for h in range(4):
                i = AT[f"h2n{h}"]
                bank_free(pe, i)
                for m in range(4):
                    k = 4 * (h % 2) + m
                    o = nc.tensor.transpose(G(i)[:, m * P:m * P + P], xT[:, k, (h // 2) * P:(h // 2) * P + P], ident)
                o.then_inc(g_ready, 1)
            pe.wait_ge(in_moe, 16 * 2)
            pe.wait_ge(in_route, 16 * 2)
            rows(AT["rt"], wr, KT, 0, NE, xT)
            pe.wait_ge(r_prob, 1)
            i = AT["pt"]
            bank_free(pe, i)
            for t in range(TT):
                o = nc.tensor.transpose(G(i)[0:NE, t * P:t * P + P], prob[:, t, :], ident)
            o.then_inc(g_ready, 1)
            pe.wait_ge(r_sel, 1)
            i = AT["mk"]
            bank_free(pe, i)
            for t in range(TT):
                o = nc.tensor.transpose(G(i)[:, t * NE:t * NE + NE], mk[0:NE, t * P:t * P + P], ident[0:NE, 0:NE])
            o.then_inc(g_ready, 1)
            taken(pe, AT["mk"])
            i = AT["pos"]
            bank_free(pe, i)
            for t in range(TT):
                for k in range(TT):
                    o = mm(G(i)[:, t * NE:t * NE + NE], tri[:, k, t * P:t * P + P], maskn[:, k, :], k == 0, k == 1)
            o.then_inc(g_ready, 1)
            pe.wait_ge(r_sel, 2)
            taken(pe, *range(AT["pos"] - 3, AT["pos"] + 1))
            taken(pe, *range(AT["h2n0"], AT["h2n0"] + 4))

            with pe.Fori(0, NE) as e:
                for k in range(KT):
                    for t in range(TT):
                        o = mm(psum[:, 3, k * CAP:k * CAP + CAP], h2n[:, t, k * P:k * P + P],
                               sel[:, t, bass.ds(e * CAP, CAP)], t == 0, t == 1)
                o.then_inc(e_gath, 1)
                pe.wait_ge(e_rep, e + 1)
                for t in range(TT):
                    o = nc.tensor.transpose(psum[:, 2, t * P:t * P + P], rep[:, t, :, :].rearrange("p j c -> p (j c)"), ident)
                o.then_inc(e_selTp, 1)
                pe.wait_ge(e_xe, e + 1)
                for i in range(8):
                    n = N_MOE + i
                    pe.wait_ge(w_ready[n % RING], e * (16 * UPE // RING) + landed(n))
                    w = slot(n).rearrange("p (k c) -> p k c", k=2)
                    for k in range(2):
                        kk = 2 * (i % 4) + k
                        for j in range(4):
                            o = mm(psum[32 * j:32 * j + 32, i // 4, :], xeT[:, kk, :], w[:, k, 512 * j:512 * j + 512],
                                   kk == 0, kk == KT - 1)
                    o.then_inc(e_unit, 1)
                pe.wait_ge(e_gu, e + 1)
                for s in range(4):
                    o = nc.tensor.transpose(psum[:, 3, s * P:s * P + P], gu[:, s * P:s * P + P], ident)
                o.then_inc(e_hTp, 1)
                pe.wait_ge(e_hT, e + 1)
                pe.wait_ge(e_selT, e + 1)
                for q in range(4):
                    n = N_MOE + 8 + q
                    pe.wait_ge(w_ready[n % RING], e * (16 * UPE // RING) + landed(n))
                    w = slot(n).rearrange("p (k c) -> p k c", k=4)
                    for s in range(4):
                        for j in range(4):
                            o = mm(psum[32 * j:32 * j + 32, 2, 0:T], hT[:, s, 32 * q:32 * q + 32],
                                   w[:, s, T * j:T * j + T], q == 0 and s == 0, q == 3 and s == 3)
                    o.then_inc(e_unit, 1)
                pe.wait_ge(e_y, e + 1)
                pe.wait_ge(e_acc, e + 1)
                for t in range(TT):
                    for j in range(4):
                        o = mm(psum[:, 4 + j, t * T:t * T + T], selT[32 * j:32 * j + 32, t * P:t * P + P],
                               ysb[32 * j:32 * j + 32, :])
                o.then_inc(e_sc, 1)

            pe.wait_ge(n_xn, 3)
            turn_x(AT["n3_0"], xn3)
            taken(pe, *range(AT["n3_0"], AT["n3_0"] + 4))

            def unit2(n):
                pe.wait_ge(w_ready[n % RING], landed2(n))

            unit2(U2AT["qa"])
            for h in range(2):
                colsT(AT[f"qa{h}"], W(U2AT["qa"], KT, 512), KT, 256 * h, xT)
            unit2(U2AT["kv"])
            w = W(U2AT["kv"], KT, 512)
            colsT(AT["kc"], w, KT, 0, xT)
            colsT(AT["ks"], w, KT, 256, xT, ms=1)
            rows(AT["vs"], w, KT, 384, P, xT)
            unit2(U2AT["kvwg"])
            w = W(U2AT["kvwg"], KT, 280)
            colsT(AT["kw"], w, KT, 0, xT, ms=1)
            rows(AT["vw"], w, KT, P, P, xT)
            rows(AT["gnsa"], w, KT, 256, 24, xT)
            unit2(U2AT["w1"])
            i = AT["hk"]
            bank_free(pe, i)
            pe.wait_ge(kb_done, 1)
            for c in range(2):
                w = W(U2AT["w1"], 16, P, 2048 * c)
                for l in range(16):
                    o = mm(G(i)[:, 32 * c:32 * c + 2 * NCMP], w[:, l, :], kb2[:, c, l, 0:2 * NCMP], l == 0, l == 15)
            o.then_inc(g_ready, 1)
            taken(pe, AT["hk"])
            i = AT["kcT"]
            bank_free(pe, i)
            w = slot(U2AT["kvwg"])[:, KT * 280:KT * 280 + 3 * HD]
            mm(G(i)[:, 0:2 * NCMP], w[:, 0:P], hk[:, 0, 0:2 * NCMP]).then_inc(g_ready, 1)
            i = AT["vcn"]
            bank_free(pe, i)
            for g in range(2):
                o = mm(G(i)[0:NCMP, g * HD:g * HD + HD], hk[:, 1, g * NCMP:g * NCMP + NCMP], w[:, P:P + HD])
            o.then_inc(g_ready, 1)

            def scores(j, J, s_, m_, base=0):
                if j >= 2:
                    pe.wait_ge(m_, base + (j - 1))
                mm(psum[:, 4 + j % 2, 0:sum(J["widths"])], J["q"], J["k"]).then_inc(s_, 1)

            def turn(j, J, x_, p_, t_, base=0):
                pe.wait_ge(x_, base + (j + 1))
                if j >= 1:
                    pe.wait_ge(p_, base + j)
                at = 0
                for i, w in enumerate(J["widths"]):
                    o = nc.tensor.transpose(psum[0:w, 6, i * P:i * P + P], ebuf[:, j % 2, at:at + w], ident)
                    at += w
                o.then_inc(t_, 1)

            def values(j, J, p_, d_, o_, base=0):
                pe.wait_ge(p_, base + (j + 1))
                if j >= 1:
                    pe.wait_ge(d_, base + j)
                n = len(J["widths"])
                for i, w in enumerate(J["widths"]):
                    o = mm(psum[:, 7, 0:HD], pbuf[0:w, j % 2, i * P:i * P + P], J["v"][i], i == 0, i == n - 1)
                o.then_inc(o_, 1)

            PW = {"za": "za", "zb": "zb", "qb": "qb", "kb": "kb", "vb": "vb"}
            NJ = len(JOBS2)
            taken(pe, *[AT[n] for n in ("qa0", "qa1", "ks", "kw", "vs", "vw", "kcT", "vcn")])
            for kind, n in PLAN2:
                if kind == "job":
                    if n == len(NSA_JOBS):
                        taken(pe, *[AT[m] for m in ("qb0", "qb1", "kb0", "kb1", "vb0", "vb1")])
                    scores(n, job2(n), j_s, j_min)
                    if n >= 1:
                        turn(n - 1, job2(n - 1), j_exp, j_p, j_t)
                    if n >= 2:
                        values(n - 2, job2(n - 2), j_p, j_done, j_o)
                    continue
                h = int(n[-1])
                if n[0] == "m":
                    u = U2AT["mg0"] + (n[1] == "B") * 2 + h // 2
                    unit2(u)
                    colsT(AT[n], W(u, KT, 512), KT, 256 * (h % 2), xT)
                else:
                    u = U2AT[n[:2]]
                    unit2(u)
                    f = colsT if n[0] in "qk" else (lambda i, w, kt, c0, xs: rows(i, w, kt, c0, 256, xs))
                    f(AT[n], W(u, KT, 512), KT, 256 * h, xT)
            turn(NJ - 1, job2(NJ - 1), j_exp, j_p, j_t)
            for j in (NJ - 2, NJ - 1):
                values(j, job2(j), j_p, j_done, j_o)
            pe.wait_ge(y_done, 1)
            for h in range(4):
                i = AT[f"yt{h}"]
                bank_free(pe, i)
                src = (oA, oB)[h // 2]
                for m in range(2):
                    for t in range(TT):
                        k = 2 * (h % 2) + m
                        o = nc.tensor.transpose(G(i)[:, m * T + t * P:m * T + t * P + P],
                                                src[:, t, k * P:k * P + P], ident)
                o.then_inc(g_ready, 1)
            taken(pe, *[AT[f"yt{h}"] for h in range(4)])
            for h in range(4):
                n = U2AT[f"ab{h // 2}"]
                unit2(n)
                if h % 2 == 0:
                    for b, nm in ((0, "wa"), (1, "wb")):
                        w = W(n, 4, 512, 2048 * b)
                        for m in range(2):
                            colsT(AT[f"{nm}{h + m}"], w, 4, 256 * m, yT, k0=4 * b)
            pe.wait_ge(m_done, 4)
            for h in range(4):
                n = U2AT[f"wo2_{h // 2}"]
                unit2(n)
                rows(AT[f"wo2_{h}"], W(n, KT, 512), KT, 256 * (h % 2), 256, mAT)

            pe.wait_ge(in_t5, 16 * 16)
            with pe.Fori(0, LAYERS) as l:
                def unit3(n):
                    pe.wait_ge(w3_ready[n % RING3], landed3(n, l))

                def W3(n, kt, c, at=0):
                    return slot(n, RING3)[:, at:at + kt * c].rearrange("p (k c) -> p k c", k=kt)

                pe.wait_ge(n3_xn, l * 2 + 1)
                turn_x(LAT["n4_0"], mix, l)
                taken(pe, *range(4), l=l)
                pe.wait_ge(nab_done, l + 1)
                win = ["qa0", "ka0", "va0", "qb0", "kb0", "vb0", "qc0", "kc0", "vc0", "cq"]
                done = set()
                for kind, n in PLAN3:
                    if kind == "job":
                        br = JOBS3[n][0]
                        if br not in done:
                            done.add(br)
                            need = {"na": ("qa0", "ka0", "va0"), "diff": ("qb0", "kb0", "vb0"),
                                    "dil": ("qc0", "kc0", "vc0"), "mla": ("qm0", "qm1", "km0", "km1", "ukv0", "ukv1")}[br]
                            taken(pe, *[LAT[m] for m in need], l=l)
                        scores(n, job3(n, l), k_s, k_min, l * NJ3)
                        if n >= 1:
                            turn(n - 1, job3(n - 1, l), k_exp, k_p, k_t, l * NJ3)
                        if n >= 2:
                            values(n - 2, job3(n - 2, l), k_p, k_done, k_o, l * NJ3)
                        continue
                    i = LAT[n]
                    if n in win:
                        at = win.index(n)
                        u = at // 2
                        unit3(u)
                        w = W3(u, KT, 512)
                        if n[0] == "v" or n == "cq":
                            rows(i, w, KT, 256 * (at % 2), 256, xT, l=l)
                        else:
                            colsT(i, w, KT, 256 * (at % 2), xT, l=l)
                    elif n == "ckv":
                        unit3(5)
                        rows(i, W3(5, KT, 160), KT, 0, P, xT, l=l)
                    elif n == "kr":
                        rows(i, W3(5, KT, 160), KT, P, 32, xT, l=l)
                    elif n in ("cqT", "ckvT"):
                        pe.wait_ge(lat_n, l + 1)
                        bank_free(pe, i, l)
                        for m in range(2 if n == "cqT" else 1):
                            for t in range(TT):
                                src = (cqn if n == "cqT" else ckvn)[:, t, m * P:m * P + P]
                                o = nc.tensor.transpose(G(i)[:, m * T + t * P:m * T + t * P + P], src, ident)
                        ready(o, l)
                    elif n[:2] == "uq":
                        t = int(n[-1])
                        taken(pe, LAT["cqT"], l=l)
                        bank_free(pe, i, l)
                        w = W3(5, 2, 384, KT * 160)
                        for k in range(2):
                            o = mm(G(i)[:, 0:384], cqT[:, k, t * P:t * P + P], w[:, k, :], k == 0, k == 1)
                        ready(o, l)
                    elif n[:3] == "ukv":
                        t = int(n[-1])
                        taken(pe, LAT["ckvT"], l=l)
                        bank_free(pe, i, l)
                        ready(mm(G(i), ckvT[:, 0, t * P:t * P + P], W3(5, 1, 512, KT * 160 + 768)[:, 0, :]), l)
                    else:
                        pe.wait_ge(rope_q if n[0] == "q" else rope_k, l + 1)
                        bank_free(pe, i, l)
                        for m in range(2):
                            for t in range(TT):
                                src = (qdn if n[0] == "q" else kcat)[:, t, 2 * int(n[-1]) + m, :]
                                o = nc.tensor.transpose(G(i)[0:96, m * T + t * P:m * T + t * P + P], src, ident)
                        ready(o, l)
                turn(NJ3 - 1, job3(NJ3 - 1, l), k_exp, k_p, k_t, l * NJ3)
                for j in (NJ3 - 2, NJ3 - 1):
                    values(j, job3(j, l), k_p, k_done, k_o, l * NJ3)
                pe.wait_ge(mix_done, l + 1)
                turn_x(LAT["mix0"], mix, l)
                taken(pe, *[LAT[f"mix{h}"] for h in range(4)], l=l)
                for h in range(4):
                    n = L3AT[f"wo{h // 2}"]
                    unit3(n)
                    rows(LAT[f"wo3_{h}"], W3(n, KT, 512), KT, 256 * (h % 2), 256, mixT, l=l)
                pe.wait_ge(n3_xn, l * 2 + 2)
                turn_x(LAT["n5_0"], mix, l)
                taken(pe, *[LAT[f"n5_{h}"] for h in range(4)], l=l)
                for i in range(11):
                    n = L3AT[f"gu{i}"]
                    unit3(n)
                    w = W3(n, KT, 512)
                    colsT(LAT[f"gu{2 * i}"], w, KT, 0, xT, l=l)
                    colsT(LAT[f"gu{2 * i + 1}"], w, KT, 256, xT, l=l)
                taken(pe, *[LAT[f"gu{i}"] for i in range(18, 22)], l=l)
                for q in range(4):
                    bank_free(pe, LAT[f"down{q}"], l)
                for u in range(6):
                    n = L3AT[f"dn{u}"]
                    unit3(n)
                    kt = min(4, FT - 4 * u)
                    w = W3(n, kt, D)
                    for k in range(kt):
                        kk = 4 * u + k
                        for q in range(4):
                            t, hf = q // 2, q % 2
                            o = mm(psum[:, q, :], actT[:, kk, t * P:t * P + P], w[:, k, 512 * hf:512 * hf + 512],
                                   kk == 0, kk == FT - 1)
                            if kk == FT - 1:
                                ready(o, l)
                    if u < 5:
                        o.then_inc(w3_dn, 1)

        @block.vector
        def _(dve):
            v = nc.vector

            def modulated(first, A, B, l=None):
                for h in range(4):
                    i = first + h
                    piece(dve, i, l)
                    for m in range(2):
                        k = 2 * h + m
                        if B is None:
                            o = v.tensor_scalar(xT[:, k, :], G(i)[:, m * T:m * T + T], A[:, k:k + 1], None, ALU.mult)
                        else:
                            o = v.tensor_scalar(xT[:, k, :], G(i)[:, m * T:m * T + T], A[:, k:k + 1], B[:, k:k + 1],
                                                ALU.mult, ALU.add)
                    o.then_inc((g_free if l is None else g3_free)[i % 4], 1)

            def normed(k, xn):
                dve.wait_ge(n_rstd, k + 1)
                for t in range(TT):
                    o = v.tensor_scalar(xn[:, t, :], x[:, t, :], rstd[:, t:t + 1], None, ALU.mult)
                o.then_inc(n_xn, 1)

            def pair(ap):
                return ap.rearrange("p (k t) -> p k t", k=2)

            dve.wait_ge(v_used, 1)
            v.tensor_copy(vec1, psum[:, 5, 0:112])
            v.tensor_copy(vec2, psum[:, 5, 128:206]).then_inc(v_cols, 1)
            dve.wait_ge(v_used, 2)
            v.scalar_tensor_tensor(t5vec[0:8, :], psum[0:8, 7, :], -1.0, K("diladd")[0:8, :], ALU.mult,
                                   ALU.add).then_inc(rel_src, 1)
            dve.wait_ge(in_lam, 32)
            lr = lamraw.rearrange("p l (a b n) -> p l a b n", a=2, b=2)
            for l in range(LAYERS):
                v.tensor_tensor(lamprod[:, l, :, :], lr[:, l, :, 0, :], lr[:, l, :, 1, :], ALU.mult)
                v.tensor_scalar(subg[:, l, :], subg[:, l, :], 1.0 - LAM_INIT[l], None, ALU.mult)
            v.drain()
            v.tensor_reduce(lamsum, lamprod.rearrange("p l c n -> p (l c) n"), AX_X, ALU.add).then_inc(lam_s, 1)
            normed(0, xn1)
            dve.wait_ge(in_b1, 16 * 4)
            dve.wait_ge(lam_e, 1)
            for l in range(LAYERS):
                v.tensor_tensor(lamneg[:, l:l + 1], lamexp[:, 2 * l + 1:2 * l + 2], lamexp[:, 2 * l:2 * l + 1], ALU.subtract)
            v.drain()
            for l in range(LAYERS):
                v.tensor_scalar(lamneg[:, l:l + 1], lamneg[:, l:l + 1], -LAM_INIT[l], None, ALU.add)
            for r, u in enumerate(GATE_UNITS):
                if u == 10:
                    dve.wait_ge(mod_mm, 10)
                    v.tensor_tensor(mod[:, 0:16], psum[:, 4, 0:16], vec1[:, 0:16], ALU.add)
                    v.tensor_tensor(mod[:, 24:40], psum[:, 4, 24:40], vec1[:, 24:40], ALU.add)
                    v.drain()
                    v.scalar_tensor_tensor(Am, mod[:, 8:16], 1.0, vec1[:, 48:56], ALU.add, ALU.mult)
                    v.scalar_tensor_tensor(Af, mod[:, 32:40], 1.0, vec1[:, 56:64], ALU.add, ALU.mult)
                dve.wait_ge(mod_mm, u + 1)
                g = (gate_m, gate_f)[r // 2][:, 512 * (r % 2):512 * (r % 2) + 512]
                v.tensor_tensor(g, psum[:, 6 + r % 2, :], g, ALU.add).then_inc(mod_done, 1)
            v.drain()
            modulated(AT["n1_0"], Am, mod[:, 0:8])
            for h in range(4):
                i = AT[f"c{h}"]
                piece(dve, i)
                if h == 0:
                    taken(dve, *[AT[f"v{j}"] for j in range(4)])
                    taken(dve, *[AT[f"b{j}"] for j in range(4)])
                    dve.wait_ge(consts_set, 3)
                v.tensor_tensor(cv[:, 2 * h:2 * h + 2, 1:T + 1], pair(G(i)), vT[:, 2 * h:2 * h + 2, :],
                                ALU.mult).then_inc(g_free[i % 4], 1)
                v.drain()
                w = [vec1[:, 72 + 8 * j + 2 * h:74 + 8 * j + 2 * h] for j in range(3)]
                for m in range(2):
                    v.tensor_scalar(mtmp[:, m * T:m * T + T], cv[:, 2 * h + m, 0:T], w[0][:, m:m + 1], None, ALU.mult)
                for j in (1, 2):
                    v.drain()
                    for m in range(2):
                        v.scalar_tensor_tensor(mtmp[:, m * T:m * T + T], cv[:, 2 * h + m, j:T + j], w[j][:, m:m + 1],
                                               mtmp[:, m * T:m * T + T], ALU.mult, ALU.add)
                v.drain()
                for m in range(2):
                    k = 2 * h + m
                    v.tensor_tensor(bT[:, k, :], bT[:, k, :], mtmp[:, m * T:m * T + T], ALU.mult).then_inc(conv_done, 1)
            for nm, gate in (("wf", gaT), ("wc", gbT)):
                for h in range(4):
                    i = AT[f"{nm}{h}"]
                    piece(dve, i)
                    if h == 0:
                        for j in range(4):
                            taken(dve, AT[("ga" if nm == "wf" else "gb") + str(j)])
                    g = gate[:, 2 * h:2 * h + 2, :]
                    v.tensor_tensor(g, pair(G(i)), g, ALU.mult).then_inc(g_free[i % 4], 1)
                    if nm == "wc":
                        v.drain()
                        z = gaT[:, 2 * h:2 * h + 2, :]
                        v.tensor_tensor(z, z, g, ALU.add).then_inc(z_done, 1)
            for h in range(4):
                i = AT[f"wo{h}"]
                piece(dve, i)
                c = slice(256 * h, 256 * h + 256)
                mt = mtmp[:, 512 * (h % 2):512 * (h % 2) + 512].rearrange("p (t n) -> p t n", t=TT)
                v.tensor_tensor(mt, G(i).rearrange("p (t n) -> p t n", t=TT),
                                gate_m[:, c].unsqueeze(1).broadcast_to([P, TT, 256]), ALU.mult).then_inc(g_free[i % 4], 1)
                v.drain()
                v.tensor_tensor(x[:, :, c], x[:, :, c], mt, ALU.add).then_inc(x1_done, 1)

            normed(1, xn2)
            modulated(AT["n2_0"], Af, mod[:, 24:32])
            i = AT["rt"]
            piece(dve, i)
            dve.wait_ge(in_moe, 16 * 2)
            dve.wait_ge(in_route, 16 * 2)
            v.tensor_tensor(lg, G(i)[:, 0:TT * NE].rearrange("p (t e) -> p t e", t=TT),
                            brow.unsqueeze(1).broadcast_to([P, TT, NE]), ALU.add).then_inc(g_free[i % 4], 1)
            v.drain()
            v.tensor_reduce(negmax, lg, AX_X, ALU.max, negate=True).then_inc(r_lg, 1)
            dve.wait_ge(r_exp, TT)
            v.reciprocal(rrec, rsum)
            v.drain()
            for t in range(TT):
                o = v.tensor_scalar(prob[:, t, :], ex[:, t, :], rrec[:, t:t + 1], None, ALU.mult)
            o.then_inc(r_prob, 1)
            i = AT["pt"]
            piece(dve, i)
            v.tensor_copy(work[0:NE, :], G(i)[0:NE, 0:T]).then_inc(g_free[i % 4], 1)
            for _ in range(CAP // 8):
                v.drain()
                v.max(top8[0:NE, :], work[0:NE, :])
                v.drain()
                v.match_replace(work[0:NE, :], top8[0:NE, :], work[0:NE, :], -1.0)
            v.drain()
            v.tensor_scalar(mk[0:NE, :], work[0:NE, :], 0.0, None, ALU.is_lt).then_inc(r_sel, 1)
            i = AT["mk"]
            piece(dve, i)
            v.tensor_copy(maskn, G(i)[:, 0:TT * NE].rearrange("p (t e) -> p t e", t=TT)).then_inc(g_free[i % 4], 1)
            v.drain()
            i = AT["pos"]
            piece(dve, i)
            v.scalar_tensor_tensor(posm, maskn, -1000.0, G(i)[:, 0:TT * NE].rearrange("p (t e) -> p t e", t=TT),
                                   ALU.mult, ALU.add).then_inc(g_free[i % 4], 1)
            v.drain()
            v.tensor_scalar(posm, posm, 1000.0, None, ALU.add)
            v.drain()
            for t in range(TT):
                s3 = sel[:, t, :].rearrange("p (e c) -> p e c", e=NE)
                v.tensor_tensor(s3, slot_id, posm[:, t, :].unsqueeze(2).broadcast_to([P, NE, CAP]), ALU.is_equal)
            v.drain()
            for t in range(TT):
                s3 = sel[:, t, :].rearrange("p (e c) -> p e c", e=NE)
                w3 = selw[:, t, :].rearrange("p (e c) -> p e c", e=NE)
                o = v.tensor_tensor(w3, s3, prob[:, t, :].unsqueeze(2).broadcast_to([P, NE, CAP]), ALU.mult)
            o.then_inc(r_sel, 1)
            v.drain()
            dve.wait_ge(e_acc, 1)
            with dve.Fori(0, NE) as e:
                for t in range(TT):
                    o = v.tensor_copy(rep[:, t, :, :],
                                      selw[:, t, bass.ds(e * CAP, CAP)].unsqueeze(1).broadcast_to([P, 4, CAP]))
                o.then_inc(e_rep, 1)
                dve.wait_ge(e_gath, e + 1)
                v.tensor_copy(xeT.rearrange("p k c -> p (k c)"), psum[:, 3, 0:KT * CAP]).then_inc(e_xe, 1)
                dve.wait_ge(e_selTp, e + 1)
                v.tensor_copy(selT, psum[:, 2, 0:T]).then_inc(e_selT, 1)
                dve.wait_ge(e_sil, e + 1)
                dve.wait_ge(e_unit, e * UPE + 8)
                v.tensor_tensor(gu, sil, psum[:, 1, :], ALU.mult).then_inc(e_gu, 1)
                dve.wait_ge(e_sc, e + 1)
                for t in range(TT):
                    a3 = acc[:, t, :].rearrange("p (j n) -> p j n", j=4)
                    o = v.tensor_tensor(a3, psum[:, 4:8, t * T:t * T + T], a3, ALU.add)
                o.then_inc(e_acc, 1)
                v.drain()
            v.tensor_tensor(acc, acc, gate_f.unsqueeze(1).broadcast_to([P, TT, D]), ALU.mult)
            v.drain()
            v.tensor_tensor(x, x, acc, ALU.add).then_inc(x2_done, 1)
            dve.wait_ge(n_rstd, 3)
            for t in range(TT):
                o = v.scalar_tensor_tensor(x[:, t, :], x[:, t, :], rstd[:, t:t + 1], gbc, ALU.mult, ALU.mult)
            o.then_inc(x3_done, 1)

            normed(3, xn3)
            v.drain()
            modulated(AT["n3_0"], vec2[:, 0:8], None)

            def doubled(name, d):
                i = AT[name]
                piece(dve, i)
                for g in range(2):
                    for hf in range(2):
                        o = v.tensor_copy(d[HD * hf:HD * hf + HD, g, :], G(i)[HD * g:HD * g + HD, 0:T])
                o.then_inc(g_free[i % 4], 1)

            i = AT["kc"]
            piece(dve, i)
            for c in range(2):
                for g in range(2):
                    v.tensor_copy(k2[0:HD, c, g, :], G(i)[HD * g:HD * g + HD, c * T:c * T + T])
                    o = v.tensor_copy(k2[HD:P, c, g, 0:T - 1], G(i)[HD * g:HD * g + HD, c * T + 1:c * T + T])
            o.then_inc(g_free[i % 4], 1)
            v.drain()
            for c in range(2):
                for g in range(2):
                    for u in range(2):
                        src = k2[:, c, g, 16 * u:16 * u + 16 * NCMP].rearrange("p (n r o) -> p r n o", r=8, o=2)[:, :, :, 0]
                        d = kb2[:, c, 8 * u:8 * u + 8, g * NCMP:g * NCMP + NCMP]
                        pe_ = vec2[:, 46 + 16 * c + 8 * u:54 + 16 * c + 8 * u].unsqueeze(2).broadcast_to([P, 8, NCMP])
                        o = v.tensor_tensor(d, src, pe_, ALU.add)
            o.then_inc(kb_done, 1)
            doubled("ks", ksT)
            doubled("kw", kwT)
            taken(dve, AT["gnsa"])
            for t in range(TT):
                o = v.tensor_scalar(gn[:, t, 0:8], gn[:, t, 0:8], K("cmpvalid")[:, t:t + 1], None, ALU.mult)
            v.drain()

            def least(j, J, s_, x_, m_, base=0):
                b = j % 2
                nk = sum(J["widths"])
                dve.wait_ge(s_, base + (j + 1))
                if j >= 2:
                    dve.wait_ge(x_, base + (j - 1))
                if "dist" in J:
                    v.scalar_tensor_tensor(sbuf[:, b, 0:nk], J["dist"], J["slope"], psum[:, 4 + b, 0:nk],
                                           ALU.mult, ALU.add)
                    v.drain()
                    v.tensor_reduce(jmin[:, b:b + 1], sbuf[:, b, 0:nk], AX_X, ALU.min).then_inc(m_, 1)
                elif J["bias"] is None:
                    v.tensor_copy(sbuf[:, b, 0:nk], psum[:, 4 + b, 0:nk])
                    v.tensor_reduce(jmin[:, b:b + 1], psum[:, 4 + b, 0:nk], AX_X, ALU.min).then_inc(m_, 1)
                else:
                    v.memset(spare[:, j:j + 1], 0.0)
                    v.tensor_tensor_reduce(sbuf[:, b, 0:nk], psum[:, 4 + b, 0:nk], J["bias"], 1.0, 3e38,
                                           ALU.add, ALU.min, jmin[:, b:b + 1]).then_inc(m_, 1)

            def finish(j, J, x_, o_, d_, base=0):
                b = j % 2
                dve.wait_ge(x_, base + (j + 1))
                v.reciprocal(jrec[:, b:b + 1], jsum[:, b:b + 1])
                v.drain()
                if J["coef"] is not None:
                    v.tensor_tensor(jrec[:, b:b + 1], jrec[:, b:b + 1], J["coef"], ALU.mult)
                    v.drain()
                dve.wait_ge(o_, base + (j + 1))
                if J["first"]:
                    v.tensor_scalar(J["out"], psum[:, 7, 0:HD], jrec[:, b:b + 1], None, ALU.mult).then_inc(d_, 1)
                else:
                    v.scalar_tensor_tensor(J["out"], psum[:, 7, 0:HD], jrec[:, b:b + 1], J["out"],
                                           ALU.mult, ALU.add).then_inc(d_, 1)

            for kind, n in PLAN2:
                if kind == "job":
                    least(n, job2(n), j_s, j_exp, j_min)
                    if n >= 2:
                        finish(n - 2, job2(n - 2), j_exp, j_o, j_done)
            for j in (NJ2 - 2, NJ2 - 1):
                finish(j, job2(j), j_exp, j_o, j_done)
            v.drain()
            taken(dve, *[AT[m] for m in ("za0", "za1", "zb0", "zb1")])
            v.tensor_tensor(oA, oA, zA, ALU.mult)
            v.tensor_tensor(oB, oB, zB, ALU.mult).then_inc(y_done, 1)
            for q in range(2):
                for nm, gate in (("wa", mAT), ("wb", mBT)):
                    for h in (2 * q, 2 * q + 1):
                        i = AT[f"{nm}{h}"]
                        piece(dve, i)
                        taken(dve, AT[("mA" if nm == "wa" else "mB") + str(h)])
                        g = gate[:, 2 * h:2 * h + 2, :]
                        v.tensor_tensor(g, pair(G(i)), g, ALU.mult).then_inc(g_free[i % 4], 1)
                        if nm == "wb":
                            v.drain()
                            m = mAT[:, 2 * h:2 * h + 2, :]
                            v.tensor_tensor(m, m, g, ALU.add).then_inc(m_done, 1)
            dve.wait_ge(in_post, 16)
            dve.wait_ge(n_rstd, 5)
            for t in range(TT):
                v.scalar_tensor_tensor(mixn[:, t, :], mixn[:, t, :], rstd[:, t:t + 1], gbc, ALU.mult, ALU.mult)
            v.drain()
            v.tensor_tensor(x, x, mixn, ALU.add).then_inc(x4_done, 1)

            cos = K("cos").rearrange("p (t n) -> p t n", t=TT)
            sin = K("sin").rearrange("p (t n) -> p t n", t=TT)
            dve.wait_ge(in_t5, 16 * 16)
            with dve.Fori(0, LAYERS) as l:
                v.drain()
                v.tensor_copy(Am, vec2[:, bass.ds(l * KT + 8, KT)])
                v.tensor_copy(Af, vec2[:, bass.ds(l * KT + 24, KT)])
                v.tensor_copy(Bm[:, 0:2], vec2[:, bass.ds(l * 2 + 40, 2)])
                v.tensor_copy(Bm[:, 2:3], vec2[:, bass.ds(l + 44, 1)])
                v.tensor_copy(subl, subg.rearrange("p l n -> p (l n)")[:, bass.ds(l * HD, HD)])

                def normed3(need):
                    dve.wait_ge(n3_rstd, need)
                    for t in range(TT):
                        o = v.tensor_scalar(mix[:, t, :], x[:, t, :], rstd[:, t:t + 1], None, ALU.mult)
                    o.then_inc(n3_xn, 1)

                normed3(l * 2 + 1)
                dve.wait_ge(in_na, l * (16 * 16) + 16 * 16)
                for h in range(4):
                    for t in range(TT):
                        o = v.scalar_tensor_tensor(nab[:, h, t, :], nab[:, h, t, :], -1.0, K("nawin"), ALU.mult, ALU.add)
                o.then_inc(nab_done, 1)
                modulated(LAT["n4_0"], Am, None, l)
                for kind, n in PLAN3:
                    if kind == "job":
                        least(n, job3(n, l), k_s, k_exp, k_min, l * NJ3)
                        if n >= 2:
                            finish(n - 2, job3(n - 2, l), k_exp, k_o, k_done, l * NJ3)
                        continue
                    if n == "kr":
                        dve.wait_ge(h_rstd, l + 1)
                        taken(dve, LAT["cq"], LAT["ckv"], l=l)
                        for t in range(TT):
                            v.tensor_scalar(cqn[:, t, :], cqn[:, t, :], hrstd[:, t:t + 1], None, ALU.mult)
                            o = v.tensor_scalar(ckvn[:, t, :], ckvn[:, t, :], hrstd[:, 2 + t:3 + t], None, ALU.mult)
                        o.then_inc(lat_n, 1)
                    elif n in ("cqT", "ckvT"):
                        i = LAT[n]
                        piece(dve, i, l)
                        if n == "cqT":
                            for m in range(2):
                                o = v.tensor_scalar(cqT[:, m, :], G(i)[:, m * T:m * T + T], Bm[:, m:m + 1], None, ALU.mult)
                        else:
                            o = v.tensor_scalar(ckvT[:, 0, :], G(i)[:, 0:T], Bm[:, 2:3], None, ALU.mult)
                        o.then_inc(g3_free[i % 4], 1)
                    elif n == "uq1":
                        taken(dve, LAT["uq0"], LAT["uq1"], l=l)
                        x1, x2 = qdn[:, :, :, 64:80], qdn[:, :, :, 80:96]
                        cb = cos.unsqueeze(2).broadcast_to([P, TT, 4, 16])
                        sb_ = sin.unsqueeze(2).broadcast_to([P, TT, 4, 16])
                        for c, (u, f) in enumerate(((x1, cb), (x2, sb_), (x1, sb_), (x2, cb))):
                            v.tensor_tensor(rp[:, c, :, :, :], u, f, ALU.mult)
                        v.drain()
                        v.tensor_tensor(x1, rp[:, 0, :, :, :], rp[:, 1, :, :, :], ALU.subtract)
                        v.tensor_tensor(x2, rp[:, 2, :, :, :], rp[:, 3, :, :, :], ALU.add).then_inc(rope_q, 1)
                    elif n == "ukv1":
                        taken(dve, LAT["kr"], LAT["ukv0"], LAT["ukv1"], l=l)
                        x1, x2 = krn[:, :, 0:16], krn[:, :, 16:32]
                        for c, (u, f) in enumerate(((x1, cos), (x2, sin), (x1, sin), (x2, cos))):
                            v.tensor_tensor(rk[:, c, :, :], u, f, ALU.mult)
                        v.drain()
                        wide = [rk[:, c, :, :].unsqueeze(2).broadcast_to([P, TT, 4, 16]) for c in range(4)]
                        v.tensor_tensor(kcat[:, :, :, 64:80], wide[0], wide[1], ALU.subtract)
                        v.tensor_tensor(kcat[:, :, :, 80:96], wide[2], wide[3], ALU.add).then_inc(rope_k, 1)
                for j in (NJ3 - 2, NJ3 - 1):
                    finish(j, job3(j, l), k_exp, k_o, k_done, l * NJ3)
                v.drain()
                mb = mix[:, :, 256:512].rearrange("p t (h n) -> p t h n", h=4)
                v.tensor_tensor(hsq, mb, mb, ALU.mult)
                v.drain()
                v.tensor_reduce(hstat[:, 0:8], hsq.rearrange("p t h n -> p (t h) n"), AX_X, ALU.add).then_inc(d_sq, 1)
                dve.wait_ge(d_rstd, l + 1)
                hr = hrstd.rearrange("p (t h) -> p t h", t=TT).unsqueeze(3).broadcast_to([P, TT, 4, HD])
                v.tensor_tensor(mb, mb, hr, ALU.mult)
                v.drain()
                for t in range(TT):
                    o = v.tensor_tensor(mb[:, t, :, :], mb[:, t, :, :], subl.unsqueeze(1).broadcast_to([P, 4, HD]), ALU.mult)
                o.then_inc(mix_done, 1)
                for h in range(4):
                    i = LAT[f"wo3_{h}"]
                    piece(dve, i, l)
                    c = slice(256 * h, 256 * h + 256)
                    v.tensor_tensor(x[:, :, c], G(i).rearrange("p (t n) -> p t n", t=TT), x[:, :, c],
                                    ALU.add).then_inc(g3_free[i % 4], 1)
                    v.drain().then_inc(xm_done, 1)
                normed3(l * 2 + 2)
                modulated(LAT["n5_0"], Af, None, l)
                for i in range(11):
                    n = LAT[f"gu{2 * i + 1}"]
                    piece(dve, n, l)
                    taken(dve, LAT[f"gu{2 * i}"], l=l)
                    g = actT[:, 2 * i:2 * i + 2, :]
                    v.tensor_tensor(g, pair(G(n)), g, ALU.mult).then_inc(g3_free[n % 4], 1)
                for q in range(4):
                    i = LAT[f"down{q}"]
                    piece(dve, i, l)
                    xs = x[:, q // 2, 512 * (q % 2):512 * (q % 2) + 512]
                    v.tensor_tensor(xs, G(i), xs, ALU.add).then_inc(g3_free[i % 4], 1)
                v.drain().then_inc(x4_done, 1)
            dve.wait_ge(in_fin, 16)
            dve.wait_ge(n3_rstd, LAYERS * 2 + 1)
            for t in range(TT):
                v.scalar_tensor_tensor(x[:, t, :], x[:, t, :], rstd[:, t:t + 1], gbc, ALU.mult, ALU.mult).then_inc(y_out, 1)

    return nc


INPUTS = ["x", "c", "w_ada", "b_ada", "g_norm_mix", "w_in", "b_gate", "w_fourier", "w_conv", "w_conv_out", "w_o",
          "g_norm_moe", "w_router", "b_router", "w_gate_e", "w_up_e", "w_down_e", "g_final", "norm_pre_2", "w_in_2",
          "cmp_pe_k_2", "cmp_w1_k_2", "cmp_w2_k_2", "cmp_pe_v_2", "cmp_w1_v_2", "cmp_w2_v_2", "w_branch_a_2",
          "w_branch_b_2", "w_o_2", "norm_post_2", "attn_norm_3", "w_in_3", "na_rpb_3", "diff_lambda_3",
          "diff_subln_3", "mla_q_norm_3", "w_uq_3", "mla_kv_norm_3", "w_ukv_3", "t5_table_3", "w_o_3", "ffn_norm_3",
          "w_gate_3", "w_up_3", "w_down_3", "final_norm_3"]


def kernel(**inputs):
    import concourse.bacc as bacc
    from concourse.bass_utils import run_bass_kernel_spmd

    nc = bacc.Bacc("TRN2", target_bir_lowering=False, num_devices=1)
    kept, cst_at, dft, moe = build_constants()
    arrays = {n: np.ascontiguousarray(inputs[n]) for n in INPUTS}
    arrays.update(c_kept=kept, c_dft=dft, c_moe=moe)
    handles = {n: nc.dram_tensor("in_" + n, v.shape, mybir.dt.from_np(v.dtype), kind="ExternalInput").ap()
               for n, v in arrays.items()}
    out = nc.dram_tensor("out", (1, T, D), F32, kind="ExternalOutput").ap()
    program(nc, handles, cst_at, out)
    r = run_bass_kernel_spmd(nc, [{"in_" + n: v for n, v in arrays.items()}], core_ids=[0])
    return r.results[0]["out"]
```

```python
import math
from contextlib import ExitStack

import numpy as np

import concourse.bass as bass
from concourse import mybir

ALU = mybir.AluOpType
ACT = mybir.ActivationFunctionType
AX_X = mybir.AxisListType.X
F32 = mybir.dt.float32
F32R = mybir.dt.float32r

P = 128
T = 256
TT = T // P
D = 1024
KT = D // P
EPS = 1e-6
NE = 16
CAP = 2 * T // NE
FE = 2048
SLOT = 4096
RING = 5
RINGM = 6
BIG = 1e30
NHEAD = 16
HD = 64
NCMP = (T - 32) // 16 + 1
DFF = ((8 * D + 3 * 256 - 1) // (3 * 256)) * 256
FT = DFF // P
LAYERS = 2
ARENA = 19728
GATE_UNITS = (4, 5, 10, 11)
NDIL = ((128, 1), (512, 4), (2048, 16))
GRID_W, NA_ROWS, NA_COLS = 64, 8, 16
NA_SPAN = T // GRID_W
REL = 2 * T
NAREL = 2 * GRID_W


def t5_bucket(rel):
    nb, exact = 16, 8
    side = np.where(rel > 0, nb, 0)
    n = np.abs(rel)
    q = np.maximum(n, 1).astype(np.float32) / np.float32(exact)
    large = exact + (np.log(q) / np.float32(math.log(1024 / exact)) * np.float32(nb - exact)).astype(np.int32)
    return side + np.where(n < exact, n, np.minimum(large, nb - 1))


def build_constants():
    c = {}
    tok = np.arange(T)
    c["ident"] = np.eye(P)
    c["ones"] = np.ones((P, P))
    q, k = tok[:, None], tok[None, :]
    causal = np.where(q >= k, (q - k).astype(np.float64), BIG)
    c["dist"] = np.concatenate([causal[:P, :P], causal[P:, :]], axis=1)
    end = np.arange(16) * 16 + 31
    dc = np.where((q >= end[None, :]) & (np.arange(16)[None, :] < NCMP), (q - end[None, :]).astype(np.float64), BIG)
    c["cmpdist"] = dc.reshape(TT, P, 16).transpose(1, 0, 2).reshape(P, 32)
    c["cmpvalid"] = (tok >= 31).astype(np.float64).reshape(TT, P).T
    col = np.arange(GRID_W)
    start = np.clip(col - NA_COLS // 2, 0, GRID_W - NA_COLS)
    out = ~((col[None, :] >= start[:, None]) & (col[None, :] < start[:, None] + NA_COLS))
    c["nawin"] = np.tile(np.where(out, BIG, 0.0), (2, NA_SPAN))
    half = 16
    freq = np.float32(10000.0) ** (-np.arange(half, dtype=np.float32) / np.float32(half))
    ang = (tok.astype(np.float32)[:, None] * freq[None, :]).astype(np.float32)
    for n, f in (("cos", np.cos), ("sin", np.sin)):
        c[n] = f(ang.astype(np.float64)).reshape(TT, P, half).transpose(1, 0, 2).reshape(P, TT * half)
    rel = np.arange(REL) - (T - 1)
    hot = np.zeros((P, REL))
    hot[t5_bucket(rel), np.arange(REL)] = 1.0
    mult = sum(((np.abs(rel) <= w // 2) & (rel % d == 0)).astype(np.int64) for w, d in NDIL)
    add = np.zeros((P, REL))
    add[4:8] = np.where(mult > 0, -np.log(np.maximum(mult, 1)), BIG)
    names = list(c)
    kept = np.concatenate([c[n] for n in names], axis=1).astype(np.float32)
    at, pos = {}, 0
    for n in names:
        at[n] = (pos, c[n].shape[1])
        pos += c[n].shape[1]
    a = 2 * np.pi * (np.outer(tok, tok) % T) / T
    s = 1.0 / math.sqrt(T * P)
    dft_s = np.concatenate([np.cos(a) * s, np.sin(a) * s], axis=1).reshape(TT, P, 2 * T).transpose(1, 0, 2)
    b = 2 * np.pi * (np.outer(np.arange(P), np.arange(P)) % P) / P
    dft = np.concatenate([dft_s.reshape(P, TT * 2 * T), np.cos(b), -np.sin(b)], axis=1).astype(np.float32)
    tri = (tok[:, None] < tok[None, :]).astype(np.float32).reshape(TT, P, T).transpose(1, 0, 2).reshape(P, TT * T)
    slots = np.tile(np.arange(CAP), (P, NE)).astype(np.float32)
    return kept, at, dft, np.concatenate([tri, slots], axis=1).astype(np.float32), \
        np.concatenate([hot, add], axis=1).astype(np.float32)


def slope(i):
    return float(np.float32(2.0 ** (-8.0 * (i + 1) / NHEAD)))


def names(prefix, n):
    return [f"{prefix}{i}" for i in range(n)]


PIECES = (names("ada", 12) + names("n1_", 4) + names("uf", 2) + names("dfta", 4) + names("dftb", 2)
          + names("v", 4) + names("b", 4) + names("c", 4) + names("ga", 4) + names("gb", 4)
          + names("wf", 4) + names("wc", 4) + names("wo", 4) + names("n2_", 4) + names("h2n", 4)
          + ["rt", "pt", "mk", "pos"]
          + names("n3_", 4) + names("qa", 2) + ["kc", "ks", "vs", "kw", "vw", "gnsa", "hk", "kcT", "vcn"]
          + names("za", 2) + names("qb", 2) + names("kb", 2) + names("vb", 2) + names("zb", 2)
          + names("mA", 4) + names("mB", 4) + names("yt", 4)
          + ["wa0", "wa1", "wb0", "wb1", "wa2", "wa3", "wb2", "wb3"] + names("wo2_", 4))
AT = {n: i for i, n in enumerate(PIECES)}
LP = (names("n4_", 4) + ["qa0", "ka0", "va0", "qb0", "kb0", "vb0", "qc0", "kc0", "vc0", "cq", "ckv", "kr", "cqT", "ckvT"]
      + names("uq", 2) + names("ukv", 2) + names("qm", 2) + names("km", 2) + names("mix", 4) + names("wo3_", 4)
      + names("n5_", 4) + names("gu", 22) + names("down", 4))
assert len(AT) == len(PIECES) 
LAT = {n: i for i, n in enumerate(LP)}
LPN = len(LP)
assert LPN % 4 == 0

UNITS = (names("ada", 12) + names("win", 11) + names("wf", 2) + names("wc", 2) + names("wo", 2))
N_MOE = len(UNITS)
UPE = 12
UNITS2 = ["qa", "kv", "kvwg", "w1", "za", "qb", "kb", "vb", "zb"] + names("mg", 4) + names("ab", 2) + names("wo2_", 2)
UAT = {n: i for i, n in enumerate(UNITS)}
U2AT = {n: i for i, n in enumerate(UNITS2)}
L3 = names("win", 6) + names("wo", 2) + names("gu", 11) + names("dn", 6)
L3AT = {n: i for i, n in enumerate(L3)}
assert len(L3) % RING == 0

JOBS3 = ([("na", h, 0, t) for h in range(4) for t in range(TT)]
         + [("diff", h, c, t) for h in range(4) for t in range(TT) for c in range(2)]
         + [("dil", h, 0, t) for h in range(4) for t in range(TT)]
         + [("mla", h, 0, t) for h in range(4) for t in range(TT)])
NJ3 = len(JOBS3)
_first = ["qa0", "ka0", "va0", "qb0", "kb0", "vb0"]
_rest = ["qc0", "kc0", "vc0", "cq", "ckv", "kr", "cqT", "ckvT", "uq0", "uq1", "ukv0", "ukv1", "qm0", "qm1", "km0", "km1"]
PLAN3 = [("piece", n) for n in _first]
for _i, _n in enumerate(_rest):
    PLAN3.append(("piece", _n))
    PLAN3 += [("job", j) for j in range(2 * _i, 2 * _i + 2)]
PLAN3 += [("job", j) for j in range(2 * len(_rest), NJ3)]
PARTS3 = {L3AT["win5"]: 3}
PARTS3.update({L3AT[f"gu{i}"]: 2 for i in range(11)})
LAST3 = {L3AT[u]: LAT[p] for u, p in (("win0", "ka0"), ("win1", "qb0"), ("win2", "vb0"), ("win3", "kc0"),
                                      ("win4", "cq"), ("win5", "ukv1"), ("wo0", "wo3_1"), ("wo1", "wo3_3"),
                                      ("dn5", "down3"))}
LAST3.update({L3AT[f"gu{i}"]: LAT[f"gu{2 * i + 1}"] for i in range(11)})
LAM_INIT = [0.8 - 0.6 * math.exp(-0.3 * l) for l in range(LAYERS)]
LAST = {UAT[f"ada{i}"]: AT[f"ada{i}"] for i in range(12)}
LAST[UAT["win0"]] = AT["uf1"]
for _i in range(10):
    LAST[UAT[f"win{_i + 1}"]] = AT[("v", "b", "c", "ga", "gb")[_i // 2] + str(2 * (_i % 2) + 1)]
for _n in ("wf", "wc", "wo"):
    for _i in range(2):
        LAST[UAT[f"{_n}{_i}"]] = AT[f"{_n}{2 * _i + 1}"]
LAST2 = ({U2AT[u]: AT[p] for u, p in (("qa", "qa1"), ("kv", "vs"), ("kvwg", "vcn"), ("w1", "hk"), ("za", "za1"),
                                         ("qb", "qb1"), ("kb", "kb1"), ("vb", "vb1"), ("zb", "zb1"),
                                         ("mg0", "mA1"), ("mg1", "mA3"), ("mg2", "mB1"), ("mg3", "mB3"),
                                         ("ab0", "wb1"), ("ab1", "wb3"), ("wo2_0", "wo2_1"), ("wo2_1", "wo2_3"))})

CH1 = [(f"uf{h}", UAT["win0"], KT, 512, 256 * h, 256, 0, f"uf{h}") for h in range(2)]
for _b, _n in enumerate(("v", "b", "c", "ga", "gb")):
    CH1 += [(f"{_n}{h}", UAT["win1"] + 2 * _b + h // 2, KT, 512, 256 * (h % 2), 256, 0, f"{_n}{h}") for h in range(4)]
for _n, _k in (("wf", 4), ("wc", KT), ("wo", KT)):
    CH1 += [(f"{_n}{h}", UAT[f"{_n}{h // 2}"], _k, 512, 256 * (h % 2), 256, 0, f"{_n}{h}") for h in range(4)]
CH2 = [(f"qa{h}", U2AT["qa"], KT, 512, 256 * h, 256, 0, f"qa{h}") for h in range(2)]
CH2 += [("kc", U2AT["kv"], KT, 512, 0, 256, 0, "kc"), ("ksvs", U2AT["kv"], KT, 512, 256, 256, 0, "vs"),
        ("kwvw", U2AT["kvwg"], KT, 280, 0, 256, 0, "vw"), ("gnsa", U2AT["kvwg"], KT, 280, 256, 24, 0, "gnsa")]
CH2 += [(f"{n}{h}", U2AT[n], KT, 512, 256 * h, 256, 0, f"{n}{h}") for n in ("za", "qb", "kb", "vb", "zb") for h in range(2)]
CH2 += [(f"m{b}{h}", U2AT[f"mg{2 * (b == 'B') + h // 2}"], KT, 512, 256 * (h % 2), 256, 0, f"m{b}{h}")
        for b in "AB" for h in range(4)]
CH2 += [(f"w{b}{2 * q + m}", U2AT[f"ab{q}"], 4, 512, 256 * m, 256, 2048 * (b == "b"), f"w{b}{2 * q + m}")
        for q in range(2) for b in "ab" for m in range(2)]
CH2 += [(f"wo2_{h}", U2AT[f"wo2_{h // 2}"], KT, 512, 256 * (h % 2), 256, 0, f"wo2_{h}") for h in range(4)]
CH3 = [(n, i // 2, KT, 512, 256 * (i % 2), 256, 0, n)
       for i, n in enumerate(("qa0", "ka0", "va0", "qb0", "kb0", "vb0", "qc0", "kc0", "vc0", "cq"))]
CH3 += [("ckvkr", 5, KT, 160, 0, 160, 0, "kr")]
CH3 += [(f"wo3_{h}", L3AT[f"wo{h // 2}"], KT, 512, 256 * (h % 2), 256, 0, f"wo3_{h}") for h in range(4)]
CH3 += [(f"gu{i}", L3AT[f"gu{i // 2}"], KT, 512, 256 * (i % 2), 256, 0, f"gu{i}") for i in range(22)]
CH3 += [(f"dn{i}", L3AT[f"dn{i // 2}"], 2, D, 0, D, 2 * D * (i % 2), f"dn{i}") for i in range(11)]
assert len(CH3) % 2 == 0
C1AT, C2AT, C3AT = ({c[0]: i for i, c in enumerate(ch)} for ch in (CH1, CH2, CH3))

NSA_JOBS = [(br, h, t) for h in range(8) for t in range(TT) for br in ("cmp", "slc", "win")]
MOBA_JOBS = [("moba", h, t) for h in range(8) for t in range(TT)]
JOBS2 = NSA_JOBS + MOBA_JOBS
_tail = (names("za", 2) + names("qb", 2) + names("kb", 2) + names("vb", 2) + names("zb", 2) + names("mA", 4)
         + names("mB", 4))
PLAN2 = []
NJ2 = len(JOBS2)
for _i, _n in enumerate(_tail):
    PLAN2.append(("piece", _n))
    PLAN2 += [("job", j) for j in range(len(JOBS2) * _i // len(_tail), len(JOBS2) * (_i + 1) // len(_tail))]


def program(nc, a, cst_at, out):
    with ExitStack() as ctx:
        def sb(name, cols, parts=P):
            return ctx.enter_context(nc.sbuf_tensor(name, [parts, cols], F32))[:, :]

        def sem(name):
            return ctx.enter_context(nc.semaphore(name))

        def dram(name, shape):
            return nc.dram_tensor(name, shape, F32, kind="Internal").ap()

        def twice(name, cols):
            with nc.sbuf_tensor(name, [P, cols], F32) as t:
                t = t[:, :]
            return t, ctx.enter_context(nc.sbuf_tensor(name + "_r", [P, cols], F32R))[:, :]

        ring, ring_r = twice("ring", RINGM * SLOT)
        x = sb("x", TT * D).rearrange("p (t d) -> p t d", t=TT)
        xR = ctx.enter_context(nc.sbuf_tensor("xR", [P, 2 * KT * T], F32R))[:, :].rearrange("p (c k t) -> p c k t", c=2, k=KT)
        cst = sb("cst", a["c_kept"].shape[1])
        vec1 = sb("vec1", 112)
        vec2 = sb("vec2", 78)
        stat = sb("stat", 512)
        mt2 = sb("mt2", 2 * 512)
        arena, arena_r = twice("arena", ARENA)
        psum = ctx.enter_context(nc.psum_tensor("psum", [P, 8, 512], F32))[:, :, :]

        def K(name):
            o, n = cst_at[name]
            return cst[:, o:o + n]

        def R(at, kt, c=2):
            return arena_r[:, at:at + c * kt * T].rearrange("p (c k t) -> p c k t", c=c, k=kt)

        ident, ones = K("ident"), K("ones")

        class Place:

            def __init__(self, at):
                self.at = at

            def __call__(self, n):
                self.at += n
                assert self.at <= ARENA, self.at
                return arena[:, self.at - n:self.at]

        pl = Place(0)
        gate_m, gate_f, gbc = pl(D), pl(D), pl(D)
        tri = pl(TT * T).rearrange("p (k t) -> p k t", k=TT)
        slot_id = pl(NE * CAP).rearrange("p (e c) -> p e c", e=NE)
        base1 = pl.at
        uf = pl(TT * 512).rearrange("p (t n) -> p t n", t=TT)
        part = uf
        v_at = pl.at
        vT = pl(KT * T).rearrange("p (k t) -> p k t", k=KT)
        cv = pl(KT * (T + 2)).rearrange("p (k t) -> p k t", k=KT)
        b_at = pl.at
        bT = pl(KT * T).rearrange("p (k t) -> p k t", k=KT)
        convH, convL = R(v_at, KT, 1)[:, 0], R(b_at, KT, 1)[:, 0]
        ga_at = pl.at
        gaT = pl(KT * T).rearrange("p (k t) -> p k t", k=KT)
        gbT = pl(KT * T).rearrange("p (k t) -> p k t", k=KT)
        Bcs = gbT.rearrange("p (g h) t -> p g (h t)", g=4)
        fmR = R(pl.at, 4)
        pl(2 * 4 * T)
        dfts = pl(TT * 2 * T).rearrange("p (k n) -> p k n", k=TT)
        dftg = pl(2 * P).rearrange("p (c n) -> p c n", c=2)
        vrow = pl(2 * P).rearrange("p (c n) -> p c n", c=2)
        t5tab = pl(8)
        t5vec = pl(REL)
        narow = pl(NAREL)
        early = Place(ga_at)
        t5hot, diladd = early(REL), early(REL)
        csil = early(KT * 32).rearrange("p (k n) -> p k n", k=KT)
        lamraw = early(LAYERS * P).rearrange("p (l n) -> p l n", l=LAYERS)
        lamprod = early(LAYERS * 2 * 32).rearrange("p (l c n) -> p l c n", l=LAYERS, c=2)
        assert early.at <= ga_at + KT * T
        xn1 = vT.rearrange("p k t -> p (k t)").rearrange("p (t d) -> p t d", t=TT)
        mtmp = uf.rearrange("p t n -> p (t n)")

        pm = Place(base1)
        h2n = pm(TT * D).rearrange("p (t d) -> p t d", t=TT)
        xTm = pm(KT * T).rearrange("p (k t) -> p k t", k=KT)
        acc = pm(TT * D).rearrange("p (t d) -> p t d", t=TT)
        sel = pm(TT * NE * CAP).rearrange("p (t n) -> p t n", t=TT)
        selw = pm(TT * NE * CAP).rearrange("p (t n) -> p t n", t=TT)
        rep = pm(TT * P).rearrange("p (t j c) -> p t j c", t=TT, j=4)
        selT = pm(T)
        xeT = pm(KT * CAP).rearrange("p (k c) -> p k c", k=KT)
        hT = pm(4 * P).rearrange("p (s n) -> p s n", s=4)
        sil = pm(512)
        gu = pm(512)
        ysb = pm(T)
        wr = pm(KT * NE).rearrange("p (k e) -> p k e", k=KT)
        brow = pm(NE)
        lg = pm(TT * NE).rearrange("p (t e) -> p t e", t=TT)
        ex = pm(TT * NE).rearrange("p (t e) -> p t e", t=TT)
        prob = pm(TT * NE).rearrange("p (t e) -> p t e", t=TT)
        pT = pm(T)
        work = pm(T)
        mk = pm(T)
        top8 = pm(8)
        maskn = pm(TT * NE).rearrange("p (t e) -> p t e", t=TT)
        posm = pm(TT * NE).rearrange("p (t e) -> p t e", t=TT)
        xn2 = h2n

        p2 = Place(D)
        zA = p2(D).rearrange("p (t n) -> p t n", t=TT)
        p2.at = 3 * D
        qaT = p2(4 * T).rearrange("p (k t) -> p k t", k=4)
        ksT = p2(2 * T).rearrange("p (g t) -> p g t", g=2)
        kwT = p2(2 * T).rearrange("p (g t) -> p g t", g=2)
        yR = R(3 * D, KT)
        k2 = p2(2 * 2 * T).rearrange("p (c g t) -> p c g t", c=2, g=2)
        kb2 = p2(2 * 16 * 32).rearrange("p (c l n) -> p c l n", c=2, l=16)
        hk = p2(64).rearrange("p (c n) -> p c n", c=2)
        kcT = p2(32)
        vcn = p2(2 * HD).rearrange("p (g n) -> p g n", g=2)
        vs = p2(TT * P).rearrange("p (t n) -> p t n", t=TT)
        vw = p2(TT * P).rearrange("p (t n) -> p t n", t=TT)
        gn = p2(TT * 24).rearrange("p (t n) -> p t n", t=TT)
        qbT = p2(4 * T).rearrange("p (k t) -> p k t", k=4)
        kbT = p2(4 * T).rearrange("p (k t) -> p k t", k=4)
        vbn = p2(TT * 512).rearrange("p (t n) -> p t n", t=TT)
        zB = p2(TT * 512).rearrange("p (t n) -> p t n", t=TT)
        oA = p2(TT * 512).rearrange("p (t n) -> p t n", t=TT)
        oB = p2(TT * 512).rearrange("p (t n) -> p t n", t=TT)
        mAT = p2(KT * T).rearrange("p (k t) -> p k t", k=KT)
        mBT = p2(KT * T).rearrange("p (k t) -> p k t", k=KT)
        xn3 = mAT.rearrange("p k t -> p (k t)").rearrange("p (t d) -> p t d", t=TT)
        mixn = mBT.rearrange("p k t -> p (k t)").rearrange("p (t d) -> p t d", t=TT)
        yjunk = arena[:, 3 * D:5 * D].rearrange("p (t d) -> p t d", t=TT)
        pj = Place(p2.at)
        sbuf = pj(2 * T).rearrange("p (b n) -> p b n", b=2)
        ebuf = pj(2 * T).rearrange("p (b n) -> p b n", b=2)
        pbuf = pj(2 * T).rearrange("p (b n) -> p b n", b=2)

        p3 = Place(0)
        nab = p3(8 * T).rearrange("p (h t n) -> p h t n", h=4, t=TT)
        p3.at = 3 * D
        qk = p3(12 * T).rearrange("p (k t) -> p k t", k=12)
        mixR = R(3 * D, KT)
        actR = R(3 * D, FT)
        v3 = p3(3 * TT * T).rearrange("p (c t n) -> p c t n", c=3, t=TT)
        cqn = p3(TT * 256).rearrange("p (t n) -> p t n", t=TT)
        ckvn = p3(TT * P).rearrange("p (t n) -> p t n", t=TT)
        krn = p3(TT * 32).rearrange("p (t n) -> p t n", t=TT)
        cqT = p3(2 * T).rearrange("p (k t) -> p k t", k=2)
        ckvT = p3(T).rearrange("p (k t) -> p k t", k=1)
        qdn = p3(TT * 4 * 96).rearrange("p (t h n) -> p t h n", t=TT, h=4)
        kcat = p3(TT * 4 * 96).rearrange("p (t h n) -> p t h n", t=TT, h=4)
        vd = p3(TT * T).rearrange("p (t n) -> p t n", t=TT)
        qmT, kmT = qk[:, 0:4, :], qk[:, 4:8, :]
        mix = p3(TT * D).rearrange("p (t d) -> p t d", t=TT)
        rp_ = mt2[:, 0:512]
        rp = rp_.rearrange("p (c t h n) -> p c t h n", c=4, t=TT, h=4)
        hsq = rp_.rearrange("p (t h n) -> p t h n", t=TT, h=4)
        rk = mt2[:, 512:512 + 4 * TT * 16].rearrange("p (c t n) -> p c t n", c=4, t=TT)
        pbuf3 = p3(2 * T).rearrange("p (b n) -> p b n", b=2)
        act_end = 3 * D + 2 * FT * T
        assert p3.at <= act_end
        p3.at = act_end
        t5b = p3(8 * TT * T).rearrange("p (h t n) -> p h t n", h=8, t=TT)
        pj.at = p3.at
        sbuf3 = pj(2 * T).rearrange("p (b n) -> p b n", b=2)
        ebuf3 = pj(2 * T).rearrange("p (b n) -> p b n", b=2)

        silu = [b.rearrange("p b n -> p (b n)") for b in (sbuf3, ebuf3)]

        st = Place(0)
        st.at = 0

        def small(n, _p=[0]):
            _p[0] += n
            assert _p[0] <= 512
            return stat[:, _p[0] - n:_p[0]]

        neghalf = small(2)
        mod = small(48)
        Am, Bm, Af, Bf = small(8), small(8), small(8), small(8)
        ssq, rstd = small(2), small(2)
        rmax, rsum, rrec = small(2), small(2), small(2)
        negmax = small(2)
        jmin, jsum, jrec = small(2), small(2), small(2)
        lamneg = small(LAYERS)
        lamsum = small(4)
        lamexp = small(4)
        subg = small(LAYERS * HD).rearrange("p (l n) -> p l n", l=LAYERS)
        hstat = small(16)
        hrstd = small(8)
        halfs = small(8)
        subl = small(HD)
        spare = small(NJ3 + 5)

        t5_row = dram("t5_row", (8, REL))
        t5_rep = dram("t5_rep", (8, (P + 1) * REL))
        na_row = dram("na_row", (LAYERS * 4 * 7, NAREL))
        na_rep = dram("na_rep", (LAYERS * 4 * 7, GRID_W * NAREL))

        w_ready = [sem(f"w_ready{i}") for i in range(RING)]
        wm_ready = [sem(f"wm_ready{i}") for i in range(RINGM)]
        w2_ready = [sem(f"w2_ready{i}") for i in range(RING)]
        c_high = [sem(f"c_high{i}") for i in range(3)]
        c_low = [sem(f"c_low{i}") for i in range(3)]
        x_high = sem("x_high")
        e_unit = sem("e_unit")
        w3_ready = [sem(f"w3_ready{i}") for i in range(RING)]
        g_ready = sem("g_ready")
        g_free = [sem(f"g_free{i}") for i in range(4)]
        in_x, in_cst, in_vec, in_b1 = sem("in_x"), sem("in_cst"), sem("in_vec"), sem("in_b1")
        in_moe, in_route = sem("in_moe"), sem("in_route")
        consts_set = sem("consts_set")
        n_sq, n_ms, n_rstd, n_xn = sem("n_sq"), sem("n_ms"), sem("n_rstd"), sem("n_xn")
        v_used = sem("v_used")
        v_cols = sem("v_cols")
        c_act = sem("c_act")
        part_ready = sem("part_ready")
        mod_mm = sem("mod_mm")
        mod_done = sem("mod_done")
        cv_done, conv_done = sem("cv_done"), sem("conv_done")
        z_done = sem("z_done")
        x1_done = sem("x1_done")
        r_lg, r_exp, r_prob, r_sel = sem("r_lg"), sem("r_exp"), sem("r_prob"), sem("r_sel")
        e_rep, e_gath, e_xe, e_selTp, e_selT = (sem(n) for n in ("e_rep", "e_gath", "e_xe", "e_selTp", "e_selT"))
        e_sil, e_gu, e_hTp, e_hT = (sem(n) for n in ("e_sil", "e_gu", "e_hTp", "e_hT"))
        e_y, e_sc, e_acc = (sem(n) for n in ("e_y", "e_sc", "e_acc"))
        x2_done, x3_done = sem("x2_done"), sem("x3_done")
        g3_ready = sem("g3_ready")
        g3_free = [sem(f"g3_free{i}") for i in range(4)]
        w3_dn = sem("w3_dn")
        n3_sq, n3_ms, n3_rstd, n3_xn = (sem(n) for n in ("n3_sq", "n3_ms", "n3_rstd", "n3_xn"))
        h_sq, h_rstd, h_ms = sem("h_sq"), sem("h_rstd"), sem("h_ms")
        d_sq, d_rstd, d_ms = sem("d_sq"), sem("d_rstd"), sem("d_ms")
        lat_n, rope_q, rope_k, mix_done = (sem(n) for n in ("lat_n", "rope_q", "rope_k", "mix_done"))
        xm_done, nab_done = sem("xm_done"), sem("nab_done")
        in_t5, in_na, in_fin, in_lam = sem("in_t5"), sem("in_na"), sem("in_fin"), sem("in_lam")
        in_rel, rel_st, rel_rep, rel_na = sem("in_rel"), sem("rel_st"), sem("rel_rep"), sem("rel_na")
        lam_s, lam_e = sem("lam_s"), sem("lam_e")
        y_out = sem("y_out")
        act_done = sem("act_done")
        k_s, k_min, k_exp, k_t, k_p, k_o, k_done = (sem(n) for n in ("k_s", "k_min", "k_exp", "k_t", "k_p", "k_o", "k_done"))
        in_post = sem("in_post")
        kb_done, gn_done, m_done, y_done, x4_done = (sem(n) for n in ("kb_done", "gn_done", "m_done", "y_done", "x4_done"))
        j_s, j_min, j_exp, j_t, j_p, j_o, j_done = (sem(n) for n in ("j_s", "j_min", "j_exp", "j_t", "j_p", "j_o", "j_done"))
        s_out = sem("s_out")
        rel_io = sem("rel_io")
        rel_src = sem("rel_src")

        def slot(n, m=RING):
            return ring[:, (n % m) * SLOT:(n % m + 1) * SLOT]

        def chunk(blk, c):
            _, n, kt, width, c0, cols, at, _ = (CH1, CH2, CH3)[blk][c]
            lo = (n % RING) * SLOT + at
            w, low = (t[:, lo:lo + kt * width].rearrange("p (k c) -> p k c", k=kt)[:, :, c0:c0 + cols]
                      for t in (ring, ring_r))
            h0 = RING * SLOT + (c % 2) * 2048
            high = ring_r[:, h0:h0 + kt * cols].rearrange("p (k c) -> p k c", k=kt)
            return w, high, low

        PARTS2 = {U2AT["kvwg"]: 4, U2AT["w1"]: 2, U2AT["ab0"]: 2, U2AT["ab1"]: 2}

        def landed(n):
            return 16 * (n // RING + 1)

        def landed2(n):
            return 16 * sum(PARTS2.get(m, 1) for m in range(n % RING, n + 1, RING))

        def landed3(n, l):
            per = 16 * sum(PARTS3.get(m, 1) for m in range(n % RING, len(L3), RING))
            return l * per + 16 * sum(PARTS3.get(m, 1) for m in range(n % RING, n + 1, RING))

        def piece(eng, i, l=None):
            if l is None:
                eng.wait_ge(g_ready, i + 1)
            else:
                eng.wait_ge(g3_ready, l * LPN + (i + 1))

        def bank_free(eng, i, l=None):
            if i >= 4:
                if l is None:
                    eng.wait_ge(g_free[i % 4], i // 4)
                else:
                    eng.wait_ge(g3_free[i % 4], l * (LPN // 4) + i // 4)

        def taken(eng, *idx, l=None):
            for i in idx:
                if l is None:
                    eng.wait_ge(g_free[i % 4], i // 4 + 1)
                else:
                    eng.wait_ge(g3_free[i % 4], l * (LPN // 4) + (i // 4 + 1))

        def G(i):
            return psum[:, i % 4, :]

        def halves(blk, c):
            kt = (CH1, CH2, CH3)[blk][c][2]
            return (slice(0, kt // 2), slice(kt // 2, kt))

        def piece_used(eng, blk, c, l=None):
            name = (CH1, CH2, CH3)[blk][c][7]
            if blk < 2:
                piece(eng, AT[name])
            elif name[:2] == "dn":
                eng.wait_ge(w3_dn, l * 10 + (int(name[2:]) + 1))
            else:
                piece(eng, LAT[name], l)

        class Splitter:

            def __init__(self, eng, blk, l=None):
                self.eng, self.blk, self.l, self.next = eng, blk, l, 0

            def ahead(self, c):
                n = len((CH1, CH2, CH3)[self.blk])
                while self.next <= min(c + 2, n - 1):
                    self.split(self.next)
                    self.next += 1

        class High(Splitter):
            def split(self, c):
                blk, l = self.blk, self.l
                n = (CH1, CH2, CH3)[blk][c][1]
                if blk == 0:
                    self.eng.wait_ge(w_ready[n % RING], landed(n))
                elif blk == 1:
                    self.eng.wait_ge(w2_ready[n % RING], landed2(n))
                else:
                    self.eng.wait_ge(w3_ready[n % RING], landed3(n, l))
                if c >= 2:
                    piece_used(self.eng, blk, c - 2, l)
                w, high, _ = chunk(blk, c)
                for k in halves(blk, c):
                    nc.scalar.copy(high[:, k, :], w[:, k, :]).then_inc(c_high[blk], 1)

        class Low(Splitter):
            def split(self, c):
                blk, l = self.blk, self.l
                w, high, low = chunk(blk, c)
                base = 0 if l is None else l * (2 * len(CH3))
                for i, k in enumerate(halves(blk, c)):
                    self.eng.wait_ge(c_high[blk], base + (2 * c + i + 1))
                    nc.vector.tensor_tensor(low[:, k, :], w[:, k, :], high[:, k, :].bitcast(F32),
                                            ALU.subtract).then_inc(c_low[blk], 1)

        def job3(j, l):
            kind, h, c, t = JOBS3[j]
            qs = slice(t * P, t * P + P)
            if kind == "mla":
                return dict(q=qmT[0:96, h, qs], k=kmT[0:96, h, :], widths=[P] * TT, bias=None,
                            v=[vd[:, i, h * HD:h * HD + HD] for i in range(TT)],
                            out=mix[:, t, 768 + h * HD:832 + h * HD], coef=None, first=True)
            b = ("na", "diff", "dil").index(kind)
            lo, n = (HD * (h % 2), HD) if kind != "diff" else (HD * (h % 2) + 32 * c, 32)
            bias = nab[:, h, t, :] if kind == "na" else t5b[:, h + 4 * (kind == "dil"), t, :]
            return dict(q=qk[lo:lo + n, 4 * b + h // 2, qs], k=qk[lo:lo + n, 4 * b + 2 + h // 2, :], widths=[P] * TT,
                        bias=bias, v=[v3[:, b, i, h * HD:h * HD + HD] for i in range(TT)],
                        out=mix[:, t, 256 * b + h * HD:256 * b + h * HD + HD],
                        coef=lamneg[:, bass.ds(l, 1)] if c else None, first=c == 0)

        def job2(j):
            br, h, t = JOBS2[j]
            lo = HD * (h % 2)
            g = h // 4
            qs = slice(t * P, t * P + P)
            part_ = slice(lo, lo + HD)
            out_ = (oB if br == "moba" else oA)[:, t, h * HD:h * HD + HD]
            dist = K("dist")[:, 0:P] if t == 0 else K("dist")[:, P:P + T]
            nk = P * (t + 1)
            if br == "cmp":
                return dict(q=qaT[part_, h // 2, qs], k=kcT[part_, g * NCMP:(g + 1) * NCMP], widths=[NCMP],
                            dist=K("cmpdist")[:, 16 * t:16 * t + NCMP], slope=slope(2 * h),
                            v=[vcn[0:NCMP, g, :]], out=out_, coef=gn[:, t, h:h + 1], first=True)
            if br == "moba":
                return dict(q=qbT[part_, h // 2, qs], k=kbT[part_, h // 2, 0:nk], widths=[P] * (t + 1), dist=dist,
                            slope=slope(2 * h + 1), v=[vbn[:, i, h * HD:h * HD + HD] for i in range(t + 1)],
                            out=out_, coef=None, first=True)
            kk, vv, i = (ksT, vs, 1) if br == "slc" else (kwT, vw, 2)
            return dict(q=qaT[part_, h // 2, qs], k=kk[part_, g, 0:nk], widths=[P] * (t + 1), dist=dist,
                        slope=slope(2 * h), v=[vv[:, u, g * HD:g * HD + HD] for u in range(t + 1)],
                        out=out_, coef=gn[:, t, 8 * i + h:8 * i + h + 1], first=False)

        block = ctx.enter_context(nc.Block())

        @block.sync
        def _(sp):
            sp.dma_start(vrow[0:48, 0, :], a["b_ada"].rearrange("l (r n) -> (l r) n", n=P)).then_inc(in_vec, 16)
            for r0, n, t in ((48, 8, a["g_norm_mix"]), (56, 8, a["g_norm_moe"]), (64, 8, a["c"]),
                             (88, 8, None), (96, 16, a["b_gate"])):
                if t is not None:
                    sp.dma_start(vrow[r0:r0 + n, 0, :], t.rearrange("l (r n) -> (l r) n", n=P)).then_inc(in_vec, 16)
            sp.dma_start(vrow[72:96, 0, :], a["w_conv"].rearrange("l w (r n) -> (l w r) n", n=P)).then_inc(in_vec, 16)
            r0 = 0
            for t in ("norm_pre_2", "attn_norm_3", "ffn_norm_3", "mla_q_norm_3", "mla_kv_norm_3"):
                v = a[t].rearrange("l (r n) -> (l r) n", n=P)
                sp.dma_start(vrow[r0:r0 + v.shape[0], 1, :], v).then_inc(in_vec, 16)
                r0 += v.shape[0]
            for t in ("cmp_pe_k_2", "cmp_pe_v_2"):
                sp.dma_start(vrow[r0:r0 + 16, 1, :], a[t].rearrange("l (r c) d -> (l r) (c d)", c=2)).then_inc(in_vec, 16)
                r0 += 16
            sp.dma_start(t5tab[0:32, :], a["t5_table_3"]).then_inc(in_rel, 16)
            sp.dma_start(t5hot[0:32, :], a["c_rel"][0:32, 0:REL]).then_inc(in_rel, 16)
            sp.dma_start(diladd[0:8, :], a["c_rel"][0:8, REL:2 * REL]).then_inc(in_rel, 16)
            sp.dma_start(lamraw, a["diff_lambda_3"].rearrange("l c n -> l (c n)").partition_broadcast(P)).then_inc(in_lam, 16)
            sp.dma_start(subg, a["diff_subln_3"].partition_broadcast(P)).then_inc(in_lam, 16)
            sp.dma_start(cst, a["c_kept"]).then_inc(in_cst, 16)
            sp.dma_start(x, a["x"].rearrange("b (t p) d -> p (b t) d", p=P)).then_inc(in_x, 16)

            def unit(n, *moves):
                if n >= RING:
                    sp.wait_ge(g_ready, LAST[n - RING] + 1)
                for dst, src in moves:
                    sp.dma_start(dst, src).then_inc(w_ready[n % RING], 16)

            def cols(w, c0, n, kt=KT):
                return w.rearrange("l (k p) n -> p (l k) n", p=P)[:, 0:kt, c0:c0 + n]

            def dst(n, kt, c, at=0):
                return slot(n)[:, at:at + kt * c].rearrange("p (k c) -> p k c", k=kt)

            for i in range(12):
                n = UAT[f"ada{i}"]
                unit(n, (dst(n, KT, 512), cols(a["w_ada"], 512 * i, 512)))
                if i == 0:
                    sp.dma_start(gate_m, a["b_ada"][:, 2 * D:3 * D].partition_broadcast(P).squeeze(1)).then_inc(in_b1, 16)
                    sp.dma_start(gate_f, a["b_ada"][:, 5 * D:6 * D].partition_broadcast(P).squeeze(1)).then_inc(in_b1, 16)
                    sp.dma_start(dfts, a["c_dft"][:, 0:TT * 2 * T].rearrange("p (k n) -> p k n", k=TT)).then_inc(in_b1, 16)
                    sp.dma_start(dftg, a["c_dft"][:, TT * 2 * T:].rearrange("p (k n) -> p k n", k=2)).then_inc(in_b1, 16)
                    sp.dma_start(arena[:, 3 * D:3 * D + 1024], a["c_moe"]).then_inc(in_moe, 16)
                    sp.dma_start(gbc, a["g_final"].unsqueeze(0).partition_broadcast(P).squeeze(1)).then_inc(in_moe, 16)
            for i in range(11):
                n = UAT[f"win{i}"]
                unit(n, (dst(n, KT, 512), cols(a["w_in"], 512 * i, 512)))
            for i in range(2):
                n = UAT[f"wf{i}"]
                unit(n, (dst(n, 4, 512), cols(a["w_fourier"], 512 * i, 512, 4)))
            for nm, w in (("wc", "w_conv_out"), ("wo", "w_o")):
                for i in range(2):
                    n = UAT[f"{nm}{i}"]
                    unit(n, (dst(n, KT, 512), cols(a[w], 512 * i, 512)))
            wg = a["w_gate_e"].rearrange("l e (k p) f -> p (l e k) f", p=P)
            wu = a["w_up_e"].rearrange("l e (k p) f -> p (l e k) f", p=P)
            wd = a["w_down_e"].rearrange("l e (k p) d -> p (l e k) d", p=P)

            def expert_unit(e, i):
                if i < 8:
                    w = wg if i < 4 else wu
                    src = w[:, bass.ds(e * KT + 2 * (i % 4), 2), :]
                    d = slot(i, RINGM).rearrange("p (k c) -> p k c", k=2)
                else:
                    src = wd[:, bass.ds(e * (FE // P) + 4 * (i - 8), 4), :]
                    d = slot(i, RINGM).rearrange("p (k c) -> p k c", k=4)
                sp.dma_start(d, src).then_inc(wm_ready[i % RINGM], 16)

            for i in [(N_MOE + j) % RING for j in range(RING)] + [RING]:
                prev = max(n for n in range(N_MOE) if n % RING == i) if i < RING else N_MOE - 1
                sp.wait_ge(g_ready, LAST[prev] + 1)
                expert_unit(0, i)
            with sp.Fori(0, NE - 1) as e:
                for i in range(RINGM, UPE):
                    sp.wait_ge(e_unit, e * UPE + (i - RINGM + 1))
                    expert_unit(e, i)
                for i in range(RINGM):
                    sp.wait_ge(e_unit, e * UPE + (i + RINGM + 1))
                    expert_unit(e + 1, i)
            for i in range(RINGM, UPE):
                sp.wait_ge(e_unit, (NE - 1) * UPE + (i - RINGM + 1))
                expert_unit(NE - 1, i)
            def unit2(name, *moves):
                n = U2AT[name]
                if n < RING:
                    sp.wait_ge(e_unit, (NE - 1) * UPE + RINGM + n + 1)
                else:
                    sp.wait_ge(g_ready, LAST2[n - RING] + 1)
                for d, src in moves:
                    sp.dma_start(d, src).then_inc(w2_ready[n % RING], 16)

            def w2cols(name, c0, n):
                unit2(name, (dst(U2AT[name], KT, n), cols(a["w_in_2"], c0, n)))

            w2cols("qa", 0, 512)
            w2cols("kv", 512, 512)
            n = U2AT["kvwg"]
            unit2("kvwg", (dst(n, KT, 280), cols(a["w_in_2"], 1024, 280)),
                  (dst(n, 1, HD, KT * 280), cols(a["cmp_w2_k_2"], 0, HD, 1)),
                  (dst(n, 1, HD, KT * 280 + HD), cols(a["cmp_w2_k_2"], 0, HD, 1)),
                  (dst(n, 1, HD, KT * 280 + P), cols(a["cmp_w2_v_2"], 0, HD, 1)))
            n = U2AT["w1"]
            unit2("w1", *[(dst(n, 16, P, 2048 * i), a[f"cmp_w1_{c}_2"].rearrange("o (l c) d e -> (c d) (o l) e", c=2))
                          for i, c in enumerate("kv")])
            for nm, c0 in (("za", 1304), ("qb", 1816), ("kb", 2328), ("vb", 2840), ("zb", 3352), ("mg0", 3864),
                           ("mg1", 4376), ("mg2", 4888), ("mg3", 5400)):
                w2cols(nm, c0, 512)
            for i in range(2):
                n = U2AT[f"ab{i}"]
                unit2(f"ab{i}", (dst(n, 4, 512), cols(a["w_branch_a_2"], 512 * i, 512, 4)),
                      (dst(n, 4, 512, 2048), cols(a["w_branch_b_2"], 512 * i, 512, 4)))
            for i in range(2):
                n = U2AT[f"wo2_{i}"]
                unit2(f"wo2_{i}", (dst(n, KT, 512), cols(a["w_o_2"], 512 * i, 512)))
            for l in range(LAYERS):
                def unit3(name, *moves):
                    n = L3AT[name]
                    if n < RING and l == 0:
                        prev = max(m for m in LAST2 if m % RING == n)
                        sp.wait_ge(g_ready, LAST2[prev] + 1)
                    else:
                        m, ll = (n - RING, l) if n >= RING else (n + len(L3) - RING, l - 1)
                        if m in LAST3:
                            sp.wait_ge(g3_ready, ll * LPN + LAST3[m] + 1)
                        else:
                            sp.wait_ge(w3_dn, ll * 10 + 2 * (m - L3AT["dn0"]) + 2)
                    for d, src in moves:
                        sp.dma_start(d, src).then_inc(w3_ready[n % RING], 16)

                def dst3(n, kt, c, at=0):
                    return slot(n)[:, at:at + kt * c].rearrange("p (k c) -> p k c", k=kt)

                def kcols(w, c0, n, k0=0, kt=KT):
                    return w[l, k0 * P:(k0 + kt) * P, c0:c0 + n].rearrange("(k p) n -> p k n", p=P)

                for i in range(5):
                    unit3(f"win{i}", (dst3(L3AT[f"win{i}"], KT, 512), kcols(a["w_in_3"], 512 * i, 512)))
                if l == 0:
                    sp.wait_ge(x4_done, 1)
                    sp.wait_ge(rel_rep, 16)
                    for h in range(8):
                        for t in range(TT):
                            o = T - 1 - t * P
                            src = t5_rep[h, o:o + P * (REL - 1)].rearrange("(q w) -> q w", w=REL - 1)[:, 0:T]
                            sp.dma_start(t5b[:, h, t, :], src).then_inc(in_t5, 16)
                n = L3AT["win5"]
                unit3("win5", (dst3(n, KT, 160), kcols(a["w_in_3"], 2560, 160)),
                      (dst3(n, 2, 384, KT * 160), kcols(a["w_uq_3"], 0, 384, 0, 2)),
                      (dst3(n, 1, 512, KT * 160 + 768), kcols(a["w_ukv_3"], 0, 512, 0, 1)))
                for i in range(2):
                    unit3(f"wo{i}", (dst3(L3AT[f"wo{i}"], KT, 512), kcols(a["w_o_3"], 512 * i, 512)))
                for i in range(11):
                    n = L3AT[f"gu{i}"]
                    d = dst3(n, KT, 512)
                    unit3(f"gu{i}", (d[:, :, 0:256], kcols(a["w_gate_3"], 256 * i, 256)),
                          (d[:, :, 256:512], kcols(a["w_up_3"], 256 * i, 256)))
                for i in range(6):
                    kt = min(4, FT - 4 * i)
                    unit3(f"dn{i}", (dst3(L3AT[f"dn{i}"], kt, D), kcols(a["w_down_3"], 0, D, 4 * i, kt)))
            sp.wait_ge(y_out, 2)
            sp.dma_start(out.rearrange("b (t p) d -> p (b t) d", p=P), x).then_inc(s_out, 16)
            sp.wait_ge(s_out, 16)

        @block.gpsimd
        def _(pool):
            nc.gpsimd.memset(neghalf, -0.5).then_inc(consts_set, 1)
            nc.gpsimd.memset(csil.rearrange("p k n -> p (k n)"), 0.0).then_inc(consts_set, 1)
            nc.gpsimd.memset(cv.rearrange("p k t -> p (k t)"), 0.0).then_inc(consts_set, 1)
            nc.gpsimd.memset(narow, 0.0).then_inc(consts_set, 1)
            nc.gpsimd.memset(halfs, -0.5).then_inc(consts_set, 1)

            def rstd_of(k):
                pool.wait_ge(n_sq, 2 * k + 2)
                nc.gpsimd.tensor_scalar(rstd, ssq, 1.0 / D, EPS, ALU.mult, ALU.add).then_inc(n_ms, 1)
                pool.wait_ge(n_ms, k + 1)
                if k == 0:
                    pool.wait_ge(consts_set, 1)
                nc.gpsimd.tensor_tensor(rstd, rstd, neghalf, ALU.pow).then_inc(n_rstd, 1)

            rstd_of(0)
            pool.wait_ge(consts_set, 4)
            for l in range(LAYERS):
                for h in range(4):
                    r = (l * 4 + h) * 7
                    pool.dma_start(narow[r:r + 7, 48:79], a["na_rpb_3"][l, h, 4:11, :]).then_inc(rel_na, 16)
            pool.wait_ge(rel_na, 16 * 8)
            pool.dma_start(na_row, narow[0:56, :]).then_inc(rel_na, 16)
            pool.wait_ge(rel_src, 1)
            pool.dma_start(t5_row, t5vec[0:8, :]).then_inc(rel_st, 16)
            pool.wait_ge(rel_na, 16 * 9)
            pool.dma_start(na_rep.rearrange("r (q n) -> r q n", q=GRID_W),
                           na_row.unsqueeze(1).broadcast_to([56, GRID_W, NAREL])).then_inc(rel_na, 16)
            pool.wait_ge(rel_st, 16)
            pool.dma_start(t5_rep[:, 0:P * REL].rearrange("r (q n) -> r q n", q=P),
                           t5_row.unsqueeze(1).broadcast_to([8, P, REL])).then_inc(rel_rep, 16)
            pool.wait_ge(rel_na, 16 * 10)
            pool.wait_ge(x1_done, 4)
            pool.dma_start(wr, a["w_router"].rearrange("l (k p) e -> p (l k) e", p=P)).then_inc(in_route, 16)
            pool.dma_start(brow, a["b_router"].partition_broadcast(P).squeeze(1)).then_inc(in_route, 16)
            rstd_of(1)
            nc.gpsimd.memset(acc.rearrange("p t d -> p (t d)"), 0.0).then_inc(e_acc, 1)
            rstd_of(2)
            pool.wait_ge(x3_done, 1)
            pool.dma_start(gbc, a["norm_post_2"].partition_broadcast(P).squeeze(1)).then_inc(in_post, 16)
            rstd_of(3)
            rstd_of(4)

            def roots(at_, dst_, src, widths, sq, ms, need, at):
                pool.wait_ge(sq, need)
                nc.gpsimd.tensor_tensor(spare[:, NJ3 + at_:NJ3 + at_ + 1], halfs[:, 0:1], halfs[:, 0:1], ALU.mult)
                for lo, hi, w in widths:
                    o = nc.gpsimd.tensor_scalar(dst_[:, lo:hi], src[:, lo:hi], 1.0 / w, EPS, ALU.mult, ALU.add)
                    o.then_inc(ms, 1)
                pool.wait_ge(ms, at)
                n = widths[-1][1]
                return nc.gpsimd.tensor_tensor(dst_[:, 0:n], dst_[:, 0:n], halfs[:, 0:n], ALU.pow)

            with pool.Fori(0, LAYERS) as l:
                pool.wait_ge(x4_done, l + 1)
                for h in range(4):
                    for t in range(TT):
                        for r in range(2):
                            qr = 2 * t + r
                            src = na_rep[bass.ds(l * 28 + (h * 7 + 3 - qr), 4), GRID_W - 1:GRID_W - 1 + GRID_W * (NAREL - 1)]
                            src = src.rearrange("r (q w) -> q r w", w=NAREL - 1)[:, :, 0:GRID_W]
                            pool.dma_start(nab[GRID_W * r:GRID_W * r + GRID_W, h, t, :].rearrange("p (r n) -> p r n", r=4),
                                           src).then_inc(in_na, 16)
                roots(0, rstd, ssq, [(0, 2, D)], n3_sq, n3_ms, l * 4 + 2, l * 2 + 1).then_inc(n3_rstd, 1)
                roots(1, hrstd, hstat, [(0, 2, 256), (2, 4, P)], h_sq, h_ms, l * 4 + 4, l * 2 + 2).then_inc(h_rstd, 1)
                roots(2, hrstd, hstat, [(0, 8, HD)], d_sq, d_ms, l + 1, l + 1).then_inc(d_rstd, 1)
                roots(3, rstd, ssq, [(0, 2, D)], n3_sq, n3_ms, l * 4 + 4, l * 2 + 2).then_inc(n3_rstd, 1)
            pool.dma_start(gbc, a["final_norm_3"].unsqueeze(0).partition_broadcast(P).squeeze(1)).then_inc(in_fin, 16)
            roots(4, rstd, ssq, [(0, 2, D)], n3_sq, n3_ms, LAYERS * 4 + 2, LAYERS * 2 + 1).then_inc(n3_rstd, 1)

        @block.scalar
        def _(act):
            def squares(xn, src=x, sq=n_sq):
                for t in range(TT):
                    nc.scalar.activation(xn[:, t, :], src[:, t, :], ACT.Square,
                                         accum_out=ssq[:, t:t + 1]).then_inc(sq, 1)

            act.wait_ge(v_cols, 1)
            act.wait_ge(consts_set, 2)
            nc.scalar.activation(csil[:, :, 0:1], vec1[:, 64:72].unsqueeze(2), ACT.Silu).then_inc(c_act, 1)
            act.wait_ge(in_x, 16)
            squares(xn1)
            act.wait_ge(lam_s, 1)
            nc.scalar.activation(lamexp, lamsum, ACT.Exp).then_inc(lam_e, 1)
            for u in range(12):
                i = AT[f"ada{u}"]
                piece(act, i)
                if u >= 2:
                    act.wait_ge(mod_mm, u - 1)
                nc.scalar.copy(part[:, u % 2, :], G(i)).then_inc(g_free[i % 4], 1)
            high = High(act, 0)
            high.ahead(-1)
            for i in (AT["uf0"], AT["uf1"]):
                high.ahead(C1AT[f"uf{i - AT['uf0']}"])
                piece(act, i)
                h = i - AT["uf0"]
                nc.scalar.copy(uf[:, :, 256 * h:256 * h + 256],
                               G(i).rearrange("p (t n) -> p t n", t=TT)).then_inc(g_free[i % 4], 1)
            for g in range(4):
                i = AT[f"dfta{g}"]
                piece(act, i)
                nc.scalar.copy(Bcs[:, g, :], G(i)).then_inc(g_free[i % 4], 1)
            for nm, dstT in (("v", vT), ("b", bT)):
                for h in range(4):
                    i = AT[f"{nm}{h}"]
                    high.ahead(C1AT[f"{nm}{h}"])
                    piece(act, i)
                    nc.scalar.copy(dstT[:, 2 * h:2 * h + 2, :],
                                   G(i).rearrange("p (k t) -> p k t", k=2)).then_inc(g_free[i % 4], 1)
            for h in range(4):
                high.ahead(C1AT[f"c{h}"])
            for b, (nm, dstT) in enumerate((("ga", gaT), ("gb", gbT))):
                for h in range(4):
                    i = AT[f"{nm}{h}"]
                    high.ahead(C1AT[f"{nm}{h}"])
                    piece(act, i)
                    for m in range(2):
                        k = 2 * h + m
                        o = nc.scalar.activation(dstT[:, k, :], G(i)[:, m * T:m * T + T], ACT.Sigmoid,
                                                 bias=vec1[:, 96 + 8 * b + k:97 + 8 * b + k])
                    o.then_inc(g_free[i % 4], 1)
            for nm in ("wf", "wc", "wo"):
                for h in range(4):
                    high.ahead(C1AT[f"{nm}{h}"])
            act.wait_ge(x1_done, 4)
            act.wait_ge(n_rstd, 1)
            act.wait_ge(n_xn, 1)
            squares(xn2)
            for h in range(4):
                i = AT[f"h2n{h}"]
                piece(act, i)
                nc.scalar.copy(h2n[:, h // 2, 512 * (h % 2):512 * (h % 2) + 512], G(i)).then_inc(g_free[i % 4], 1)
            act.wait_ge(r_lg, 1)
            for t in range(TT):
                nc.scalar.activation(ex[:, t, :], lg[:, t, :], ACT.Exp, bias=negmax[:, t:t + 1],
                                     accum_out=rsum[:, t:t + 1]).then_inc(r_exp, 1)
            with act.Fori(0, NE) as e:
                act.wait_ge(e_unit, e * UPE + 4)
                nc.scalar.activation(sil, psum[:, 0, :], ACT.Silu).then_inc(e_sil, 1)
                act.wait_ge(e_hTp, e + 1)
                nc.scalar.copy(hT.rearrange("p s n -> p (s n)"), psum[:, 3, :]).then_inc(e_hT, 1)
                act.wait_ge(e_unit, e * UPE + UPE)
                nc.scalar.copy(ysb, psum[:, 2, 0:T]).then_inc(e_y, 1)
            act.wait_ge(x2_done, 1)
            squares(xn2)

            act.wait_ge(x3_done, 1)
            squares(xn3)
            high = High(act, 1)
            high.ahead(-1)

            def take(name, d, func=ACT.Copy, scale=1.0, src=None, l=None):
                i = AT[name] if l is None else LAT[name]
                piece(act, i, l)
                src = G(i) if src is None else src(G(i))
                free = g_free if l is None else g3_free
                return nc.scalar.activation(d, src, func, scale=scale).then_inc(free[i % 4], 1)

            def two(g):
                return g.rearrange("p (k n) -> p k n", k=2)

            SC = HD ** -0.5
            for h in range(2):
                high.ahead(C2AT[f"qa{h}"])
                take(f"qa{h}", qaT[:, 2 * h:2 * h + 2, :], scale=-SC, src=two)
            high.ahead(C2AT["kc"])
            high.ahead(C2AT["ksvs"])
            take("vs", vs, src=lambda g: two(g[:, 0:2 * P]))
            high.ahead(C2AT["kwvw"])
            take("vw", vw, src=lambda g: two(g[:, 0:2 * P]))
            high.ahead(C2AT["gnsa"])
            take("gnsa", gn, ACT.Sigmoid, src=lambda g: two(g[:, 0:48]))
            take("hk", hk[:, :, 0:2 * NCMP], ACT.Silu, src=lambda g: two(g[:, 0:64])[:, :, 0:2 * NCMP])
            take("kcT", kcT[:, 0:2 * NCMP], src=lambda g: g[:, 0:2 * NCMP])
            take("vcn", vcn[0:NCMP, :, :], src=lambda g: two(g[0:NCMP, 0:2 * HD]))

            def exp_of(j, J, mins, exps, turned, ended, base=0, sbuf=sbuf, ebuf=ebuf):
                b = j % 2
                act.wait_ge(mins, base + (j + 1))
                nk = sum(J["widths"])
                if j >= 2:
                    act.wait_ge(turned, base + (j - 1))
                    act.wait_ge(ended, base + (j - 1))
                nc.scalar.activation(ebuf[:, b, 0:nk], sbuf[:, b, 0:nk], ACT.Exp, bias=jmin[:, b:b + 1], scale=-1.0,
                                     accum_out=jsum[:, b:b + 1]).then_inc(exps, 1)

            def probs_of(j, J, turned, used, probs, base=0, pbuf=pbuf):
                b = j % 2
                act.wait_ge(turned, base + (j + 1))
                if j >= 2:
                    act.wait_ge(used, base + (j - 1))
                w = J["widths"]
                d = pbuf[0:w[0], b, 0:len(w) * P]
                nc.scalar.copy(d, psum[0:w[0], 6, 0:len(w) * P]).then_inc(probs, 1)

            for kind, n in PLAN2:
                if kind == "job":
                    exp_of(n, job2(n), j_min, j_exp, j_t, j_done)
                    if n >= 1:
                        probs_of(n - 1, job2(n - 1), j_t, j_o, j_p)
                    continue
                h = int(n[-1])
                high.ahead(C2AT[n])
                if n[:2] == "za":
                    take(n, zA[:, :, 256 * h:256 * h + 256], ACT.Silu, src=two)
                elif n[:2] == "zb":
                    take(n, zB[:, :, 256 * h:256 * h + 256], ACT.Silu, src=two)
                elif n[:2] == "qb":
                    take(n, qbT[:, 2 * h:2 * h + 2, :], scale=-SC, src=two)
                elif n[:2] == "kb":
                    take(n, kbT[:, 2 * h:2 * h + 2, :], src=two)
                elif n[:2] == "vb":
                    take(n, vbn[:, :, 256 * h:256 * h + 256], src=two)
                else:
                    take(n, (mAT if n[1] == "A" else mBT)[:, 2 * h:2 * h + 2, :], ACT.Sigmoid, src=two)
            probs_of(len(JOBS2) - 1, job2(len(JOBS2) - 1), j_t, j_o, j_p)
            for q in range(2):
                for nm in ("wa", "wb"):
                    for h in (2 * q, 2 * q + 1):
                        high.ahead(C2AT[f"{nm}{h}"])
            for h in range(4):
                high.ahead(C2AT[f"wo2_{h}"])
                take(f"wo2_{h}", mixn[:, :, 256 * h:256 * h + 256], src=two)
            nc.scalar.drain()
            squares(yjunk, mixn)

            Q = {"qa0": (0, -SC), "ka0": (2, 1.0), "qb0": (4, -((HD // 2) ** -0.5)), "kb0": (6, 1.0), "qc0": (8, -SC),
                 "kc0": (10, 1.0)}
            with act.Fori(0, LAYERS) as l:
                act.wait_ge(x4_done, l + 1)
                squares(mix, sq=n3_sq)
                high = High(act, 2, l)
                high.ahead(-1)
                for kind, n in PLAN3:
                    if kind == "job":
                        exp_of(n, job3(n, l), k_min, k_exp, k_t, k_done, l * NJ3, sbuf3, ebuf3)
                        if n >= 1:
                            probs_of(n - 1, job3(n - 1, l), k_t, k_o, k_p, l * NJ3, pbuf3)
                        continue
                    c = "ckvkr" if n == "kr" else n
                    if c in C3AT:
                        high.ahead(C3AT[c])
                    if n in Q:
                        at, sc = Q[n]
                        take(n, qk[:, at:at + 2, :], scale=sc, src=two, l=l)
                    elif n in ("va0", "vb0", "vc0"):
                        take(n, v3[:, "abc".index(n[1]), :, :], src=two, l=l)
                    elif n == "cq":
                        take(n, cqn, src=two, l=l)
                    elif n == "ckv":
                        take(n, ckvn, src=lambda g: two(g[:, 0:2 * P]), l=l)
                    elif n == "kr":
                        take(n, krn, src=lambda g: two(g[:, 0:64]), l=l)
                        nc.scalar.drain()
                        for t in range(TT):
                            nc.scalar.activation(cqT[:, t, :], cqn[:, t, :], ACT.Square,
                                                 accum_out=hstat[:, t:t + 1]).then_inc(h_sq, 1)
                            nc.scalar.activation(ckvT[:, 0, t * P:t * P + P], ckvn[:, t, :], ACT.Square,
                                                 accum_out=hstat[:, 2 + t:3 + t]).then_inc(h_sq, 1)
                    elif n[:2] == "uq":
                        t = int(n[-1])
                        take(n, qdn[:, t, :, :], scale=-(96.0 ** -0.5),
                             src=lambda g: g[:, 0:384].rearrange("p (h n) -> p h n", h=4), l=l)
                    elif n[:3] == "ukv":
                        t = int(n[-1])
                        i = LAT[n]
                        piece(act, i, l)
                        g = G(i).rearrange("p (h c n) -> p h c n", h=4, c=2)
                        nc.scalar.copy(kcat[:, t, :, 0:HD], g[:, :, 0, :])
                        nc.scalar.copy(vd[:, t, :].rearrange("p (h n) -> p h n", h=4),
                                       g[:, :, 1, :]).then_inc(g3_free[i % 4], 1)
                    elif n[:2] in ("qm", "km"):
                        h = 2 * int(n[-1])
                        take(n, (qmT if n[0] == "q" else kmT)[0:96, h:h + 2, :], src=lambda g: two(g[0:96, :]), l=l)
                probs_of(NJ3 - 1, job3(NJ3 - 1, l), k_t, k_o, k_p, l * NJ3, pbuf3)
                for h in range(4):
                    high.ahead(C3AT[f"wo3_{h}"])
                act.wait_ge(xm_done, l * 4 + 4)
                squares(mix, sq=n3_sq)
                for i in range(11):
                    high.ahead(C3AT[f"gu{2 * i}"])
                    if i >= 2:
                        taken(act, LAT[f"gu{2 * i - 3}"], l=l)
                    take(f"gu{2 * i}", silu[i % 2], ACT.Silu, l=l)
                    high.ahead(C3AT[f"gu{2 * i + 1}"])
                for i in range(11):
                    high.ahead(C3AT[f"dn{i}"])
            act.wait_ge(x4_done, LAYERS + 1)
            squares(mix, sq=n3_sq)

        @block.tensor
        def _(pe):
            def mm(o, l, r, s=True, e=True):
                return nc.tensor.matmul(o, l, r, start=s, stop=e)

            def unit(n):
                pe.wait_ge(w_ready[n % RING], landed(n))

            def ready(o, l):
                return o.then_inc(g_ready if l is None else g3_ready, 1)

            def rows(i, w, kt, c0, width, xs, l=None):
                bank_free(pe, i, l)
                for t in range(TT):
                    for k in range(kt):
                        o = mm(G(i)[:, t * width:(t + 1) * width], xs[:, k, t * P:t * P + P], w[:, k, c0:c0 + width],
                               k == 0, k == kt - 1)
                return ready(o, l)

            def colsT(i, w, kt, c0, xs, ms=2, k0=0, l=None):
                bank_free(pe, i, l)
                for m in range(ms):
                    for k in range(kt):
                        o = mm(G(i)[:, m * T:m * T + T], w[:, k, c0 + m * P:c0 + m * P + P], xs[:, k0 + k, :],
                               k == 0, k == kt - 1)
                return ready(o, l)

            def split_ready(blk, name, l):
                c = (C1AT, C2AT, C3AT)[blk][name]
                pe.wait_ge(c_low[blk], (0 if l is None else l * (2 * len(CH3))) + 2 * (c + 1))
                return chunk(blk, c)[1:]

            def product(o, pairs):
                for j, (lhs, rhs, first, last) in enumerate(pairs):
                    (lh, ll), (rh, rl) = lhs, rhs
                    mm(o, lh, rh, first, False)
                    mm(o, lh, rl, False, False)
                    r = mm(o, ll, rh, False, last)
                return r

            def rows3(i, blk, name, xs, l=None, c0=0, width=256):
                wh, wl = split_ready(blk, name, l)
                kt = wh.shape[1]
                bank_free(pe, i, l)
                for t in range(TT):
                    ts = slice(t * P, t * P + P)
                    o = product(G(i)[:, t * width:(t + 1) * width],
                                [((xs[0][:, k, ts], xs[1][:, k, ts]),
                                  (wh[:, k, c0:c0 + width], wl[:, k, c0:c0 + width]), k == 0, k == kt - 1)
                                 for k in range(kt)])
                return ready(o, l)

            def cols3(i, blk, name, xs, l=None, c0=0, ms=2, k0=0):
                wh, wl = split_ready(blk, name, l)
                kt = wh.shape[1]
                bank_free(pe, i, l)
                for m in range(ms):
                    cs = slice(c0 + m * P, c0 + m * P + P)
                    o = product(G(i)[:, m * T:m * T + T],
                                [((wh[:, k, cs], wl[:, k, cs]), (xs[0][:, k0 + k, :], xs[1][:, k0 + k, :]),
                                  k == 0, k == kt - 1) for k in range(kt)])
                return ready(o, l)

            def turn_x(first, src, l=None):
                for h in range(4):
                    i = first + h
                    bank_free(pe, i, l)
                    for m in range(2):
                        for t in range(TT):
                            k = 2 * h + m
                            o = nc.tensor.transpose(G(i)[:, m * T + t * P:m * T + t * P + P],
                                                    src[:, t, k * P:k * P + P], ident)
                    ready(o, l)

            pe.wait_ge(in_vec, 16 * 13)
            pe.wait_ge(in_cst, 16)
            nc.tensor.transpose(psum[:, 5, 0:112], vrow[0:112, 0, :], ident[0:112, 0:112])
            nc.tensor.transpose(psum[:, 5, 128:206], vrow[0:78, 1, :], ident[0:78, 0:78]).then_inc(v_used, 1)
            pe.wait_ge(in_rel, 48)
            mm(psum[0:8, 7, :], t5tab[0:32, :], t5hot[0:32, :]).then_inc(v_used, 1)
            pe.wait_ge(rel_src, 1)
            pe.wait_ge(c_act, 1)

            def mod_second(u):
                taken(pe, AT[f"ada{u}"])
                if u not in GATE_UNITS:
                    for s in range(4):
                        o = mm(psum[:, 4, 4 * u + s:4 * u + s + 1], part[:, u % 2, s * P:s * P + P], ones[:, 0:1])
                    o.then_inc(mod_mm, 1)
                else:
                    r = GATE_UNITS.index(u)
                    if r >= 2:
                        pe.wait_ge(mod_done, r - 1)
                    mm(psum[:, 6 + r % 2, :], ones, part[:, u % 2, :]).then_inc(mod_mm, 1)

            for u in range(12):
                i, n = AT[f"ada{u}"], UAT[f"ada{u}"]
                unit(n)
                bank_free(pe, i)
                w = slot(n).rearrange("p (k c) -> p k c", k=KT)
                for k in range(2):
                    for j in range(4):
                        o = mm(G(i)[32 * j:32 * j + 32, :], csil[:, 2 * j + k, :], w[:, 2 * j + k, :], k == 0, k == 1)
                o.then_inc(g_ready, 1)
                if u >= 1:
                    mod_second(u - 1)
            mod_second(11)

            def W(n, kt, c, at=0):
                return slot(n)[:, at:at + kt * c].rearrange("p (k c) -> p k c", k=kt)

            xs = (xR[:, 0], xR[:, 1])
            pe.wait_ge(n_xn, 1)
            turn_x(AT["n1_0"], xn1)
            taken(pe, *range(AT["n1_0"], AT["n1_0"] + 4))
            for h in range(2):
                rows3(AT[f"uf{h}"], 0, f"uf{h}", xs)
            taken(pe, AT["uf0"], AT["uf1"])
            pe.wait_ge(in_b1, 16 * 4)
            for g in range(4):
                i = AT[f"dfta{g}"]
                bank_free(pe, i)
                for k in range(TT):
                    o = mm(G(i), uf[:, k, g * P:g * P + P], dfts[:, k, :], k == 0, k == 1)
                o.then_inc(g_ready, 1)
            for h in range(2):
                i = AT[f"dftb{h}"]
                bank_free(pe, i)
                for m in range(2):
                    g = 2 * h + m
                    taken(pe, AT[f"dfta{g}"])
                    for c in range(2):
                        o = mm(G(i)[:, m * T:m * T + T], dftg[:, c, :], Bcs[:, g, c * T:c * T + T], c == 0, c == 1)
                o.then_inc(g_ready, 1)
            for b, nm in enumerate(("v", "b", "c", "ga", "gb")):
                for h in range(4):
                    cols3(AT[f"{nm}{h}"], 0, f"{nm}{h}", xs)
            taken(pe, AT["dftb0"], AT["dftb1"])
            for h in range(4):
                cols3(AT[f"wf{h}"], 0, f"wf{h}", (fmR[:, 0], fmR[:, 1]))
            pe.wait_ge(conv_done, 4)
            for h in range(4):
                cols3(AT[f"wc{h}"], 0, f"wc{h}", (convH, convL))
            pe.wait_ge(z_done, 4)
            for h in range(4):
                rows3(AT[f"wo{h}"], 0, f"wo{h}", xs)

            pe.wait_ge(n_xn, 2)
            turn_x(AT["n2_0"], xn2)
            taken(pe, *range(AT["n2_0"], AT["n2_0"] + 4))
            for h in range(4):
                i = AT[f"h2n{h}"]
                bank_free(pe, i)
                for m in range(4):
                    k = 4 * (h % 2) + m
                    o = nc.tensor.transpose(G(i)[:, m * P:m * P + P], xTm[:, k, (h // 2) * P:(h // 2) * P + P], ident)
                o.then_inc(g_ready, 1)
            pe.wait_ge(in_moe, 16 * 2)
            pe.wait_ge(in_route, 16 * 2)
            rows(AT["rt"], wr, KT, 0, NE, xTm)
            pe.wait_ge(r_prob, 1)
            i = AT["pt"]
            bank_free(pe, i)
            for t in range(TT):
                o = nc.tensor.transpose(G(i)[0:NE, t * P:t * P + P], prob[:, t, :], ident)
            o.then_inc(g_ready, 1)
            pe.wait_ge(r_sel, 1)
            i = AT["mk"]
            bank_free(pe, i)
            for t in range(TT):
                o = nc.tensor.transpose(G(i)[:, t * NE:t * NE + NE], mk[0:NE, t * P:t * P + P], ident[0:NE, 0:NE])
            o.then_inc(g_ready, 1)
            taken(pe, AT["mk"])
            i = AT["pos"]
            bank_free(pe, i)
            for t in range(TT):
                for k in range(TT):
                    o = mm(G(i)[:, t * NE:t * NE + NE], tri[:, k, t * P:t * P + P], maskn[:, k, :], k == 0, k == 1)
            o.then_inc(g_ready, 1)
            pe.wait_ge(r_sel, 2)
            taken(pe, *range(AT["pos"] - 3, AT["pos"] + 1))
            taken(pe, *range(AT["h2n0"], AT["h2n0"] + 4))

            def landed_e(e, i):
                pe.wait_ge(wm_ready[i % RINGM], e * (16 * UPE // RINGM) + 16 * (i // RINGM + 1))

            with pe.Fori(0, NE) as e:
                for k in range(KT):
                    for t in range(TT):
                        o = mm(psum[:, 3, k * CAP:k * CAP + CAP], h2n[:, t, k * P:k * P + P],
                               sel[:, t, bass.ds(e * CAP, CAP)], t == 0, t == 1)
                o.then_inc(e_gath, 1)
                pe.wait_ge(e_rep, e + 1)
                for t in range(TT):
                    o = nc.tensor.transpose(psum[:, 2, t * P:t * P + P], rep[:, t, :, :].rearrange("p j c -> p (j c)"), ident)
                o.then_inc(e_selTp, 1)
                pe.wait_ge(e_xe, e + 1)
                for i in range(8):
                    landed_e(e, i)
                    w = slot(i, RINGM).rearrange("p (k c) -> p k c", k=2)
                    for k in range(2):
                        kk = 2 * (i % 4) + k
                        for j in range(4):
                            o = mm(psum[32 * j:32 * j + 32, i // 4, :], xeT[:, kk, :], w[:, k, 512 * j:512 * j + 512],
                                   kk == 0, kk == KT - 1)
                    o.then_inc(e_unit, 1)
                pe.wait_ge(e_gu, e + 1)
                for s in range(4):
                    o = nc.tensor.transpose(psum[:, 3, s * P:s * P + P], gu[:, s * P:s * P + P], ident)
                o.then_inc(e_hTp, 1)
                pe.wait_ge(e_hT, e + 1)
                pe.wait_ge(e_selT, e + 1)
                for q in range(4):
                    landed_e(e, 8 + q)
                    w = slot(8 + q, RINGM).rearrange("p (k c) -> p k c", k=4)
                    for s in range(4):
                        for j in range(4):
                            o = mm(psum[32 * j:32 * j + 32, 2, 0:T], hT[:, s, 32 * q:32 * q + 32],
                                   w[:, s, T * j:T * j + T], q == 0 and s == 0, q == 3 and s == 3)
                    o.then_inc(e_unit, 1)
                pe.wait_ge(e_y, e + 1)
                pe.wait_ge(e_acc, e + 1)
                for t in range(TT):
                    for j in range(4):
                        o = mm(psum[:, 4 + j, t * T:t * T + T], selT[32 * j:32 * j + 32, t * P:t * P + P],
                               ysb[32 * j:32 * j + 32, :])
                o.then_inc(e_sc, 1)

            pe.wait_ge(n_xn, 3)
            turn_x(AT["n3_0"], xn3)
            taken(pe, *range(AT["n3_0"], AT["n3_0"] + 4))

            def unit2(n):
                pe.wait_ge(w2_ready[n % RING], landed2(n))

            for h in range(2):
                cols3(AT[f"qa{h}"], 1, f"qa{h}", xs)
            cols3(AT["kc"], 1, "kc", xs)
            cols3(AT["ks"], 1, "ksvs", xs, ms=1)
            rows3(AT["vs"], 1, "ksvs", xs, c0=P, width=P)
            cols3(AT["kw"], 1, "kwvw", xs, ms=1)
            rows3(AT["vw"], 1, "kwvw", xs, c0=P, width=P)
            rows3(AT["gnsa"], 1, "gnsa", xs, width=24)
            unit2(U2AT["w1"])
            i = AT["hk"]
            bank_free(pe, i)
            pe.wait_ge(kb_done, 1)
            for c in range(2):
                w = W(U2AT["w1"], 16, P, 2048 * c)
                for l in range(16):
                    o = mm(G(i)[:, 32 * c:32 * c + 2 * NCMP], w[:, l, :], kb2[:, c, l, 0:2 * NCMP], l == 0, l == 15)
            o.then_inc(g_ready, 1)
            taken(pe, AT["hk"])
            i = AT["kcT"]
            bank_free(pe, i)
            w = slot(U2AT["kvwg"])[:, KT * 280:KT * 280 + 3 * HD]
            mm(G(i)[:, 0:2 * NCMP], w[:, 0:P], hk[:, 0, 0:2 * NCMP]).then_inc(g_ready, 1)
            i = AT["vcn"]
            bank_free(pe, i)
            for g in range(2):
                o = mm(G(i)[0:NCMP, g * HD:g * HD + HD], hk[:, 1, g * NCMP:g * NCMP + NCMP], w[:, P:P + HD])
            o.then_inc(g_ready, 1)

            def scores(j, J, s_, m_, base=0):
                if j >= 2:
                    pe.wait_ge(m_, base + (j - 1))
                mm(psum[:, 4 + j % 2, 0:sum(J["widths"])], J["q"], J["k"]).then_inc(s_, 1)

            def turn(j, J, x_, p_, t_, base=0, ebuf=ebuf):
                pe.wait_ge(x_, base + (j + 1))
                if j >= 1:
                    pe.wait_ge(p_, base + j)
                at = 0
                for i, w in enumerate(J["widths"]):
                    o = nc.tensor.transpose(psum[0:w, 6, i * P:i * P + P], ebuf[:, j % 2, at:at + w], ident)
                    at += w
                o.then_inc(t_, 1)

            def values(j, J, p_, d_, o_, base=0, pbuf=pbuf):
                pe.wait_ge(p_, base + (j + 1))
                if j >= 1:
                    pe.wait_ge(d_, base + j)
                n = len(J["widths"])
                for i, w in enumerate(J["widths"]):
                    o = mm(psum[:, 7, 0:HD], pbuf[0:w, j % 2, i * P:i * P + P], J["v"][i], i == 0, i == n - 1)
                o.then_inc(o_, 1)

            NJ = len(JOBS2)
            taken(pe, *[AT[n] for n in ("qa0", "qa1", "ks", "kw", "vs", "vw", "kcT", "vcn")])
            for kind, n in PLAN2:
                if kind == "job":
                    if n == len(NSA_JOBS):
                        taken(pe, *[AT[m] for m in ("qb0", "qb1", "kb0", "kb1", "vb0", "vb1")])
                    scores(n, job2(n), j_s, j_min)
                    if n >= 1:
                        turn(n - 1, job2(n - 1), j_exp, j_p, j_t)
                    if n >= 2:
                        values(n - 2, job2(n - 2), j_p, j_done, j_o)
                    continue
                (cols3 if n[0] in "mqk" else rows3)(AT[n], 1, n, xs)
            turn(NJ - 1, job2(NJ - 1), j_exp, j_p, j_t)
            for j in (NJ - 2, NJ - 1):
                values(j, job2(j), j_p, j_done, j_o)
            pe.wait_ge(y_done, 1)
            for h in range(4):
                i = AT[f"yt{h}"]
                bank_free(pe, i)
                src = (oA, oB)[h // 2]
                for m in range(2):
                    for t in range(TT):
                        k = 2 * (h % 2) + m
                        o = nc.tensor.transpose(G(i)[:, m * T + t * P:m * T + t * P + P],
                                                src[:, t, k * P:k * P + P], ident)
                o.then_inc(g_ready, 1)
            taken(pe, *[AT[f"yt{h}"] for h in range(4)])
            for q in range(2):
                for b, nm in ((0, "wa"), (1, "wb")):
                    for h in (2 * q, 2 * q + 1):
                        cols3(AT[f"{nm}{h}"], 1, f"{nm}{h}", (yR[:, 0], yR[:, 1]), k0=4 * b)
            pe.wait_ge(m_done, 4)
            for h in range(4):
                rows3(AT[f"wo2_{h}"], 1, f"wo2_{h}", xs)

            with pe.Fori(0, LAYERS) as l:
                def unit3(n):
                    pe.wait_ge(w3_ready[n % RING], landed3(n, l))

                def W3(n, kt, c, at=0):
                    return slot(n)[:, at:at + kt * c].rearrange("p (k c) -> p k c", k=kt)

                pe.wait_ge(n3_xn, l * 2 + 1)
                turn_x(LAT["n4_0"], mix, l)
                taken(pe, *range(4), l=l)
                pe.wait_ge(nab_done, l + 1)
                win = ["qa0", "ka0", "va0", "qb0", "kb0", "vb0", "qc0", "kc0", "vc0", "cq"]
                done = set()
                for kind, n in PLAN3:
                    if kind == "job":
                        br = JOBS3[n][0]
                        if br not in done:
                            done.add(br)
                            need = {"na": ("qa0", "ka0", "va0"), "diff": ("qb0", "kb0", "vb0"),
                                    "dil": ("qc0", "kc0", "vc0"), "mla": ("qm0", "qm1", "km0", "km1", "ukv0", "ukv1")}[br]
                            taken(pe, *[LAT[m] for m in need], l=l)
                        scores(n, job3(n, l), k_s, k_min, l * NJ3)
                        if n >= 1:
                            turn(n - 1, job3(n - 1, l), k_exp, k_p, k_t, l * NJ3, ebuf3)
                        if n >= 2:
                            values(n - 2, job3(n - 2, l), k_p, k_done, k_o, l * NJ3, pbuf3)
                        continue
                    i = LAT[n]
                    if n in win:
                        (rows3 if n[0] == "v" or n == "cq" else cols3)(i, 2, n, xs, l)
                    elif n == "ckv":
                        rows3(i, 2, "ckvkr", xs, l, width=P)
                    elif n == "kr":
                        rows3(i, 2, "ckvkr", xs, l, c0=P, width=32)
                    elif n in ("cqT", "ckvT"):
                        pe.wait_ge(lat_n, l + 1)
                        bank_free(pe, i, l)
                        for m in range(2 if n == "cqT" else 1):
                            for t in range(TT):
                                src = (cqn if n == "cqT" else ckvn)[:, t, m * P:m * P + P]
                                o = nc.tensor.transpose(G(i)[:, m * T + t * P:m * T + t * P + P], src, ident)
                        ready(o, l)
                    elif n[:2] == "uq":
                        t = int(n[-1])
                        taken(pe, LAT["cqT"], l=l)
                        bank_free(pe, i, l)
                        w = W3(5, 2, 384, KT * 160)
                        for k in range(2):
                            o = mm(G(i)[:, 0:384], cqT[:, k, t * P:t * P + P], w[:, k, :], k == 0, k == 1)
                        ready(o, l)
                    elif n[:3] == "ukv":
                        t = int(n[-1])
                        taken(pe, LAT["ckvT"], l=l)
                        bank_free(pe, i, l)
                        ready(mm(G(i), ckvT[:, 0, t * P:t * P + P], W3(5, 1, 512, KT * 160 + 768)[:, 0, :]), l)
                    else:
                        pe.wait_ge(rope_q if n[0] == "q" else rope_k, l + 1)
                        bank_free(pe, i, l)
                        for m in range(2):
                            for t in range(TT):
                                src = (qdn if n[0] == "q" else kcat)[:, t, 2 * int(n[-1]) + m, :]
                                o = nc.tensor.transpose(G(i)[0:96, m * T + t * P:m * T + t * P + P], src, ident)
                        ready(o, l)
                turn(NJ3 - 1, job3(NJ3 - 1, l), k_exp, k_p, k_t, l * NJ3, ebuf3)
                for j in (NJ3 - 2, NJ3 - 1):
                    values(j, job3(j, l), k_p, k_done, k_o, l * NJ3, pbuf3)
                pe.wait_ge(mix_done, l + 1)
                turn_x(LAT["mix0"], mix, l)
                taken(pe, *[LAT[f"mix{h}"] for h in range(4)], l=l)
                for h in range(4):
                    rows3(LAT[f"wo3_{h}"], 2, f"wo3_{h}", (mixR[:, 0], mixR[:, 1]), l)
                pe.wait_ge(n3_xn, l * 2 + 2)
                turn_x(LAT["n5_0"], mix, l)
                taken(pe, *[LAT[f"n5_{h}"] for h in range(4)], l=l)
                for i in range(22):
                    cols3(LAT[f"gu{i}"], 2, f"gu{i}", xs, l)
                pe.wait_ge(act_done, l * 11 + 11)
                for q in range(4):
                    bank_free(pe, LAT[f"down{q}"], l)
                for c in range(FT // 2):
                    wh, wl = split_ready(2, f"dn{c}", l)
                    for k in range(2):
                        kk = 2 * c + k
                        for q in range(4):
                            ts, hs = slice(q // 2 * P, q // 2 * P + P), slice(512 * (q % 2), 512 * (q % 2) + 512)
                            o = product(psum[:, q, :], [((actR[:, 0, kk, ts], actR[:, 1, kk, ts]),
                                                         (wh[:, k, hs], wl[:, k, hs]), kk == 0, kk == FT - 1)])
                            if kk == FT - 1:
                                ready(o, l)
                    if c < FT // 2 - 1:
                        o.then_inc(w3_dn, 1)

        @block.vector
        def _(dve):
            v = nc.vector
            xs = (xR[:, 0], xR[:, 1])

            def temp(h, k=2):
                return mt2[:, 512 * (h % 2):512 * (h % 2) + 512].rearrange("p (k t) -> p k t", k=k)

            def parts(src, xs, ks):
                v.tensor_copy(xs[0][:, ks, :], src)
                v.drain()
                return v.tensor_tensor(xs[1][:, ks, :], src, xs[0][:, ks, :].bitcast(F32), ALU.subtract)

            def modulated(first, A, B, l=None, whole=None):
                for h in range(4):
                    i = first + h
                    piece(dve, i, l)
                    d = temp(h) if whole is None else whole[:, 2 * h:2 * h + 2, :]
                    for m in range(2):
                        k = 2 * h + m
                        if B is None:
                            o = v.tensor_scalar(d[:, m, :], G(i)[:, m * T:m * T + T], A[:, k:k + 1], None, ALU.mult)
                        else:
                            o = v.tensor_scalar(d[:, m, :], G(i)[:, m * T:m * T + T], A[:, k:k + 1], B[:, k:k + 1],
                                                ALU.mult, ALU.add)
                    if whole is None:
                        v.drain()
                        o = parts(d, xs, slice(2 * h, 2 * h + 2))
                    o.then_inc((g_free if l is None else g3_free)[i % 4], 1)

            def normed(k, xn):
                dve.wait_ge(n_rstd, k + 1)
                for t in range(TT):
                    o = v.tensor_scalar(xn[:, t, :], x[:, t, :], rstd[:, t:t + 1], None, ALU.mult)
                o.then_inc(n_xn, 1)

            def pair(ap):
                return ap.rearrange("p (k t) -> p k t", k=2)

            dve.wait_ge(v_used, 1)
            v.tensor_copy(vec1, psum[:, 5, 0:112])
            v.tensor_copy(vec2, psum[:, 5, 128:206]).then_inc(v_cols, 1)
            dve.wait_ge(v_used, 2)
            dve.wait_ge(in_rel, 48)
            v.scalar_tensor_tensor(t5vec[0:8, :], psum[0:8, 7, :], -1.0, diladd[0:8, :], ALU.mult,
                                   ALU.add).then_inc(rel_src, 1)
            dve.wait_ge(in_lam, 32)
            lr = lamraw.rearrange("p l (a b n) -> p l a b n", a=2, b=2)
            for l in range(LAYERS):
                v.tensor_tensor(lamprod[:, l, :, :], lr[:, l, :, 0, :], lr[:, l, :, 1, :], ALU.mult)
                v.tensor_scalar(subg[:, l, :], subg[:, l, :], 1.0 - LAM_INIT[l], None, ALU.mult)
            v.drain()
            v.tensor_reduce(lamsum, lamprod.rearrange("p l c n -> p (l c) n"), AX_X, ALU.add).then_inc(lam_s, 1)
            normed(0, xn1)
            dve.wait_ge(in_b1, 16 * 4)
            dve.wait_ge(lam_e, 1)
            for l in range(LAYERS):
                v.tensor_tensor(lamneg[:, l:l + 1], lamexp[:, 2 * l + 1:2 * l + 2], lamexp[:, 2 * l:2 * l + 1], ALU.subtract)
            v.drain()
            for l in range(LAYERS):
                v.tensor_scalar(lamneg[:, l:l + 1], lamneg[:, l:l + 1], -LAM_INIT[l], None, ALU.add)
            for r, u in enumerate(GATE_UNITS):
                if u == 10:
                    dve.wait_ge(mod_mm, 10)
                    v.tensor_tensor(mod[:, 0:16], psum[:, 4, 0:16], vec1[:, 0:16], ALU.add)
                    v.tensor_tensor(mod[:, 24:40], psum[:, 4, 24:40], vec1[:, 24:40], ALU.add)
                    v.drain()
                    v.scalar_tensor_tensor(Am, mod[:, 8:16], 1.0, vec1[:, 48:56], ALU.add, ALU.mult)
                    v.scalar_tensor_tensor(Af, mod[:, 32:40], 1.0, vec1[:, 56:64], ALU.add, ALU.mult)
                dve.wait_ge(mod_mm, u + 1)
                g = (gate_m, gate_f)[r // 2][:, 512 * (r % 2):512 * (r % 2) + 512]
                v.tensor_tensor(g, psum[:, 6 + r % 2, :], g, ALU.add).then_inc(mod_done, 1)
            v.drain()
            low = Low(dve, 0)
            low.ahead(-1)
            modulated(AT["n1_0"], Am, mod[:, 0:8])
            for h in range(2):
                low.ahead(C1AT[f"uf{h}"])
            for h in range(2):
                i = AT[f"dftb{h}"]
                piece(dve, i)
                parts(pair(G(i)), (fmR[:, 0], fmR[:, 1]), slice(2 * h, 2 * h + 2)).then_inc(g_free[i % 4], 1)
            for nm in "vb":
                for h in range(4):
                    low.ahead(C1AT[f"{nm}{h}"])
            for h in range(4):
                i = AT[f"c{h}"]
                low.ahead(C1AT[f"c{h}"])
                piece(dve, i)
                if h == 0:
                    taken(dve, *[AT[f"v{j}"] for j in range(4)])
                    taken(dve, *[AT[f"b{j}"] for j in range(4)])
                    dve.wait_ge(consts_set, 3)
                v.tensor_tensor(cv[:, 2 * h:2 * h + 2, 1:T + 1], pair(G(i)), vT[:, 2 * h:2 * h + 2, :],
                                ALU.mult).then_inc(g_free[i % 4], 1)
                v.drain()
                w = [vec1[:, 72 + 8 * j + 2 * h:74 + 8 * j + 2 * h] for j in range(3)]
                for m in range(2):
                    v.tensor_scalar(mtmp[:, m * T:m * T + T], cv[:, 2 * h + m, 0:T], w[0][:, m:m + 1], None, ALU.mult)
                for j in (1, 2):
                    v.drain()
                    for m in range(2):
                        v.scalar_tensor_tensor(mtmp[:, m * T:m * T + T], cv[:, 2 * h + m, j:T + j], w[j][:, m:m + 1],
                                               mtmp[:, m * T:m * T + T], ALU.mult, ALU.add)
                v.drain()
                v.tensor_tensor(temp(h), bT[:, 2 * h:2 * h + 2, :], mtmp[:, 0:2 * T].rearrange("p (k t) -> p k t", k=2),
                                ALU.mult)
                v.drain()
                parts(temp(h), (convH, convL), slice(2 * h, 2 * h + 2)).then_inc(conv_done, 1)
            for nm in ("ga", "gb"):
                for h in range(4):
                    low.ahead(C1AT[f"{nm}{h}"])
            for nm, gate in (("wf", gaT), ("wc", gbT)):
                for h in range(4):
                    i = AT[f"{nm}{h}"]
                    low.ahead(C1AT[f"{nm}{h}"])
                    piece(dve, i)
                    if h == 0:
                        for j in range(4):
                            taken(dve, AT[("ga" if nm == "wf" else "gb") + str(j)])
                    g = gate[:, 2 * h:2 * h + 2, :]
                    v.tensor_tensor(g, pair(G(i)), g, ALU.mult).then_inc(g_free[i % 4], 1)
                    if nm == "wc":
                        v.drain()
                        z = gaT[:, 2 * h:2 * h + 2, :]
                        v.tensor_tensor(temp(h), z, g, ALU.add)
                        v.drain()
                        parts(temp(h), xs, slice(2 * h, 2 * h + 2)).then_inc(z_done, 1)
            for h in range(4):
                i = AT[f"wo{h}"]
                low.ahead(C1AT[f"wo{h}"])
                piece(dve, i)
                c = slice(256 * h, 256 * h + 256)
                mt = mtmp[:, 512 * (h % 2):512 * (h % 2) + 512].rearrange("p (t n) -> p t n", t=TT)
                v.tensor_tensor(mt, G(i).rearrange("p (t n) -> p t n", t=TT),
                                gate_m[:, c].unsqueeze(1).broadcast_to([P, TT, 256]), ALU.mult).then_inc(g_free[i % 4], 1)
                v.drain()
                v.tensor_tensor(x[:, :, c], x[:, :, c], mt, ALU.add).then_inc(x1_done, 1)

            normed(1, xn2)
            modulated(AT["n2_0"], Af, mod[:, 24:32], whole=xTm)
            i = AT["rt"]
            piece(dve, i)
            dve.wait_ge(in_moe, 16 * 2)
            dve.wait_ge(in_route, 16 * 2)
            v.tensor_tensor(lg, G(i)[:, 0:TT * NE].rearrange("p (t e) -> p t e", t=TT),
                            brow.unsqueeze(1).broadcast_to([P, TT, NE]), ALU.add).then_inc(g_free[i % 4], 1)
            v.drain()
            v.tensor_reduce(negmax, lg, AX_X, ALU.max, negate=True).then_inc(r_lg, 1)
            dve.wait_ge(r_exp, TT)
            v.reciprocal(rrec, rsum)
            v.drain()
            for t in range(TT):
                o = v.tensor_scalar(prob[:, t, :], ex[:, t, :], rrec[:, t:t + 1], None, ALU.mult)
            o.then_inc(r_prob, 1)
            i = AT["pt"]
            piece(dve, i)
            v.tensor_copy(work[0:NE, :], G(i)[0:NE, 0:T]).then_inc(g_free[i % 4], 1)
            for _ in range(CAP // 8):
                v.drain()
                v.max(top8[0:NE, :], work[0:NE, :])
                v.drain()
                v.match_replace(work[0:NE, :], top8[0:NE, :], work[0:NE, :], -1.0)
            v.drain()
            v.tensor_scalar(mk[0:NE, :], work[0:NE, :], 0.0, None, ALU.is_lt).then_inc(r_sel, 1)
            i = AT["mk"]
            piece(dve, i)
            v.tensor_copy(maskn, G(i)[:, 0:TT * NE].rearrange("p (t e) -> p t e", t=TT)).then_inc(g_free[i % 4], 1)
            v.drain()
            i = AT["pos"]
            piece(dve, i)
            v.scalar_tensor_tensor(posm, maskn, -1000.0, G(i)[:, 0:TT * NE].rearrange("p (t e) -> p t e", t=TT),
                                   ALU.mult, ALU.add).then_inc(g_free[i % 4], 1)
            v.drain()
            v.tensor_scalar(posm, posm, 1000.0, None, ALU.add)
            v.drain()
            for t in range(TT):
                s3 = sel[:, t, :].rearrange("p (e c) -> p e c", e=NE)
                v.tensor_tensor(s3, slot_id, posm[:, t, :].unsqueeze(2).broadcast_to([P, NE, CAP]), ALU.is_equal)
            v.drain()
            for t in range(TT):
                s3 = sel[:, t, :].rearrange("p (e c) -> p e c", e=NE)
                w3 = selw[:, t, :].rearrange("p (e c) -> p e c", e=NE)
                o = v.tensor_tensor(w3, s3, prob[:, t, :].unsqueeze(2).broadcast_to([P, NE, CAP]), ALU.mult)
            o.then_inc(r_sel, 1)
            v.drain()
            dve.wait_ge(e_acc, 1)
            with dve.Fori(0, NE) as e:
                for t in range(TT):
                    o = v.tensor_copy(rep[:, t, :, :],
                                      selw[:, t, bass.ds(e * CAP, CAP)].unsqueeze(1).broadcast_to([P, 4, CAP]))
                o.then_inc(e_rep, 1)
                dve.wait_ge(e_gath, e + 1)
                v.tensor_copy(xeT.rearrange("p k c -> p (k c)"), psum[:, 3, 0:KT * CAP]).then_inc(e_xe, 1)
                dve.wait_ge(e_selTp, e + 1)
                v.tensor_copy(selT, psum[:, 2, 0:T]).then_inc(e_selT, 1)
                dve.wait_ge(e_sil, e + 1)
                dve.wait_ge(e_unit, e * UPE + 8)
                v.tensor_tensor(gu, sil, psum[:, 1, :], ALU.mult).then_inc(e_gu, 1)
                dve.wait_ge(e_sc, e + 1)
                for t in range(TT):
                    a3 = acc[:, t, :].rearrange("p (j n) -> p j n", j=4)
                    o = v.tensor_tensor(a3, psum[:, 4:8, t * T:t * T + T], a3, ALU.add)
                o.then_inc(e_acc, 1)
                v.drain()
            v.tensor_tensor(acc, acc, gate_f.unsqueeze(1).broadcast_to([P, TT, D]), ALU.mult)
            v.drain()
            v.tensor_tensor(x, x, acc, ALU.add).then_inc(x2_done, 1)
            dve.wait_ge(n_rstd, 3)
            for t in range(TT):
                o = v.scalar_tensor_tensor(x[:, t, :], x[:, t, :], rstd[:, t:t + 1], gbc, ALU.mult, ALU.mult)
            o.then_inc(x3_done, 1)

            normed(3, xn3)
            low = Low(dve, 1)
            low.ahead(-1)
            v.drain()
            modulated(AT["n3_0"], vec2[:, 0:8], None)
            for c in ("qa0", "qa1", "kc"):
                low.ahead(C2AT[c])

            def doubled(name, d):
                i = AT[name]
                piece(dve, i)
                for g in range(2):
                    for hf in range(2):
                        o = v.tensor_copy(d[HD * hf:HD * hf + HD, g, :], G(i)[HD * g:HD * g + HD, 0:T])
                o.then_inc(g_free[i % 4], 1)

            i = AT["kc"]
            piece(dve, i)
            for c in range(2):
                for g in range(2):
                    v.tensor_copy(k2[0:HD, c, g, :], G(i)[HD * g:HD * g + HD, c * T:c * T + T])
                    o = v.tensor_copy(k2[HD:P, c, g, 0:T - 1], G(i)[HD * g:HD * g + HD, c * T + 1:c * T + T])
            o.then_inc(g_free[i % 4], 1)
            v.drain()
            for c in range(2):
                for g in range(2):
                    for u in range(2):
                        src = k2[:, c, g, 16 * u:16 * u + 16 * NCMP].rearrange("p (n r o) -> p r n o", r=8, o=2)[:, :, :, 0]
                        d = kb2[:, c, 8 * u:8 * u + 8, g * NCMP:g * NCMP + NCMP]
                        pe_ = vec2[:, 46 + 16 * c + 8 * u:54 + 16 * c + 8 * u].unsqueeze(2).broadcast_to([P, 8, NCMP])
                        o = v.tensor_tensor(d, src, pe_, ALU.add)
            o.then_inc(kb_done, 1)
            doubled("ks", ksT)
            low.ahead(C2AT["ksvs"])
            doubled("kw", kwT)
            low.ahead(C2AT["kwvw"])
            low.ahead(C2AT["gnsa"])
            taken(dve, AT["gnsa"])
            for t in range(TT):
                o = v.tensor_scalar(gn[:, t, 0:8], gn[:, t, 0:8], K("cmpvalid")[:, t:t + 1], None, ALU.mult)
            v.drain()

            def least(j, J, s_, x_, m_, base=0, sbuf=sbuf):
                b = j % 2
                nk = sum(J["widths"])
                dve.wait_ge(s_, base + (j + 1))
                if j >= 2:
                    dve.wait_ge(x_, base + (j - 1))
                if "dist" in J:
                    v.scalar_tensor_tensor(sbuf[:, b, 0:nk], J["dist"], J["slope"], psum[:, 4 + b, 0:nk],
                                           ALU.mult, ALU.add)
                    v.drain()
                    v.tensor_reduce(jmin[:, b:b + 1], sbuf[:, b, 0:nk], AX_X, ALU.min).then_inc(m_, 1)
                elif J["bias"] is None:
                    v.tensor_copy(sbuf[:, b, 0:nk], psum[:, 4 + b, 0:nk])
                    v.tensor_reduce(jmin[:, b:b + 1], psum[:, 4 + b, 0:nk], AX_X, ALU.min).then_inc(m_, 1)
                else:
                    v.memset(spare[:, j:j + 1], 0.0)
                    v.tensor_tensor_reduce(sbuf[:, b, 0:nk], psum[:, 4 + b, 0:nk], J["bias"], 1.0, 3e38,
                                           ALU.add, ALU.min, jmin[:, b:b + 1]).then_inc(m_, 1)

            def finish(j, J, x_, o_, d_, base=0):
                b = j % 2
                dve.wait_ge(x_, base + (j + 1))
                v.reciprocal(jrec[:, b:b + 1], jsum[:, b:b + 1])
                v.drain()
                if J["coef"] is not None:
                    v.tensor_tensor(jrec[:, b:b + 1], jrec[:, b:b + 1], J["coef"], ALU.mult)
                    v.drain()
                dve.wait_ge(o_, base + (j + 1))
                if J["first"]:
                    v.tensor_scalar(J["out"], psum[:, 7, 0:HD], jrec[:, b:b + 1], None, ALU.mult).then_inc(d_, 1)
                else:
                    v.scalar_tensor_tensor(J["out"], psum[:, 7, 0:HD], jrec[:, b:b + 1], J["out"],
                                           ALU.mult, ALU.add).then_inc(d_, 1)

            for kind, n in PLAN2:
                if kind == "job":
                    least(n, job2(n), j_s, j_exp, j_min)
                    if n >= 2:
                        finish(n - 2, job2(n - 2), j_exp, j_o, j_done)
                else:
                    low.ahead(C2AT[n])
            for j in (NJ2 - 2, NJ2 - 1):
                finish(j, job2(j), j_exp, j_o, j_done)
            v.drain()
            taken(dve, *[AT[m] for m in ("za0", "za1", "zb0", "zb1")])
            v.tensor_tensor(oA, oA, zA, ALU.mult)
            v.tensor_tensor(oB, oB, zB, ALU.mult).then_inc(y_done, 1)
            for h in range(4):
                i = AT[f"yt{h}"]
                piece(dve, i)
                parts(pair(G(i)), (yR[:, 0], yR[:, 1]), slice(2 * h, 2 * h + 2)).then_inc(g_free[i % 4], 1)
            for q in range(2):
                for nm, gate in (("wa", mAT), ("wb", mBT)):
                    for h in (2 * q, 2 * q + 1):
                        i = AT[f"{nm}{h}"]
                        low.ahead(C2AT[f"{nm}{h}"])
                        piece(dve, i)
                        taken(dve, AT[("mA" if nm == "wa" else "mB") + str(h)])
                        g = gate[:, 2 * h:2 * h + 2, :]
                        v.tensor_tensor(g, pair(G(i)), g, ALU.mult).then_inc(g_free[i % 4], 1)
                        if nm == "wb":
                            v.drain()
                            m = mAT[:, 2 * h:2 * h + 2, :]
                            v.tensor_tensor(temp(h), m, g, ALU.add)
                            v.drain()
                            parts(temp(h), xs, slice(2 * h, 2 * h + 2)).then_inc(m_done, 1)
            for h in range(4):
                low.ahead(C2AT[f"wo2_{h}"])
            dve.wait_ge(in_post, 16)
            dve.wait_ge(n_rstd, 5)
            for t in range(TT):
                v.scalar_tensor_tensor(mixn[:, t, :], mixn[:, t, :], rstd[:, t:t + 1], gbc, ALU.mult, ALU.mult)
            v.drain()
            v.tensor_tensor(x, x, mixn, ALU.add).then_inc(x4_done, 1)

            cos = K("cos").rearrange("p (t n) -> p t n", t=TT)
            sin = K("sin").rearrange("p (t n) -> p t n", t=TT)
            with dve.Fori(0, LAYERS) as l:
                v.drain()
                v.tensor_copy(Am, vec2[:, bass.ds(l * KT + 8, KT)])
                v.tensor_copy(Af, vec2[:, bass.ds(l * KT + 24, KT)])
                v.tensor_copy(Bm[:, 0:2], vec2[:, bass.ds(l * 2 + 40, 2)])
                v.tensor_copy(Bm[:, 2:3], vec2[:, bass.ds(l + 44, 1)])
                v.tensor_copy(subl, subg.rearrange("p l n -> p (l n)")[:, bass.ds(l * HD, HD)])

                def normed3(need):
                    dve.wait_ge(n3_rstd, need)
                    for t in range(TT):
                        o = v.tensor_scalar(mix[:, t, :], x[:, t, :], rstd[:, t:t + 1], None, ALU.mult)
                    o.then_inc(n3_xn, 1)

                normed3(l * 2 + 1)
                low = Low(dve, 2, l)
                low.ahead(-1)
                dve.wait_ge(in_na, l * (16 * 16) + 16 * 16)
                for h in range(4):
                    for t in range(TT):
                        o = v.scalar_tensor_tensor(nab[:, h, t, :], nab[:, h, t, :], -1.0, K("nawin"), ALU.mult, ALU.add)
                o.then_inc(nab_done, 1)
                modulated(LAT["n4_0"], Am, None, l)
                for kind, n in PLAN3:
                    if kind == "job":
                        if n == 8:
                            dve.wait_ge(in_t5, 16 * 16)
                        least(n, job3(n, l), k_s, k_exp, k_min, l * NJ3, sbuf3)
                        if n >= 2:
                            finish(n - 2, job3(n - 2, l), k_exp, k_o, k_done, l * NJ3)
                        continue
                    c = "ckvkr" if n == "kr" else n
                    if c in C3AT:
                        low.ahead(C3AT[c])
                    if n == "kr":
                        dve.wait_ge(h_rstd, l + 1)
                        taken(dve, LAT["cq"], LAT["ckv"], l=l)
                        for t in range(TT):
                            v.tensor_scalar(cqn[:, t, :], cqn[:, t, :], hrstd[:, t:t + 1], None, ALU.mult)
                            o = v.tensor_scalar(ckvn[:, t, :], ckvn[:, t, :], hrstd[:, 2 + t:3 + t], None, ALU.mult)
                        o.then_inc(lat_n, 1)
                    elif n in ("cqT", "ckvT"):
                        i = LAT[n]
                        piece(dve, i, l)
                        if n == "cqT":
                            for m in range(2):
                                o = v.tensor_scalar(cqT[:, m, :], G(i)[:, m * T:m * T + T], Bm[:, m:m + 1], None, ALU.mult)
                        else:
                            o = v.tensor_scalar(ckvT[:, 0, :], G(i)[:, 0:T], Bm[:, 2:3], None, ALU.mult)
                        o.then_inc(g3_free[i % 4], 1)
                    elif n == "uq1":
                        taken(dve, LAT["uq0"], LAT["uq1"], l=l)
                        x1, x2 = qdn[:, :, :, 64:80], qdn[:, :, :, 80:96]
                        cb = cos.unsqueeze(2).broadcast_to([P, TT, 4, 16])
                        sb_ = sin.unsqueeze(2).broadcast_to([P, TT, 4, 16])
                        for c, (u, f) in enumerate(((x1, cb), (x2, sb_), (x1, sb_), (x2, cb))):
                            v.tensor_tensor(rp[:, c, :, :, :], u, f, ALU.mult)
                        v.drain()
                        v.tensor_tensor(x1, rp[:, 0, :, :, :], rp[:, 1, :, :, :], ALU.subtract)
                        v.tensor_tensor(x2, rp[:, 2, :, :, :], rp[:, 3, :, :, :], ALU.add).then_inc(rope_q, 1)
                    elif n == "ukv1":
                        taken(dve, LAT["kr"], LAT["ukv0"], LAT["ukv1"], l=l)
                        x1, x2 = krn[:, :, 0:16], krn[:, :, 16:32]
                        for c, (u, f) in enumerate(((x1, cos), (x2, sin), (x1, sin), (x2, cos))):
                            v.tensor_tensor(rk[:, c, :, :], u, f, ALU.mult)
                        v.drain()
                        wide = [rk[:, c, :, :].unsqueeze(2).broadcast_to([P, TT, 4, 16]) for c in range(4)]
                        v.tensor_tensor(kcat[:, :, :, 64:80], wide[0], wide[1], ALU.subtract)
                        v.tensor_tensor(kcat[:, :, :, 80:96], wide[2], wide[3], ALU.add).then_inc(rope_k, 1)
                for j in (NJ3 - 2, NJ3 - 1):
                    finish(j, job3(j, l), k_exp, k_o, k_done, l * NJ3)
                v.drain()
                mb = mix[:, :, 256:512].rearrange("p t (h n) -> p t h n", h=4)
                v.tensor_tensor(hsq, mb, mb, ALU.mult)
                v.drain()
                v.tensor_reduce(hstat[:, 0:8], hsq.rearrange("p t h n -> p (t h) n"), AX_X, ALU.add).then_inc(d_sq, 1)
                dve.wait_ge(d_rstd, l + 1)
                hr = hrstd.rearrange("p (t h) -> p t h", t=TT).unsqueeze(3).broadcast_to([P, TT, 4, HD])
                v.tensor_tensor(mb, mb, hr, ALU.mult)
                v.drain()
                for t in range(TT):
                    o = v.tensor_tensor(mb[:, t, :, :], mb[:, t, :, :], subl.unsqueeze(1).broadcast_to([P, 4, HD]), ALU.mult)
                o.then_inc(mix_done, 1)
                for h in range(4):
                    i = LAT[f"mix{h}"]
                    piece(dve, i, l)
                    parts(pair(G(i)), (mixR[:, 0], mixR[:, 1]), slice(2 * h, 2 * h + 2)).then_inc(g3_free[i % 4], 1)
                for h in range(4):
                    i = LAT[f"wo3_{h}"]
                    low.ahead(C3AT[f"wo3_{h}"])
                    piece(dve, i, l)
                    c = slice(256 * h, 256 * h + 256)
                    v.tensor_tensor(x[:, :, c], G(i).rearrange("p (t n) -> p t n", t=TT), x[:, :, c],
                                    ALU.add).then_inc(g3_free[i % 4], 1)
                    v.drain().then_inc(xm_done, 1)
                normed3(l * 2 + 2)
                modulated(LAT["n5_0"], Af, None, l)
                for i in range(11):
                    n = LAT[f"gu{2 * i + 1}"]
                    low.ahead(C3AT[f"gu{2 * i}"])
                    low.ahead(C3AT[f"gu{2 * i + 1}"])
                    piece(dve, n, l)
                    taken(dve, LAT[f"gu{2 * i}"], l=l)
                    v.tensor_tensor(temp(i), pair(G(n)), pair(silu[i % 2]), ALU.mult).then_inc(g3_free[n % 4], 1)
                    v.drain()
                    parts(temp(i), (actR[:, 0], actR[:, 1]), slice(2 * i, 2 * i + 2)).then_inc(act_done, 1)
                for c in range(FT // 2):
                    low.ahead(C3AT[f"dn{c}"])
                for q in range(4):
                    i = LAT[f"down{q}"]
                    piece(dve, i, l)
                    xs = x[:, q // 2, 512 * (q % 2):512 * (q % 2) + 512]
                    v.tensor_tensor(xs, G(i), xs, ALU.add).then_inc(g3_free[i % 4], 1)
                v.drain().then_inc(x4_done, 1)
            dve.wait_ge(in_fin, 16)
            dve.wait_ge(n3_rstd, LAYERS * 2 + 1)
            for t in range(TT):
                v.scalar_tensor_tensor(x[:, t, :], x[:, t, :], rstd[:, t:t + 1], gbc, ALU.mult, ALU.mult).then_inc(y_out, 1)

    return nc


INPUTS = ["x", "c", "w_ada", "b_ada", "g_norm_mix", "w_in", "b_gate", "w_fourier", "w_conv", "w_conv_out", "w_o",
          "g_norm_moe", "w_router", "b_router", "w_gate_e", "w_up_e", "w_down_e", "g_final", "norm_pre_2", "w_in_2",
          "cmp_pe_k_2", "cmp_w1_k_2", "cmp_w2_k_2", "cmp_pe_v_2", "cmp_w1_v_2", "cmp_w2_v_2", "w_branch_a_2",
          "w_branch_b_2", "w_o_2", "norm_post_2", "attn_norm_3", "w_in_3", "na_rpb_3", "diff_lambda_3",
          "diff_subln_3", "mla_q_norm_3", "w_uq_3", "mla_kv_norm_3", "w_ukv_3", "t5_table_3", "w_o_3", "ffn_norm_3",
          "w_gate_3", "w_up_3", "w_down_3", "final_norm_3"]


def kernel(**inputs):
    import concourse.bacc as bacc
    from concourse.bass_utils import run_bass_kernel_spmd

    nc = bacc.Bacc("TRN2", target_bir_lowering=False, num_devices=1)
    kept, cst_at, dft, moe, rel = build_constants()
    arrays = {n: np.ascontiguousarray(inputs[n]) for n in INPUTS}
    arrays.update(c_kept=kept, c_dft=dft, c_moe=moe, c_rel=rel)
    handles = {n: nc.dram_tensor("in_" + n, v.shape, mybir.dt.from_np(v.dtype), kind="ExternalInput").ap()
               for n, v in arrays.items()}
    out = nc.dram_tensor("out", (1, T, D), F32, kind="ExternalOutput").ap()
    program(nc, handles, cst_at, out)
    r = run_bass_kernel_spmd(nc, [{"in_" + n: v for n, v in arrays.items()}], core_ids=[0])
    return r.results[0]["out"]
```

```python
import math
from contextlib import ExitStack

import numpy as np

import concourse.bass as bass
from concourse import mybir

ALU = mybir.AluOpType
ACT = mybir.ActivationFunctionType
AX_X = mybir.AxisListType.X
F32 = mybir.dt.float32
F32R = mybir.dt.float32r

P = 128
T = 256
TT = T // P
D = 1024
KT = D // P
EPS = 1e-6
NE = 16
CAP = 2 * T // NE
FE = 2048
SLOT = 4096
RING = 5
RINGM = 6
BIG = 1e30
NHEAD = 16
HD = 64
NCMP = (T - 32) // 16 + 1
DFF = ((8 * D + 3 * 256 - 1) // (3 * 256)) * 256
FT = DFF // P
LAYERS = 2
ARENA = 19728
GATE_UNITS = (4, 5, 10, 11)
NDIL = ((128, 1), (512, 4), (2048, 16))
GRID_W, NA_ROWS, NA_COLS = 64, 8, 16
NA_SPAN = T // GRID_W
REL = 2 * T
NAREL = 2 * GRID_W


def t5_bucket(rel):
    nb, exact = 16, 8
    side = np.where(rel > 0, nb, 0)
    n = np.abs(rel)
    q = np.maximum(n, 1).astype(np.float32) / np.float32(exact)
    large = exact + (np.log(q) / np.float32(math.log(1024 / exact)) * np.float32(nb - exact)).astype(np.int32)
    return side + np.where(n < exact, n, np.minimum(large, nb - 1))


def build_constants():
    c = {}
    tok = np.arange(T)
    c["ident"] = np.eye(P)
    c["ones"] = np.ones((P, P))
    q, k = tok[:, None], tok[None, :]
    causal = np.where(q >= k, (q - k).astype(np.float64), BIG)
    c["dist"] = np.concatenate([causal[:P, :P], causal[P:, :]], axis=1)
    end = np.arange(16) * 16 + 31
    dc = np.where((q >= end[None, :]) & (np.arange(16)[None, :] < NCMP), (q - end[None, :]).astype(np.float64), BIG)
    c["cmpdist"] = dc.reshape(TT, P, 16).transpose(1, 0, 2).reshape(P, 32)
    c["cmpvalid"] = (tok >= 31).astype(np.float64).reshape(TT, P).T
    col = np.arange(GRID_W)
    start = np.clip(col - NA_COLS // 2, 0, GRID_W - NA_COLS)
    out = ~((col[None, :] >= start[:, None]) & (col[None, :] < start[:, None] + NA_COLS))
    c["nawin"] = np.tile(np.where(out, BIG, 0.0), (2, NA_SPAN))
    half = 16
    freq = np.float32(10000.0) ** (-np.arange(half, dtype=np.float32) / np.float32(half))
    ang = (tok.astype(np.float32)[:, None] * freq[None, :]).astype(np.float32)
    for n, f in (("cos", np.cos), ("sin", np.sin)):
        c[n] = f(ang.astype(np.float64)).reshape(TT, P, half).transpose(1, 0, 2).reshape(P, TT * half)
    rel = np.arange(REL) - (T - 1)
    hot = np.zeros((P, REL))
    hot[t5_bucket(rel), np.arange(REL)] = 1.0
    mult = sum(((np.abs(rel) <= w // 2) & (rel % d == 0)).astype(np.int64) for w, d in NDIL)
    add = np.zeros((P, REL))
    add[4:8] = np.where(mult > 0, -np.log(np.maximum(mult, 1)), BIG)
    names = list(c)
    kept = np.concatenate([c[n] for n in names], axis=1).astype(np.float32)
    at, pos = {}, 0
    for n in names:
        at[n] = (pos, c[n].shape[1])
        pos += c[n].shape[1]
    a = 2 * np.pi * (np.outer(tok, tok) % T) / T
    s = 1.0 / math.sqrt(T * P)
    dft_s = np.concatenate([np.cos(a) * s, np.sin(a) * s], axis=1).reshape(TT, P, 2 * T).transpose(1, 0, 2)
    b = 2 * np.pi * (np.outer(np.arange(P), np.arange(P)) % P) / P
    dft = np.concatenate([dft_s.reshape(P, TT * 2 * T), np.cos(b), -np.sin(b)], axis=1).astype(np.float32)
    tri = (tok[:, None] < tok[None, :]).astype(np.float32).reshape(TT, P, T).transpose(1, 0, 2).reshape(P, TT * T)
    slots = np.tile(np.arange(CAP), (P, NE)).astype(np.float32)
    return kept, at, dft, np.concatenate([tri, slots], axis=1).astype(np.float32), \
        np.concatenate([hot, add], axis=1).astype(np.float32)


def slope(i):
    return float(np.float32(2.0 ** (-8.0 * (i + 1) / NHEAD)))


def names(prefix, n):
    return [f"{prefix}{i}" for i in range(n)]


PIECES = (names("ada", 12) + names("n1_", 4) + names("uf", 2) + names("dfta", 4) + names("dftb", 2)
          + names("v", 4) + names("b", 4) + names("c", 4) + names("ga", 4) + names("gb", 4)
          + names("wf", 4) + names("wc", 4) + names("wo", 4) + names("n2_", 4)
          + ["rt"] + names("h2n", 4) + ["pt", "mk", "pos"]
          + names("n3_", 4) + names("qa", 2) + ["kc", "ks", "vs", "kw", "vw", "gnsa", "za0", "hk", "za1", "kcT", "vcn"]
          + names("qb", 2) + names("kb", 2) + names("vb", 2) + names("zb", 2)
          + names("mA", 4) + names("mB", 4) + names("yt", 4)
          + ["wa0", "wa1", "wb0", "wb1", "wa2", "wa3", "wb2", "wb3"] + names("wo2_", 4))
AT = {n: i for i, n in enumerate(PIECES)}
LP = (names("n4_", 4) + ["qa0", "ka0", "va0", "qb0", "kb0", "vb0", "vc0", "cq", "ckv", "kr", "qc0", "kc0", "cqT", "ckvT"]
      + names("uq", 2) + names("ukv", 2) + names("qm", 2) + names("km", 2) + names("mix", 4) + names("wo3_", 4)
      + names("n5_", 4) + names("gu", 22) + names("down", 4))
assert len(AT) == len(PIECES) 
LAT = {n: i for i, n in enumerate(LP)}
LPN = len(LP)
assert LPN % 4 == 0

UNITS = (names("ada", 12) + names("win", 11) + names("wf", 2) + names("wc", 2) + names("wo", 2))
N_MOE = len(UNITS)
UPE = 12
UNITS2 = ["qa", "kv", "kvwg", "w1", "za", "qb", "kb", "vb", "zb"] + names("mg", 4) + names("ab", 2) + names("wo2_", 2)
UAT = {n: i for i, n in enumerate(UNITS)}
U2AT = {n: i for i, n in enumerate(UNITS2)}
L3 = names("win", 6) + names("wo", 2) + names("gu", 11) + names("dn", 6)
L3AT = {n: i for i, n in enumerate(L3)}
assert len(L3) % RING == 0

JOBS3 = ([("na", h, 0, t) for h in range(4) for t in range(TT)]
         + [("diff", h, c, t) for h in range(4) for t in range(TT) for c in range(2)]
         + [("dil", h, 0, t) for h in range(4) for t in range(TT)]
         + [("mla", h, 0, t) for h in range(4) for t in range(TT)])
NJ3 = len(JOBS3)
NMLA = 4 * TT
_first = ["qa0", "ka0", "va0"]
_rest = ["qb0", "kb0", "vb0", "vc0", "cq", "ckv", "kr", "qc0", "kc0", "cqT", "ckvT", "uq0", "uq1", "ukv0", "ukv1", "qm0", "qm1", "km0", "km1"]
PLAN3 = [("piece", n) for n in _first]
for _i, _n in enumerate(_rest):
    PLAN3.append(("piece", _n))
    PLAN3 += [("job", j) for j in range((NJ3 - NMLA) * _i // len(_rest), (NJ3 - NMLA) * (_i + 1) // len(_rest))]
PLAN3 += [("job", j) for j in range(NJ3 - NMLA, NJ3)]
PARTS3 = {L3AT["win4"]: 3}
PARTS3.update({L3AT[f"gu{i}"]: 2 for i in range(11)})
LAST3 = {L3AT[u]: LAT[p] for u, p in (("win0", "ka0"), ("win1", "qb0"), ("win2", "vb0"), ("win3", "cq"),
                                      ("win4", "ukv1"), ("win5", "kc0"), ("wo0", "wo3_1"), ("wo1", "wo3_3"),
                                      ("dn5", "down3"))}
LAST3.update({L3AT[f"gu{i}"]: LAT[f"gu{2 * i + 1}"] for i in range(11)})
LAM_INIT = [0.8 - 0.6 * math.exp(-0.3 * l) for l in range(LAYERS)]
LAST = {UAT[f"ada{i}"]: AT[f"ada{i}"] for i in range(12)}
LAST[UAT["win0"]] = AT["uf1"]
for _i in range(10):
    LAST[UAT[f"win{_i + 1}"]] = AT[("v", "b", "c", "ga", "gb")[_i // 2] + str(2 * (_i % 2) + 1)]
for _n in ("wf", "wc", "wo"):
    for _i in range(2):
        LAST[UAT[f"{_n}{_i}"]] = AT[f"{_n}{2 * _i + 1}"]
LAST2 = ({U2AT[u]: AT[p] for u, p in (("qa", "qa1"), ("kv", "vs"), ("kvwg", "vcn"), ("w1", "hk"), ("za", "za1"),
                                         ("qb", "qb1"), ("kb", "kb1"), ("vb", "vb1"), ("zb", "zb1"),
                                         ("mg0", "mA1"), ("mg1", "mA3"), ("mg2", "mB1"), ("mg3", "mB3"),
                                         ("ab0", "wb1"), ("ab1", "wb3"), ("wo2_0", "wo2_1"), ("wo2_1", "wo2_3"))})

CH1 = [(f"uf{h}", UAT["win0"], KT, 512, 256 * h, 256, 0, f"uf{h}") for h in range(2)]
for _b, _n in enumerate(("v", "b", "c", "ga", "gb")):
    CH1 += [(f"{_n}{h}", UAT["win1"] + 2 * _b + h // 2, KT, 512, 256 * (h % 2), 256, 0, f"{_n}{h}") for h in range(4)]
for _n, _k in (("wf", 4), ("wc", KT), ("wo", KT)):
    CH1 += [(f"{_n}{h}", UAT[f"{_n}{h // 2}"], _k, 512, 256 * (h % 2), 256, 0, f"{_n}{h}") for h in range(4)]
CH2 = [(f"qa{h}", U2AT["qa"], KT, 512, 256 * h, 256, 0, f"qa{h}") for h in range(2)]
CH2 += [("kc", U2AT["kv"], KT, 512, 0, 256, 0, "kc"), ("ksvs", U2AT["kv"], KT, 512, 256, 256, 0, "vs"),
        ("kwvw", U2AT["kvwg"], KT, 280, 0, 256, 0, "vw"), ("gnsa", U2AT["kvwg"], KT, 280, 256, 24, 0, "gnsa")]
CH2 += [(f"{n}{h}", U2AT[n], KT, 512, 256 * h, 256, 0, f"{n}{h}") for n in ("za", "qb", "kb", "vb", "zb") for h in range(2)]
CH2 += [(f"m{b}{h}", U2AT[f"mg{2 * (b == 'B') + h // 2}"], KT, 512, 256 * (h % 2), 256, 0, f"m{b}{h}")
        for b in "AB" for h in range(4)]
CH2 += [(f"w{b}{2 * q + m}", U2AT[f"ab{q}"], 4, 512, 256 * m, 256, 2048 * (b == "b"), f"w{b}{2 * q + m}")
        for q in range(2) for b in "ab" for m in range(2)]
CH2 += [(f"wo2_{h}", U2AT[f"wo2_{h // 2}"], KT, 512, 256 * (h % 2), 256, 0, f"wo2_{h}") for h in range(4)]
CH3 = [(n, i // 2, KT, 512, 256 * (i % 2), 256, 0, n)
       for i, n in enumerate(("qa0", "ka0", "va0", "qb0", "kb0", "vb0", "vc0", "cq"))]
CH3 += [("ckvkr", 4, KT, 160, 0, 160, 0, "kr")]
CH3 += [(n, 5, KT, 512, 256 * i, 256, 0, n) for i, n in enumerate(("qc0", "kc0"))]
CH3 += [(f"wo3_{h}", L3AT[f"wo{h // 2}"], KT, 512, 256 * (h % 2), 256, 0, f"wo3_{h}") for h in range(4)]
CH3 += [(f"gu{i}", L3AT[f"gu{i // 2}"], KT, 512, 256 * (i % 2), 256, 0, f"gu{i}") for i in range(22)]
CH3 += [(f"dn{i}", L3AT[f"dn{i // 2}"], 2, D, 0, D, 2 * D * (i % 2), f"dn{i}") for i in range(11)]
assert len(CH3) % 2 == 0
C1AT, C2AT, C3AT = ({c[0]: i for i, c in enumerate(ch)} for ch in (CH1, CH2, CH3))

NSA_JOBS = [(br, h, t) for h in range(8) for br in ("cmp", "slc", "win") for t in range(TT)]
MOBA_JOBS = [("moba", h, t) for h in range(8) for t in range(TT)]
JOBS2 = NSA_JOBS + MOBA_JOBS
_tail = (names("qb", 2) + names("kb", 2) + names("vb", 2) + names("zb", 2) + names("mA", 4)
         + names("mB", 4))
PLAN2 = []
NJ2 = len(JOBS2)
for _i, _n in enumerate(_tail):
    PLAN2.append(("piece", _n))
    PLAN2 += [("job", j) for j in range(len(JOBS2) * _i // len(_tail), len(JOBS2) * (_i + 1) // len(_tail))]


def with_splits(plan, chunks):
    last = {c[7]: i for i, c in enumerate(chunks)}
    own = [n for kind, n in plan if kind == "piece" and n in last]
    full = []
    for kind, n in plan:
        if kind == "piece" and n in own[1:]:
            full += [("split", (last[n] + 1, i)) for i in range(2)]
        if (kind, n) == ("piece", "cqT"):
            full += [("split", (last[own[-1]] + 2, i)) for i in range(2)]
        full.append((kind, n))
    return full


PLAN2 = with_splits(PLAN2, CH2)
PLAN3 = with_splits(PLAN3, CH3)


def program(nc, a, cst_at, out):
    with ExitStack() as ctx:
        def sb(name, cols, parts=P):
            return ctx.enter_context(nc.sbuf_tensor(name, [parts, cols], F32))[:, :]

        def sem(name):
            return ctx.enter_context(nc.semaphore(name))

        def dram(name, shape):
            return nc.dram_tensor(name, shape, F32, kind="Internal").ap()

        def twice(name, cols):
            with nc.sbuf_tensor(name, [P, cols], F32) as t:
                t = t[:, :]
            return t, ctx.enter_context(nc.sbuf_tensor(name + "_r", [P, cols], F32R))[:, :]

        ring, ring_r = twice("ring", RINGM * SLOT)
        x = sb("x", TT * D).rearrange("p (t d) -> p t d", t=TT)
        xR = ctx.enter_context(nc.sbuf_tensor("xR", [P, 2 * KT * T], F32R))[:, :].rearrange("p (c k t) -> p c k t", c=2, k=KT)
        cst = sb("cst", a["c_kept"].shape[1])
        vec1 = sb("vec1", 112)
        vec2 = sb("vec2", 78)
        stat = sb("stat", 512)
        mt2 = sb("mt2", 2 * 512)
        arena, arena_r = twice("arena", ARENA)
        psum = ctx.enter_context(nc.psum_tensor("psum", [P, 8, 512], F32))[:, :, :]

        def K(name):
            o, n = cst_at[name]
            return cst[:, o:o + n]

        def R(at, kt, c=2):
            return arena_r[:, at:at + c * kt * T].rearrange("p (c k t) -> p c k t", c=c, k=kt)

        ident, ones = K("ident"), K("ones")

        class Place:

            def __init__(self, at):
                self.at = at

            def __call__(self, n):
                self.at += n
                assert self.at <= ARENA, self.at
                return arena[:, self.at - n:self.at]

        pl = Place(0)
        gate_m, gate_f, gbc = pl(D), pl(D), pl(D)
        tri = pl(TT * T).rearrange("p (k t) -> p k t", k=TT)
        slot_id = pl(NE * CAP).rearrange("p (e c) -> p e c", e=NE)
        base1 = pl.at
        uf = pl(TT * 512).rearrange("p (t n) -> p t n", t=TT)
        part = uf
        v_at = pl.at
        vT = pl(KT * T).rearrange("p (k t) -> p k t", k=KT)
        cv = pl(KT * (T + 2)).rearrange("p (k t) -> p k t", k=KT)
        b_at = pl.at
        bT = pl(KT * T).rearrange("p (k t) -> p k t", k=KT)
        convH, convL = R(v_at, KT, 1)[:, 0], R(b_at, KT, 1)[:, 0]
        ga_at = pl.at
        gaT = pl(KT * T).rearrange("p (k t) -> p k t", k=KT)
        gbT = pl(KT * T).rearrange("p (k t) -> p k t", k=KT)
        Bcs = gbT.rearrange("p (g h) t -> p g (h t)", g=4)
        fmR = R(pl.at, 4)
        pl(2 * 4 * T)
        dfts = pl(TT * 2 * T).rearrange("p (k n) -> p k n", k=TT)
        dftg = pl(2 * P).rearrange("p (c n) -> p c n", c=2)
        vrow = pl(2 * P).rearrange("p (c n) -> p c n", c=2)
        t5tab = pl(8)
        t5vec = pl(REL)
        narow = pl(NAREL)
        early = Place(ga_at)
        t5hot, diladd = early(REL), early(REL)
        csil = early(KT * 32).rearrange("p (k n) -> p k n", k=KT)
        lamraw = early(LAYERS * P).rearrange("p (l n) -> p l n", l=LAYERS)
        lamprod = early(LAYERS * 2 * 32).rearrange("p (l c n) -> p l c n", l=LAYERS, c=2)
        assert early.at <= ga_at + KT * T
        xn1 = vT.rearrange("p k t -> p (k t)").rearrange("p (t d) -> p t d", t=TT)
        mtmp = uf.rearrange("p t n -> p (t n)")

        pm = Place(base1)
        h2n = pm(TT * D).rearrange("p (t d) -> p t d", t=TT)
        xTm = pm(KT * T).rearrange("p (k t) -> p k t", k=KT)
        acc = pm(TT * D).rearrange("p (t d) -> p t d", t=TT)
        sel = pm(TT * NE * CAP).rearrange("p (t n) -> p t n", t=TT)
        selw = pm(TT * NE * CAP).rearrange("p (t n) -> p t n", t=TT)
        rep = pm(TT * P).rearrange("p (t j c) -> p t j c", t=TT, j=4)
        selT = pm(T)
        xeT = pm(KT * CAP).rearrange("p (k c) -> p k c", k=KT)
        hT = pm(4 * P).rearrange("p (s n) -> p s n", s=4)
        sil = pm(512)
        gu = pm(512)
        ysb = pm(T)
        wr = pm(KT * NE).rearrange("p (k e) -> p k e", k=KT)
        brow = pm(NE)
        lg = pm(TT * NE).rearrange("p (t e) -> p t e", t=TT)
        ex = pm(TT * NE).rearrange("p (t e) -> p t e", t=TT)
        prob = pm(TT * NE).rearrange("p (t e) -> p t e", t=TT)
        work = pm(T)
        mk = pm(T)
        top8 = pm(8)
        maskn = pm(TT * NE).rearrange("p (t e) -> p t e", t=TT)
        posm = pm(TT * NE).rearrange("p (t e) -> p t e", t=TT)
        xn2 = h2n

        p2 = Place(D)
        zA = p2(D).rearrange("p (t n) -> p t n", t=TT)
        p2.at = 3 * D
        qaT = p2(4 * T).rearrange("p (k t) -> p k t", k=4)
        ksT = p2(2 * T).rearrange("p (g t) -> p g t", g=2)
        kwT = p2(2 * T).rearrange("p (g t) -> p g t", g=2)
        yR = R(3 * D, KT)
        k2 = p2(2 * 2 * T).rearrange("p (c g t) -> p c g t", c=2, g=2)
        kb2 = p2(2 * 16 * 32).rearrange("p (c l n) -> p c l n", c=2, l=16)
        hk = p2(64).rearrange("p (c n) -> p c n", c=2)
        kcT = p2(32)
        vcn = p2(2 * HD).rearrange("p (g n) -> p g n", g=2)
        vs = p2(TT * P).rearrange("p (t n) -> p t n", t=TT)
        vw = p2(TT * P).rearrange("p (t n) -> p t n", t=TT)
        gn = p2(TT * 24).rearrange("p (t n) -> p t n", t=TT)
        qbT = p2(4 * T).rearrange("p (k t) -> p k t", k=4)
        kbT = p2(4 * T).rearrange("p (k t) -> p k t", k=4)
        vbn = p2(TT * 512).rearrange("p (t n) -> p t n", t=TT)
        zB = p2(TT * 512).rearrange("p (t n) -> p t n", t=TT)
        oA = p2(TT * 512).rearrange("p (t n) -> p t n", t=TT)
        oB = p2(TT * 512).rearrange("p (t n) -> p t n", t=TT)
        mAT = p2(KT * T).rearrange("p (k t) -> p k t", k=KT)
        mBT = p2(KT * T).rearrange("p (k t) -> p k t", k=KT)
        xn3 = mAT.rearrange("p k t -> p (k t)").rearrange("p (t d) -> p t d", t=TT)
        mixn = mBT.rearrange("p k t -> p (k t)").rearrange("p (t d) -> p t d", t=TT)
        yjunk = arena[:, 3 * D:5 * D].rearrange("p (t d) -> p t d", t=TT)
        pj = Place(p2.at)
        sbuf = pj(4 * T).rearrange("p (b n) -> p b n", b=4)
        pbuf = pj(2 * T).rearrange("p (b n) -> p b n", b=2)

        p3 = Place(0)
        nab = p3(8 * T).rearrange("p (h t n) -> p h t n", h=4, t=TT)
        p3.at = 3 * D
        qk = p3(12 * T).rearrange("p (k t) -> p k t", k=12)
        mixR = R(3 * D, KT)
        actR = R(3 * D, FT)
        v3 = p3(3 * TT * T).rearrange("p (c t n) -> p c t n", c=3, t=TT)
        cqn = p3(TT * 256).rearrange("p (t n) -> p t n", t=TT)
        ckvn = p3(TT * P).rearrange("p (t n) -> p t n", t=TT)
        krn = p3(TT * 32).rearrange("p (t n) -> p t n", t=TT)
        cqT = p3(2 * T).rearrange("p (k t) -> p k t", k=2)
        ckvT = p3(T).rearrange("p (k t) -> p k t", k=1)
        qdn = p3(TT * 4 * 96).rearrange("p (t h n) -> p t h n", t=TT, h=4)
        kcat = p3(TT * 4 * 96).rearrange("p (t h n) -> p t h n", t=TT, h=4)
        vd = p3(TT * T).rearrange("p (t n) -> p t n", t=TT)
        qmT, kmT = qk[:, 0:4, :], qk[:, 4:8, :]
        mix = p3(TT * D).rearrange("p (t d) -> p t d", t=TT)
        rp_ = mt2[:, 0:512]
        rp = rp_.rearrange("p (c t h n) -> p c t h n", c=4, t=TT, h=4)
        hsq = rp_.rearrange("p (t h n) -> p t h n", t=TT, h=4)
        rk = mt2[:, 512:512 + 4 * TT * 16].rearrange("p (c t n) -> p c t n", c=4, t=TT)
        pbuf3 = p3(2 * T).rearrange("p (b n) -> p b n", b=2)
        act_end = 3 * D + 2 * FT * T
        assert p3.at <= act_end
        p3.at = act_end
        t5b = p3(8 * TT * T).rearrange("p (h t n) -> p h t n", h=8, t=TT)
        pj.at = p3.at
        sbuf3 = pj(4 * T).rearrange("p (b n) -> p b n", b=4)

        silu = [sbuf3[:, 2 * b:2 * b + 2, :].rearrange("p b n -> p (b n)") for b in range(2)]

        def small(n, _p=[0]):
            _p[0] += n
            assert _p[0] <= 512
            return stat[:, _p[0] - n:_p[0]]

        neghalf = small(2)
        mod = small(48)
        Am, Bm, Af = small(8), small(8), small(8)
        ssq, rstd = small(2), small(2)
        rsum, rrec = small(2), small(2)
        negmax = small(2)
        jmin, jsum, jrec = small(4), small(4), small(4)
        lamneg = small(LAYERS)
        lamsum = small(4)
        lamexp = small(4)
        subg = small(LAYERS * HD).rearrange("p (l n) -> p l n", l=LAYERS)
        hstat = small(16)
        hrstd = small(8)
        halfs = small(8)
        subl = small(HD)
        spare = small(NJ3)

        t5_row = dram("t5_row", (8, REL))
        t5_rep = dram("t5_rep", (8, (P + 1) * REL))
        na_row = dram("na_row", (LAYERS * 4 * 7, NAREL))
        na_rep = dram("na_rep", (LAYERS * 4 * 7, GRID_W * NAREL))

        w_ready = [sem(f"w_ready{i}") for i in range(RING)]
        wm_ready = [sem(f"wm_ready{i}") for i in range(RINGM)]
        w2_ready = [sem(f"w2_ready{i}") for i in range(RING)]
        c_high = [sem(f"c_high{i}") for i in range(3)]
        c_low = [sem(f"c_low{i}") for i in range(3)]
        e_unit = sem("e_unit")
        w3_ready = [sem(f"w3_ready{i}") for i in range(RING)]
        g_ready = sem("g_ready")
        g_free = [sem(f"g_free{i}") for i in range(4)]
        in_x, in_cst, in_vec, in_b1 = sem("in_x"), sem("in_cst"), sem("in_vec"), sem("in_b1")
        in_moe, in_route = sem("in_moe"), sem("in_route")
        consts_set = sem("consts_set")
        n_sq, n_ms, n_rstd, n_xn = sem("n_sq"), sem("n_ms"), sem("n_rstd"), sem("n_xn")
        v_used = sem("v_used")
        v_cols = sem("v_cols")
        c_act = sem("c_act")
        mod_mm = sem("mod_mm")
        mod_done = sem("mod_done")
        conv_done = sem("conv_done")
        z_done = sem("z_done")
        x1_done = sem("x1_done")
        r_lg, r_exp, r_prob, r_sel = sem("r_lg"), sem("r_exp"), sem("r_prob"), sem("r_sel")
        e_rep, e_gath, e_xe, e_selTp, e_selT = (sem(n) for n in ("e_rep", "e_gath", "e_xe", "e_selTp", "e_selT"))
        e_sil, e_gu, e_hTp, e_hT = (sem(n) for n in ("e_sil", "e_gu", "e_hTp", "e_hT"))
        e_y, e_sc, e_acc = (sem(n) for n in ("e_y", "e_sc", "e_acc"))
        x2_done, x3_done = sem("x2_done"), sem("x3_done")
        g3_ready = sem("g3_ready")
        g3_free = [sem(f"g3_free{i}") for i in range(4)]
        w3_dn = sem("w3_dn")
        n3_sq, n3_ms, n3_rstd, n3_xn = (sem(n) for n in ("n3_sq", "n3_ms", "n3_rstd", "n3_xn"))
        h_sq, h_rstd, h_ms = sem("h_sq"), sem("h_rstd"), sem("h_ms")
        d_sq, d_rstd, d_ms = sem("d_sq"), sem("d_rstd"), sem("d_ms")
        lat_n, rope_q, rope_k, mix_done = (sem(n) for n in ("lat_n", "rope_q", "rope_k", "mix_done"))
        xm_done = sem("xm_done")
        in_t5, in_na, in_fin, in_lam = sem("in_t5"), sem("in_na"), sem("in_fin"), sem("in_lam")
        in_rel, rel_st, rel_rep, rel_na = sem("in_rel"), sem("rel_st"), sem("rel_rep"), sem("rel_na")
        lam_s, lam_e = sem("lam_s"), sem("lam_e")
        y_out = sem("y_out")
        merge_done = sem("merge_done")
        act_done = sem("act_done")
        k_s, k_min, k_exp, k_t, k_p, k_o, k_done = (sem(n) for n in ("k_s", "k_min", "k_exp", "k_t", "k_p", "k_o", "k_done"))
        in_post = sem("in_post")
        kb_done, gn_done, m_done, y_done, x4_done = (sem(n) for n in ("kb_done", "gn_done", "m_done", "y_done", "x4_done"))
        j_s, j_min, j_exp, j_t, j_p, j_o, j_done = (sem(n) for n in ("j_s", "j_min", "j_exp", "j_t", "j_p", "j_o", "j_done"))
        s_out = sem("s_out")
        rel_src = sem("rel_src")

        def slot(n, m=RING):
            return ring[:, (n % m) * SLOT:(n % m + 1) * SLOT]

        def chunk(blk, c):
            _, n, kt, width, c0, cols, at, _ = (CH1, CH2, CH3)[blk][c]
            lo = (n % RING) * SLOT + at
            w, low = (t[:, lo:lo + kt * width].rearrange("p (k c) -> p k c", k=kt)[:, :, c0:c0 + cols]
                      for t in (ring, ring_r))
            h0 = RING * SLOT + (c % 2) * 2048
            high = ring_r[:, h0:h0 + kt * cols].rearrange("p (k c) -> p k c", k=kt)
            return w, high, low

        PARTS2 = {U2AT["kvwg"]: 4, U2AT["w1"]: 2, U2AT["ab0"]: 2, U2AT["ab1"]: 2}

        def landed(n):
            return 16 * (n // RING + 1)

        def landed2(n):
            return 16 * sum(PARTS2.get(m, 1) for m in range(n % RING, n + 1, RING))

        def landed3(n, l):
            per = 16 * sum(PARTS3.get(m, 1) for m in range(n % RING, len(L3), RING))
            return l * per + 16 * sum(PARTS3.get(m, 1) for m in range(n % RING, n + 1, RING))

        def piece(eng, i, l=None):
            if l is None:
                eng.wait_ge(g_ready, i + 1)
            else:
                eng.wait_ge(g3_ready, l * LPN + (i + 1))

        def bank_free(eng, i, l=None):
            if i >= 4:
                if l is None:
                    eng.wait_ge(g_free[i % 4], i // 4)
                else:
                    eng.wait_ge(g3_free[i % 4], l * (LPN // 4) + i // 4)

        def taken(eng, *idx, l=None):
            for i in sorted({i % 4: i for i in sorted(idx)}.values()):
                if l is None:
                    eng.wait_ge(g_free[i % 4], i // 4 + 1)
                else:
                    eng.wait_ge(g3_free[i % 4], l * (LPN // 4) + (i // 4 + 1))

        def G(i):
            return psum[:, i % 4, :]

        def halves(blk, c):
            kt = (CH1, CH2, CH3)[blk][c][2]
            return (slice(0, kt // 2), slice(kt // 2, kt))

        def piece_used(eng, blk, c, l=None):
            name = (CH1, CH2, CH3)[blk][c][7]
            if blk < 2:
                piece(eng, AT[name])
            elif name[:2] == "dn":
                eng.wait_ge(w3_dn, l * 10 + (int(name[2:]) + 1))
            else:
                piece(eng, LAT[name], l)

        class Splitter:

            def __init__(self, eng, blk, l=None):
                self.eng, self.blk, self.l, self.next = eng, blk, l, 0

            def ahead(self, c):
                n = len((CH1, CH2, CH3)[self.blk])
                while self.next <= min(c + 2, n - 1):
                    for i in range(2):
                        self.half(self.next, i)

            def half(self, c, i):
                self.split(c, i)
                self.next = c + i

        class High(Splitter):
            def split(self, c, i):
                blk, l = self.blk, self.l
                n = (CH1, CH2, CH3)[blk][c][1]
                if i == 0:
                    if blk == 0:
                        self.eng.wait_ge(w_ready[n % RING], landed(n))
                    elif blk == 1:
                        self.eng.wait_ge(w2_ready[n % RING], landed2(n))
                    else:
                        self.eng.wait_ge(w3_ready[n % RING], landed3(n, l))
                    if c >= 2:
                        piece_used(self.eng, blk, c - 2, l)
                w, high, _ = chunk(blk, c)
                k = halves(blk, c)[i]
                nc.scalar.copy(high[:, k, :], w[:, k, :]).then_inc(c_high[blk], 1)

        class Low(Splitter):
            def split(self, c, i):
                blk, l = self.blk, self.l
                w, high, low = chunk(blk, c)
                base = 0 if l is None else l * (2 * len(CH3))
                k = halves(blk, c)[i]
                self.eng.wait_ge(c_high[blk], base + (2 * c + i + 1))
                nc.vector.tensor_tensor(low[:, k, :], w[:, k, :], high[:, k, :].bitcast(F32),
                                        ALU.subtract).then_inc(c_low[blk], 1)

        def job3(j, l):
            kind, h, c, t = JOBS3[j]
            qs = slice(t * P, t * P + P)
            if kind == "mla":
                return dict(q=qmT[0:96, h, qs], k=kmT[0:96, h, :], widths=[P] * TT, bias=None,
                            v=[vd[:, i, h * HD:h * HD + HD] for i in range(TT)],
                            out=mix[:, t, 768 + h * HD:832 + h * HD], coef=None, first=True)
            b = ("na", "diff", "dil").index(kind)
            lo, n = (HD * (h % 2), HD) if kind != "diff" else (HD * (h % 2) + 32 * c, 32)
            bias = nab[:, h, t, :] if kind == "na" else t5b[:, h + 4 * (kind == "dil"), t, :]
            return dict(q=qk[lo:lo + n, 4 * b + h // 2, qs], k=qk[lo:lo + n, 4 * b + 2 + h // 2, :], widths=[P] * TT,
                        bias=bias, v=[v3[:, b, i, h * HD:h * HD + HD] for i in range(TT)],
                        out=mix[:, t, 256 * b + h * HD:256 * b + h * HD + HD],
                        coef=lamneg[:, bass.ds(l, 1)] if c else None, first=c == 0)

        def job2(j):
            br, h, t = JOBS2[j]
            lo = HD * (h % 2)
            g = h // 4
            qs = slice(t * P, t * P + P)
            part_ = slice(lo, lo + HD)
            out_ = (oB if br == "moba" else oA)[:, t, h * HD:h * HD + HD]
            dist = K("dist")[:, 0:P] if t == 0 else K("dist")[:, P:P + T]
            nk = P * (t + 1)
            if br == "cmp":
                return dict(q=qaT[part_, h // 2, qs], k=kcT[part_, g * NCMP:(g + 1) * NCMP], widths=[NCMP],
                            dist=K("cmpdist")[:, 16 * t:16 * t + NCMP], slope=slope(2 * h),
                            v=[vcn[0:NCMP, g, :]], out=out_, coef=gn[:, t, h:h + 1], first=True)
            if br == "moba":
                return dict(q=qbT[part_, h // 2, qs], k=kbT[part_, h // 2, 0:nk], widths=[P] * (t + 1), dist=dist,
                            slope=slope(2 * h + 1), v=[vbn[:, i, h * HD:h * HD + HD] for i in range(t + 1)],
                            out=out_, coef=None, first=True)
            kk, vv, i = (ksT, vs, 1) if br == "slc" else (kwT, vw, 2)
            return dict(q=qaT[part_, h // 2, qs], k=kk[part_, g, 0:nk], widths=[P] * (t + 1), dist=dist,
                        slope=slope(2 * h), v=[vv[:, u, g * HD:g * HD + HD] for u in range(t + 1)],
                        out=out_, coef=gn[:, t, 8 * i + h:8 * i + h + 1], first=False)

        block = ctx.enter_context(nc.Block())

        @block.sync
        def _(sp):
            sp.dma_start(vrow[0:48, 0, :], a["b_ada"].rearrange("l (r n) -> (l r) n", n=P)).then_inc(in_vec, 16)
            for r0, n, t in ((48, 8, a["g_norm_mix"]), (56, 8, a["g_norm_moe"]), (64, 8, a["c"]),
                             (88, 8, None), (96, 16, a["b_gate"])):
                if t is not None:
                    sp.dma_start(vrow[r0:r0 + n, 0, :], t.rearrange("l (r n) -> (l r) n", n=P)).then_inc(in_vec, 16)
            sp.dma_start(vrow[72:96, 0, :], a["w_conv"].rearrange("l w (r n) -> (l w r) n", n=P)).then_inc(in_vec, 16)
            r0 = 0
            for t in ("norm_pre_2", "attn_norm_3", "ffn_norm_3", "mla_q_norm_3", "mla_kv_norm_3"):
                v = a[t].rearrange("l (r n) -> (l r) n", n=P)
                sp.dma_start(vrow[r0:r0 + v.shape[0], 1, :], v).then_inc(in_vec, 16)
                r0 += v.shape[0]
            for t in ("cmp_pe_k_2", "cmp_pe_v_2"):
                sp.dma_start(vrow[r0:r0 + 16, 1, :], a[t].rearrange("l (r c) d -> (l r) (c d)", c=2)).then_inc(in_vec, 16)
                r0 += 16
            sp.dma_start(t5tab[0:32, :], a["t5_table_3"]).then_inc(in_rel, 16)
            sp.dma_start(t5hot[0:32, :], a["c_rel"][0:32, 0:REL]).then_inc(in_rel, 16)
            sp.dma_start(diladd[0:8, :], a["c_rel"][0:8, REL:2 * REL]).then_inc(in_rel, 16)
            sp.dma_start(lamraw, a["diff_lambda_3"].rearrange("l c n -> l (c n)").partition_broadcast(P)).then_inc(in_lam, 16)
            sp.dma_start(subg, a["diff_subln_3"].partition_broadcast(P)).then_inc(in_lam, 16)
            sp.dma_start(cst, a["c_kept"]).then_inc(in_cst, 16)
            sp.dma_start(x, a["x"].rearrange("b (t p) d -> p (b t) d", p=P)).then_inc(in_x, 16)

            def unit(n, *moves):
                if n >= RING:
                    sp.wait_ge(g_ready, LAST[n - RING] + 1)
                for dst, src in moves:
                    sp.dma_start(dst, src).then_inc(w_ready[n % RING], 16)

            def cols(w, c0, n, kt=KT):
                return w.rearrange("l (k p) n -> p (l k) n", p=P)[:, 0:kt, c0:c0 + n]

            def dst(n, kt, c, at=0):
                return slot(n)[:, at:at + kt * c].rearrange("p (k c) -> p k c", k=kt)

            for i in range(12):
                n = UAT[f"ada{i}"]
                unit(n, (dst(n, KT, 512), cols(a["w_ada"], 512 * i, 512)))
                if i == 0:
                    sp.dma_start(gate_m, a["b_ada"][:, 2 * D:3 * D].partition_broadcast(P).squeeze(1)).then_inc(in_b1, 16)
                    sp.dma_start(gate_f, a["b_ada"][:, 5 * D:6 * D].partition_broadcast(P).squeeze(1)).then_inc(in_b1, 16)
                    sp.dma_start(dfts, a["c_dft"][:, 0:TT * 2 * T].rearrange("p (k n) -> p k n", k=TT)).then_inc(in_b1, 16)
                    sp.dma_start(dftg, a["c_dft"][:, TT * 2 * T:].rearrange("p (k n) -> p k n", k=2)).then_inc(in_b1, 16)
                    sp.dma_start(arena[:, 3 * D:3 * D + 1024], a["c_moe"]).then_inc(in_moe, 16)
                    sp.dma_start(gbc, a["g_final"].unsqueeze(0).partition_broadcast(P).squeeze(1)).then_inc(in_moe, 16)
            for i in range(11):
                n = UAT[f"win{i}"]
                unit(n, (dst(n, KT, 512), cols(a["w_in"], 512 * i, 512)))
            for i in range(2):
                n = UAT[f"wf{i}"]
                unit(n, (dst(n, 4, 512), cols(a["w_fourier"], 512 * i, 512, 4)))
            for nm, w in (("wc", "w_conv_out"), ("wo", "w_o")):
                for i in range(2):
                    n = UAT[f"{nm}{i}"]
                    unit(n, (dst(n, KT, 512), cols(a[w], 512 * i, 512)))
            wg = a["w_gate_e"].rearrange("l e (k p) f -> p (l e k) f", p=P)
            wu = a["w_up_e"].rearrange("l e (k p) f -> p (l e k) f", p=P)
            wd = a["w_down_e"].rearrange("l e (k p) d -> p (l e k) d", p=P)

            def expert_unit(e, i):
                if i < 8:
                    w = wg if i < 4 else wu
                    src = w[:, bass.ds(e * KT + 2 * (i % 4), 2), :]
                    d = slot(i, RINGM).rearrange("p (k c) -> p k c", k=2)
                else:
                    src = wd[:, bass.ds(e * (FE // P) + 4 * (i - 8), 4), :]
                    d = slot(i, RINGM).rearrange("p (k c) -> p k c", k=4)
                sp.dma_start(d, src).then_inc(wm_ready[i % RINGM], 16)

            for i in [(N_MOE + j) % RING for j in range(RING)] + [RING]:
                prev = max(n for n in range(N_MOE) if n % RING == i) if i < RING else N_MOE - 1
                sp.wait_ge(g_ready, LAST[prev] + 1)
                expert_unit(0, i)
            with sp.Fori(0, NE - 1) as e:
                for i in range(RINGM, UPE):
                    sp.wait_ge(e_unit, e * UPE + (i - RINGM + 1))
                    expert_unit(e, i)
                for i in range(RINGM):
                    sp.wait_ge(e_unit, e * UPE + (i + RINGM + 1))
                    expert_unit(e + 1, i)
            for i in range(RINGM, UPE):
                sp.wait_ge(e_unit, (NE - 1) * UPE + (i - RINGM + 1))
                expert_unit(NE - 1, i)
            def unit2(name, *moves):
                n = U2AT[name]
                if n < RING:
                    sp.wait_ge(e_unit, (NE - 1) * UPE + RINGM + n + 1)
                else:
                    sp.wait_ge(g_ready, LAST2[n - RING] + 1)
                for d, src in moves:
                    sp.dma_start(d, src).then_inc(w2_ready[n % RING], 16)

            def w2cols(name, c0, n):
                unit2(name, (dst(U2AT[name], KT, n), cols(a["w_in_2"], c0, n)))

            w2cols("qa", 0, 512)
            w2cols("kv", 512, 512)
            n = U2AT["kvwg"]
            unit2("kvwg", (dst(n, KT, 280), cols(a["w_in_2"], 1024, 280)),
                  (dst(n, 1, HD, KT * 280), cols(a["cmp_w2_k_2"], 0, HD, 1)),
                  (dst(n, 1, HD, KT * 280 + HD), cols(a["cmp_w2_k_2"], 0, HD, 1)),
                  (dst(n, 1, HD, KT * 280 + P), cols(a["cmp_w2_v_2"], 0, HD, 1)))
            n = U2AT["w1"]
            unit2("w1", *[(dst(n, 16, P, 2048 * i), a[f"cmp_w1_{c}_2"].rearrange("o (l c) d e -> (c d) (o l) e", c=2))
                          for i, c in enumerate("kv")])
            for nm, c0 in (("za", 1304), ("qb", 1816), ("kb", 2328), ("vb", 2840), ("zb", 3352), ("mg0", 3864),
                           ("mg1", 4376), ("mg2", 4888), ("mg3", 5400)):
                w2cols(nm, c0, 512)
            for i in range(2):
                n = U2AT[f"ab{i}"]
                unit2(f"ab{i}", (dst(n, 4, 512), cols(a["w_branch_a_2"], 512 * i, 512, 4)),
                      (dst(n, 4, 512, 2048), cols(a["w_branch_b_2"], 512 * i, 512, 4)))
            for i in range(2):
                n = U2AT[f"wo2_{i}"]
                unit2(f"wo2_{i}", (dst(n, KT, 512), cols(a["w_o_2"], 512 * i, 512)))
            for l in range(LAYERS):
                def unit3(name, *moves):
                    n = L3AT[name]
                    if n < RING and l == 0:
                        prev = max(m for m in LAST2 if m % RING == n)
                        sp.wait_ge(g_ready, LAST2[prev] + 1)
                    else:
                        m, ll = (n - RING, l) if n >= RING else (n + len(L3) - RING, l - 1)
                        if m in LAST3:
                            sp.wait_ge(g3_ready, ll * LPN + LAST3[m] + 1)
                        else:
                            sp.wait_ge(w3_dn, ll * 10 + 2 * (m - L3AT["dn0"]) + 2)
                    for d, src in moves:
                        sp.dma_start(d, src).then_inc(w3_ready[n % RING], 16)

                def dst3(n, kt, c, at=0):
                    return slot(n)[:, at:at + kt * c].rearrange("p (k c) -> p k c", k=kt)

                def kcols(w, c0, n, k0=0, kt=KT):
                    return w[l, k0 * P:(k0 + kt) * P, c0:c0 + n].rearrange("(k p) n -> p k n", p=P)

                for i, c0 in enumerate((0, 512, 1024, 2048)):
                    unit3(f"win{i}", (dst3(L3AT[f"win{i}"], KT, 512), kcols(a["w_in_3"], c0, 512)))
                n = L3AT["win4"]
                unit3("win4", (dst3(n, KT, 160), kcols(a["w_in_3"], 2560, 160)),
                      (dst3(n, 2, 384, KT * 160), kcols(a["w_uq_3"], 0, 384, 0, 2)),
                      (dst3(n, 1, 512, KT * 160 + 768), kcols(a["w_ukv_3"], 0, 512, 0, 1)))
                if l == 0:
                    sp.wait_ge(x4_done, 1)
                    sp.wait_ge(rel_rep, 16)
                    for h in range(8):
                        for t in range(TT):
                            o = T - 1 - t * P
                            src = t5_rep[h, o:o + P * (REL - 1)].rearrange("(q w) -> q w", w=REL - 1)[:, 0:T]
                            sp.dma_start(t5b[:, h, t, :], src).then_inc(in_t5, 16)
                unit3("win5", (dst3(L3AT["win5"], KT, 512), kcols(a["w_in_3"], 1536, 512)))
                for i in range(2):
                    unit3(f"wo{i}", (dst3(L3AT[f"wo{i}"], KT, 512), kcols(a["w_o_3"], 512 * i, 512)))
                for i in range(11):
                    n = L3AT[f"gu{i}"]
                    d = dst3(n, KT, 512)
                    unit3(f"gu{i}", (d[:, :, 0:256], kcols(a["w_gate_3"], 256 * i, 256)),
                          (d[:, :, 256:512], kcols(a["w_up_3"], 256 * i, 256)))
                for i in range(6):
                    kt = min(4, FT - 4 * i)
                    unit3(f"dn{i}", (dst3(L3AT[f"dn{i}"], kt, D), kcols(a["w_down_3"], 0, D, 4 * i, kt)))
            sp.wait_ge(y_out, 2)
            sp.dma_start(out.rearrange("b (t p) d -> p (b t) d", p=P), x).then_inc(s_out, 16)
            sp.wait_ge(s_out, 16)

        @block.gpsimd
        def _(pool):
            nc.gpsimd.memset(neghalf, -0.5).then_inc(consts_set, 1)
            nc.gpsimd.memset(csil.rearrange("p k n -> p (k n)"), 0.0).then_inc(consts_set, 1)
            nc.gpsimd.memset(cv.rearrange("p k t -> p (k t)"), 0.0).then_inc(consts_set, 1)
            nc.gpsimd.memset(narow, 0.0).then_inc(consts_set, 1)
            nc.gpsimd.memset(halfs, -0.5).then_inc(consts_set, 1)

            def rstd_of(k):
                pool.wait_ge(n_sq, 2 * k + 2)
                nc.gpsimd.tensor_scalar(rstd, ssq, 1.0 / D, EPS, ALU.mult, ALU.add).then_inc(n_ms, 1)
                pool.wait_ge(n_ms, k + 1)
                if k == 0:
                    pool.wait_ge(consts_set, 1)
                nc.gpsimd.tensor_tensor(rstd, rstd, neghalf, ALU.pow).then_inc(n_rstd, 1)

            rstd_of(0)
            pool.wait_ge(consts_set, 4)
            for l in range(LAYERS):
                for h in range(4):
                    r = (l * 4 + h) * 7
                    pool.dma_start(narow[r:r + 7, 48:79], a["na_rpb_3"][l, h, 4:11, :]).then_inc(rel_na, 16)
            pool.wait_ge(rel_na, 16 * 8)
            pool.dma_start(na_row, narow[0:56, :]).then_inc(rel_na, 16)
            pool.wait_ge(rel_src, 1)
            pool.dma_start(t5_row, t5vec[0:8, :]).then_inc(rel_st, 16)
            pool.wait_ge(rel_na, 16 * 9)
            pool.dma_start(na_rep.rearrange("r (q n) -> r q n", q=GRID_W),
                           na_row.unsqueeze(1).broadcast_to([56, GRID_W, NAREL])).then_inc(rel_na, 16)
            pool.wait_ge(rel_st, 16)
            pool.dma_start(t5_rep[:, 0:P * REL].rearrange("r (q n) -> r q n", q=P),
                           t5_row.unsqueeze(1).broadcast_to([8, P, REL])).then_inc(rel_rep, 16)
            pool.wait_ge(rel_na, 16 * 10)
            pool.wait_ge(x1_done, 4)
            pool.dma_start(wr, a["w_router"].rearrange("l (k p) e -> p (l k) e", p=P)).then_inc(in_route, 16)
            pool.dma_start(brow, a["b_router"].partition_broadcast(P).squeeze(1)).then_inc(in_route, 16)
            rstd_of(1)
            nc.gpsimd.memset(acc.rearrange("p t d -> p (t d)"), 0.0).then_inc(e_acc, 1)
            rstd_of(2)
            pool.wait_ge(x3_done, TT)
            pool.dma_start(gbc, a["norm_post_2"].partition_broadcast(P).squeeze(1)).then_inc(in_post, 16)
            rstd_of(3)

            def bias_loads(l):
                for h in range(4):
                    for t in range(TT):
                        for r in range(2):
                            row = l * 28 + (h * 7 + 3 - 2 * t - r)
                            src = na_rep[row:row + 4, GRID_W - 1:GRID_W - 1 + GRID_W * (NAREL - 1)]
                            src = src.rearrange("r (q w) -> q r w", w=NAREL - 1)[:, :, 0:GRID_W]
                            pool.dma_start(nab[GRID_W * r:GRID_W * r + GRID_W, h, t, :].rearrange("p (r n) -> p r n", r=4),
                                           src).then_inc(in_na, 16)

            pool.wait_ge(y_done, 1)
            bias_loads(0)
            rstd_of(4)

            def roots(dst_, src, widths, sq, ms, need, at):
                pool.wait_ge(sq, need)
                for lo, hi, w in widths:
                    o = nc.gpsimd.tensor_scalar(dst_[:, lo:hi], src[:, lo:hi], 1.0 / w, EPS, ALU.mult, ALU.add)
                    o.then_inc(ms, 1)
                pool.wait_ge(ms, at)
                n = widths[-1][1]
                return nc.gpsimd.tensor_tensor(dst_[:, 0:n], dst_[:, 0:n], halfs[:, 0:n], ALU.pow)

            for l in range(LAYERS):
                roots(rstd, ssq, [(0, 2, D)], n3_sq, n3_ms, l * 4 + 2, l * 2 + 1).then_inc(n3_rstd, 1)
                roots(hrstd, hstat, [(0, 2, 256), (2, 4, P)], h_sq, h_ms, l * 4 + 4, l * 2 + 2).then_inc(h_rstd, 1)
                if l + 1 < LAYERS:
                    pool.wait_ge(k_done, l * NJ3 + 8)
                    bias_loads(l + 1)
                roots(hrstd, hstat, [(0, 8, HD)], d_sq, d_ms, l + 1, l + 1).then_inc(d_rstd, 1)
                roots(rstd, ssq, [(0, 2, D)], n3_sq, n3_ms, l * 4 + 4, l * 2 + 2).then_inc(n3_rstd, 1)
            pool.dma_start(gbc, a["final_norm_3"].unsqueeze(0).partition_broadcast(P).squeeze(1)).then_inc(in_fin, 16)
            roots(rstd, ssq, [(0, 2, D)], n3_sq, n3_ms, LAYERS * 4 + 2, LAYERS * 2 + 1).then_inc(n3_rstd, 1)

        @block.scalar
        def _(act):
            def squares(xn, src=x, sq=n_sq, done=None):
                for t in range(TT):
                    if done is not None:
                        act.wait_ge(done, t + 1)
                    nc.scalar.activation(xn[:, t, :], src[:, t, :], ACT.Square,
                                         accum_out=ssq[:, t:t + 1]).then_inc(sq, 1)

            act.wait_ge(v_cols, 1)
            act.wait_ge(consts_set, 2)
            nc.scalar.activation(csil[:, :, 0:1], vec1[:, 64:72].unsqueeze(2), ACT.Silu).then_inc(c_act, 1)
            act.wait_ge(in_x, 16)
            squares(xn1)
            act.wait_ge(lam_s, 1)
            nc.scalar.activation(lamexp, lamsum, ACT.Exp).then_inc(lam_e, 1)
            for u in range(12):
                i = AT[f"ada{u}"]
                piece(act, i)
                if u >= 2:
                    act.wait_ge(mod_mm, u - 1)
                nc.scalar.copy(part[:, u % 2, :], G(i)).then_inc(g_free[i % 4], 1)
            high = High(act, 0)
            high.ahead(-1)
            for i in (AT["uf0"], AT["uf1"]):
                high.ahead(C1AT[f"uf{i - AT['uf0']}"])
                piece(act, i)
                h = i - AT["uf0"]
                nc.scalar.copy(uf[:, :, 256 * h:256 * h + 256],
                               G(i).rearrange("p (t n) -> p t n", t=TT)).then_inc(g_free[i % 4], 1)
            for g in range(4):
                i = AT[f"dfta{g}"]
                piece(act, i)
                nc.scalar.copy(Bcs[:, g, :], G(i)).then_inc(g_free[i % 4], 1)
            for nm, dstT in (("v", vT), ("b", bT)):
                for h in range(4):
                    i = AT[f"{nm}{h}"]
                    high.ahead(C1AT[f"{nm}{h}"])
                    piece(act, i)
                    nc.scalar.copy(dstT[:, 2 * h:2 * h + 2, :],
                                   G(i).rearrange("p (k t) -> p k t", k=2)).then_inc(g_free[i % 4], 1)
            for h in range(4):
                high.ahead(C1AT[f"c{h}"])
            for b, (nm, dstT) in enumerate((("ga", gaT), ("gb", gbT))):
                for h in range(4):
                    i = AT[f"{nm}{h}"]
                    high.ahead(C1AT[f"{nm}{h}"])
                    piece(act, i)
                    for m in range(2):
                        k = 2 * h + m
                        o = nc.scalar.activation(dstT[:, k, :], G(i)[:, m * T:m * T + T], ACT.Sigmoid,
                                                 bias=vec1[:, 96 + 8 * b + k:97 + 8 * b + k])
                    o.then_inc(g_free[i % 4], 1)
            for nm in ("wf", "wc", "wo"):
                for h in range(4):
                    high.ahead(C1AT[f"{nm}{h}"])
            act.wait_ge(x1_done, 4)
            act.wait_ge(n_rstd, 1)
            act.wait_ge(n_xn, 1)
            squares(xn2)
            act.wait_ge(r_lg, 1)
            for t in range(TT):
                nc.scalar.activation(ex[:, t, :], lg[:, t, :], ACT.Exp, bias=negmax[:, t:t + 1],
                                     accum_out=rsum[:, t:t + 1]).then_inc(r_exp, 1)
            for h in range(4):
                i = AT[f"h2n{h}"]
                piece(act, i)
                nc.scalar.copy(h2n[:, h // 2, 512 * (h % 2):512 * (h % 2) + 512], G(i)).then_inc(g_free[i % 4], 1)
            with act.Fori(0, NE) as e:
                act.wait_ge(e_unit, e * UPE + 4)
                nc.scalar.activation(sil, psum[:, 0, :], ACT.Silu).then_inc(e_sil, 1)
                act.wait_ge(e_hTp, e + 1)
                nc.scalar.copy(hT.rearrange("p s n -> p (s n)"), psum[:, 3, :]).then_inc(e_hT, 1)
                act.wait_ge(e_unit, e * UPE + UPE)
                nc.scalar.copy(ysb, psum[:, 2, 0:T]).then_inc(e_y, 1)
            high = High(act, 1)
            for i in range(2):
                high.half(0, i)
            squares(xn2, done=x2_done)

            high.ahead(-1)
            squares(xn3, done=x3_done)

            def take(name, d, func=ACT.Copy, scale=1.0, src=None, l=None):
                i = AT[name] if l is None else LAT[name]
                piece(act, i, l)
                src = G(i) if src is None else src(G(i))
                free = g_free if l is None else g3_free
                return nc.scalar.activation(d, src, func, scale=scale).then_inc(free[i % 4], 1)

            def two(g):
                return g.rearrange("p (k n) -> p k n", k=2)

            SC = HD ** -0.5
            for h in range(2):
                high.ahead(C2AT[f"qa{h}"])
                take(f"qa{h}", qaT[:, 2 * h:2 * h + 2, :], scale=-SC, src=two)
            high.ahead(C2AT["kc"])
            high.ahead(C2AT["ksvs"])
            take("vs", vs, src=lambda g: two(g[:, 0:2 * P]))
            high.ahead(C2AT["kwvw"])
            take("vw", vw, src=lambda g: two(g[:, 0:2 * P]))
            high.ahead(C2AT["gnsa"])
            take("gnsa", gn, ACT.Sigmoid, src=lambda g: two(g[:, 0:48]))
            high.ahead(C2AT["za0"])
            take("za0", zA[:, :, 0:256], ACT.Silu, src=two)
            take("hk", hk[:, :, 0:2 * NCMP], ACT.Silu, src=lambda g: two(g[:, 0:64])[:, :, 0:2 * NCMP])
            high.ahead(C2AT["za1"])
            take("za1", zA[:, :, 256:512], ACT.Silu, src=two)
            take("kcT", kcT[:, 0:2 * NCMP], src=lambda g: g[:, 0:2 * NCMP])
            take("vcn", vcn[0:NCMP, :, :], src=lambda g: two(g[0:NCMP, 0:2 * HD]))

            def exp_of(j, J, mins, exps, base=0, sbuf=sbuf):
                b = j % 4
                act.wait_ge(mins, base + (j + 1))
                nk = sum(J["widths"])
                nc.scalar.activation(sbuf[:, b, 0:nk], sbuf[:, b, 0:nk], ACT.Exp, bias=jmin[:, b:b + 1], scale=-1.0,
                                     accum_out=jsum[:, b:b + 1]).then_inc(exps, 1)

            def probs_of(j, J, turned, used, probs, base=0, pbuf=pbuf):
                b = j % 2
                act.wait_ge(turned, base + (j + 1))
                if j >= 2:
                    act.wait_ge(used, base + (j - 1))
                w = J["widths"]
                d = pbuf[0:w[0], b, 0:len(w) * P]
                nc.scalar.copy(d, psum[0:w[0], 6, 0:len(w) * P]).then_inc(probs, 1)

            for kind, n in PLAN2:
                if kind == "job":
                    if n >= 2:
                        probs_of(n - 2, job2(n - 2), j_t, j_o, j_p)
                    exp_of(n, job2(n), j_min, j_exp)
                    continue
                if kind == "split":
                    high.half(*n)
                    continue
                h = int(n[-1])
                if n[:2] == "zb":
                    take(n, zB[:, :, 256 * h:256 * h + 256], ACT.Silu, src=two)
                elif n[:2] == "qb":
                    take(n, qbT[:, 2 * h:2 * h + 2, :], scale=-SC, src=two)
                elif n[:2] == "kb":
                    take(n, kbT[:, 2 * h:2 * h + 2, :], src=two)
                elif n[:2] == "vb":
                    take(n, vbn[:, :, 256 * h:256 * h + 256], src=two)
                else:
                    take(n, (mAT if n[1] == "A" else mBT)[:, 2 * h:2 * h + 2, :], src=two)
            for j in (NJ2 - 2, NJ2 - 1):
                probs_of(j, job2(j), j_t, j_o, j_p)
            nc.scalar.drain()
            for g in (mAT, mBT):
                nc.scalar.activation(g, g, ACT.Sigmoid).then_inc(merge_done, 1)
            high.ahead(C2AT["mB3"])
            for q in range(2):
                for nm in ("wa", "wb"):
                    for h in (2 * q, 2 * q + 1):
                        high.ahead(C2AT[f"{nm}{h}"])
            for h in range(4):
                high.ahead(C2AT[f"wo2_{h}"])
                take(f"wo2_{h}", mixn[:, :, 256 * h:256 * h + 256], src=two)
            nc.scalar.drain()
            squares(yjunk, mixn)

            Q = {"qa0": (0, -SC), "ka0": (2, 1.0), "qb0": (4, -((HD // 2) ** -0.5)), "kb0": (6, 1.0), "qc0": (8, -SC),
                 "kc0": (10, 1.0)}
            with act.Fori(0, LAYERS) as l:
                act.wait_ge(x4_done, l + 1)
                squares(mix, sq=n3_sq)
                high = High(act, 2, l)
                high.ahead(-1)
                for kind, n in PLAN3:
                    if kind == "job":
                        if n >= 2:
                            probs_of(n - 2, job3(n - 2, l), k_t, k_o, k_p, l * NJ3, pbuf3)
                        exp_of(n, job3(n, l), k_min, k_exp, l * NJ3, sbuf3)
                        continue
                    if kind == "split":
                        high.half(*n)
                        continue
                    if n in Q:
                        at, sc = Q[n]
                        take(n, qk[:, at:at + 2, :], scale=sc, src=two, l=l)
                    elif n in ("va0", "vb0", "vc0"):
                        take(n, v3[:, "abc".index(n[1]), :, :], src=two, l=l)
                    elif n == "cq":
                        take(n, cqn, src=two, l=l)
                    elif n == "ckv":
                        take(n, ckvn, src=lambda g: two(g[:, 0:2 * P]), l=l)
                    elif n == "kr":
                        take(n, krn, src=lambda g: two(g[:, 0:64]), l=l)
                        nc.scalar.drain()
                        for t in range(TT):
                            nc.scalar.activation(cqT[:, t, :], cqn[:, t, :], ACT.Square,
                                                 accum_out=hstat[:, t:t + 1]).then_inc(h_sq, 1)
                            nc.scalar.activation(ckvT[:, 0, t * P:t * P + P], ckvn[:, t, :], ACT.Square,
                                                 accum_out=hstat[:, 2 + t:3 + t]).then_inc(h_sq, 1)
                    elif n[:2] == "uq":
                        t = int(n[-1])
                        take(n, qdn[:, t, :, :], scale=-(96.0 ** -0.5),
                             src=lambda g: g[:, 0:384].rearrange("p (h n) -> p h n", h=4), l=l)
                    elif n[:3] == "ukv":
                        t = int(n[-1])
                        i = LAT[n]
                        piece(act, i, l)
                        g = G(i).rearrange("p (h c n) -> p h c n", h=4, c=2)
                        nc.scalar.copy(kcat[:, t, :, 0:HD], g[:, :, 0, :])
                        nc.scalar.copy(vd[:, t, :].rearrange("p (h n) -> p h n", h=4),
                                       g[:, :, 1, :]).then_inc(g3_free[i % 4], 1)
                    elif n[:2] in ("qm", "km"):
                        h = 2 * int(n[-1])
                        take(n, (qmT if n[0] == "q" else kmT)[0:96, h:h + 2, :], src=lambda g: two(g[0:96, :]), l=l)
                for j in (NJ3 - 2, NJ3 - 1):
                    probs_of(j, job3(j, l), k_t, k_o, k_p, l * NJ3, pbuf3)
                for h in range(3):
                    high.ahead(C3AT[f"wo3_{h}"])
                act.wait_ge(xm_done, l * 4 + 4)
                squares(mix, sq=n3_sq)
                high.ahead(C3AT["wo3_3"])
                for i in range(11):
                    high.ahead(C3AT[f"gu{2 * i}"])
                    if i >= 2:
                        taken(act, LAT[f"gu{2 * i - 3}"], l=l)
                    take(f"gu{2 * i}", silu[i % 2], ACT.Silu, l=l)
                    high.ahead(C3AT[f"gu{2 * i + 1}"])
                for i in range(11):
                    high.ahead(C3AT[f"dn{i}"])
            act.wait_ge(x4_done, LAYERS + 1)
            squares(mix, sq=n3_sq)

        @block.tensor
        def _(pe):
            def mm(o, l, r, s=True, e=True):
                return nc.tensor.matmul(o, l, r, start=s, stop=e)

            def unit(n):
                pe.wait_ge(w_ready[n % RING], landed(n))

            def ready(o, l):
                return o.then_inc(g_ready if l is None else g3_ready, 1)

            def rows(i, w, kt, c0, width, xs, l=None):
                bank_free(pe, i, l)
                for t in range(TT):
                    for k in range(kt):
                        o = mm(G(i)[:, t * width:(t + 1) * width], xs[:, k, t * P:t * P + P], w[:, k, c0:c0 + width],
                               k == 0, k == kt - 1)
                return ready(o, l)

            def split_ready(blk, name, l):
                c = (C1AT, C2AT, C3AT)[blk][name]
                pe.wait_ge(c_low[blk], (0 if l is None else l * (2 * len(CH3))) + 2 * (c + 1))
                return chunk(blk, c)[1:]

            def product(o, lhs, rhs, first, last):
                (lh, ll), (rh, rl) = lhs, rhs
                mm(o, lh, rh, first, False)
                mm(o, lh, rl, False, False)
                return mm(o, ll, rh, False, last)

            def follow(first, k, l):
                if first is not None and k % 2 == 0:
                    taken(pe, first + k // 2, l=l)

            def rows3(i, blk, name, xs, l=None, c0=0, width=256, first=None, counted=None):
                wh, wl = split_ready(blk, name, l)
                kt = wh.shape[1]
                bank_free(pe, i, l)
                for t in range(TT):
                    ts = slice(t * P, t * P + P)
                    for k in range(kt):
                        follow(first if t == 0 else None, k, l)
                        if counted is not None and t == 0 and k % 2 == 0:
                            pe.wait_ge(counted, k // 2 + 1)
                        o = product(G(i)[:, t * width:(t + 1) * width], (xs[0][:, k, ts], xs[1][:, k, ts]),
                                    (wh[:, k, c0:c0 + width], wl[:, k, c0:c0 + width]), k == 0, k == kt - 1)
                return ready(o, l)

            def cols3(i, blk, name, xs, l=None, c0=0, ms=2, k0=0, first=None):
                wh, wl = split_ready(blk, name, l)
                kt = wh.shape[1]
                bank_free(pe, i, l)
                for m in range(ms):
                    cs = slice(c0 + m * P, c0 + m * P + P)
                    for k in range(kt):
                        follow(first if m == 0 else None, k, l)
                        o = product(G(i)[:, m * T:m * T + T], (wh[:, k, cs], wl[:, k, cs]),
                                    (xs[0][:, k0 + k, :], xs[1][:, k0 + k, :]), k == 0, k == kt - 1)
                return ready(o, l)

            def turn_x(first, src, l=None):
                for h in range(4):
                    i = first + h
                    bank_free(pe, i, l)
                    for m in range(2):
                        for t in range(TT):
                            k = 2 * h + m
                            o = nc.tensor.transpose(G(i)[:, m * T + t * P:m * T + t * P + P],
                                                    src[:, t, k * P:k * P + P], ident)
                    ready(o, l)

            pe.wait_ge(in_vec, 16 * 13)
            pe.wait_ge(in_cst, 16)
            nc.tensor.transpose(psum[:, 5, 0:112], vrow[0:112, 0, :], ident[0:112, 0:112])
            nc.tensor.transpose(psum[:, 5, 128:206], vrow[0:78, 1, :], ident[0:78, 0:78]).then_inc(v_used, 1)
            pe.wait_ge(in_rel, 48)
            mm(psum[0:8, 7, :], t5tab[0:32, :], t5hot[0:32, :]).then_inc(v_used, 1)
            pe.wait_ge(rel_src, 1)
            pe.wait_ge(c_act, 1)

            def mod_second(u):
                taken(pe, AT[f"ada{u}"])
                if u not in GATE_UNITS:
                    for s in range(4):
                        o = mm(psum[:, 4, 4 * u + s:4 * u + s + 1], part[:, u % 2, s * P:s * P + P], ones[:, 0:1])
                    o.then_inc(mod_mm, 1)
                else:
                    r = GATE_UNITS.index(u)
                    if r >= 2:
                        pe.wait_ge(mod_done, r - 1)
                    mm(psum[:, 6 + r % 2, :], ones, part[:, u % 2, :]).then_inc(mod_mm, 1)

            for u in range(12):
                i, n = AT[f"ada{u}"], UAT[f"ada{u}"]
                unit(n)
                bank_free(pe, i)
                w = slot(n).rearrange("p (k c) -> p k c", k=KT)
                for k in range(2):
                    for j in range(4):
                        o = mm(G(i)[32 * j:32 * j + 32, :], csil[:, 2 * j + k, :], w[:, 2 * j + k, :], k == 0, k == 1)
                o.then_inc(g_ready, 1)
                if u >= 1:
                    mod_second(u - 1)
            mod_second(11)

            def W(n, kt, c, at=0):
                return slot(n)[:, at:at + kt * c].rearrange("p (k c) -> p k c", k=kt)

            xs = (xR[:, 0], xR[:, 1])
            pe.wait_ge(n_xn, 1)
            turn_x(AT["n1_0"], xn1)
            for h in range(2):
                rows3(AT[f"uf{h}"], 0, f"uf{h}", xs, first=AT["n1_0"] if h == 0 else None)
            taken(pe, AT["uf0"], AT["uf1"])
            pe.wait_ge(in_b1, 16 * 4)
            for g in range(4):
                i = AT[f"dfta{g}"]
                bank_free(pe, i)
                for k in range(TT):
                    o = mm(G(i), uf[:, k, g * P:g * P + P], dfts[:, k, :], k == 0, k == 1)
                o.then_inc(g_ready, 1)
            for h in range(2):
                i = AT[f"dftb{h}"]
                bank_free(pe, i)
                for m in range(2):
                    g = 2 * h + m
                    taken(pe, AT[f"dfta{g}"])
                    for c in range(2):
                        o = mm(G(i)[:, m * T:m * T + T], dftg[:, c, :], Bcs[:, g, c * T:c * T + T], c == 0, c == 1)
                o.then_inc(g_ready, 1)
            for b, nm in enumerate(("v", "b", "c", "ga", "gb")):
                for h in range(4):
                    cols3(AT[f"{nm}{h}"], 0, f"{nm}{h}", xs)
            taken(pe, AT["dftb0"], AT["dftb1"])
            for h in range(4):
                cols3(AT[f"wf{h}"], 0, f"wf{h}", (fmR[:, 0], fmR[:, 1]))
            pe.wait_ge(conv_done, 4)
            for h in range(4):
                cols3(AT[f"wc{h}"], 0, f"wc{h}", (convH, convL))
            for h in range(4):
                rows3(AT[f"wo{h}"], 0, f"wo{h}", xs, counted=z_done if h == 0 else None)

            pe.wait_ge(n_xn, 2)
            turn_x(AT["n2_0"], xn2)
            taken(pe, *range(AT["n2_0"], AT["n2_0"] + 4))
            pe.wait_ge(in_moe, 16 * 2)
            pe.wait_ge(in_route, 16 * 2)
            rows(AT["rt"], wr, KT, 0, NE, xTm)
            for h in range(4):
                i = AT[f"h2n{h}"]
                bank_free(pe, i)
                for m in range(4):
                    k = 4 * (h % 2) + m
                    o = nc.tensor.transpose(G(i)[:, m * P:m * P + P], xTm[:, k, (h // 2) * P:(h // 2) * P + P], ident)
                o.then_inc(g_ready, 1)
            pe.wait_ge(r_prob, 1)
            i = AT["pt"]
            bank_free(pe, i)
            for t in range(TT):
                o = nc.tensor.transpose(G(i)[0:NE, t * P:t * P + P], prob[:, t, :], ident)
            o.then_inc(g_ready, 1)
            pe.wait_ge(r_sel, 1)
            i = AT["mk"]
            bank_free(pe, i)
            for t in range(TT):
                o = nc.tensor.transpose(G(i)[:, t * NE:t * NE + NE], mk[0:NE, t * P:t * P + P], ident[0:NE, 0:NE])
            o.then_inc(g_ready, 1)
            taken(pe, AT["mk"])
            i = AT["pos"]
            bank_free(pe, i)
            for t in range(TT):
                for k in range(TT):
                    o = mm(G(i)[:, t * NE:t * NE + NE], tri[:, k, t * P:t * P + P], maskn[:, k, :], k == 0, k == 1)
            o.then_inc(g_ready, 1)
            pe.wait_ge(r_sel, 2)
            taken(pe, *range(AT["h2n0"], AT["pos"] + 1))

            def landed_e(e, i):
                pe.wait_ge(wm_ready[i % RINGM], e * (16 * UPE // RINGM) + 16 * (i // RINGM + 1))

            with pe.Fori(0, NE) as e:
                for k in range(KT):
                    for t in range(TT):
                        o = mm(psum[:, 3, k * CAP:k * CAP + CAP], h2n[:, t, k * P:k * P + P],
                               sel[:, t, bass.ds(e * CAP, CAP)], t == 0, t == 1)
                o.then_inc(e_gath, 1)
                pe.wait_ge(e_rep, e + 1)
                for t in range(TT):
                    o = nc.tensor.transpose(psum[:, 2, t * P:t * P + P], rep[:, t, :, :].rearrange("p j c -> p (j c)"), ident)
                o.then_inc(e_selTp, 1)
                pe.wait_ge(e_xe, e + 1)
                for i in range(8):
                    landed_e(e, i)
                    w = slot(i, RINGM).rearrange("p (k c) -> p k c", k=2)
                    for k in range(2):
                        kk = 2 * (i % 4) + k
                        for j in range(4):
                            o = mm(psum[32 * j:32 * j + 32, i // 4, :], xeT[:, kk, :], w[:, k, 512 * j:512 * j + 512],
                                   kk == 0, kk == KT - 1)
                    o.then_inc(e_unit, 1)
                pe.wait_ge(e_gu, e + 1)
                for s in range(4):
                    o = nc.tensor.transpose(psum[:, 3, s * P:s * P + P], gu[:, s * P:s * P + P], ident)
                o.then_inc(e_hTp, 1)
                pe.wait_ge(e_hT, e + 1)
                pe.wait_ge(e_selT, e + 1)
                for q in range(4):
                    landed_e(e, 8 + q)
                    w = slot(8 + q, RINGM).rearrange("p (k c) -> p k c", k=4)
                    for s in range(4):
                        for j in range(4):
                            o = mm(psum[32 * j:32 * j + 32, 2, 0:T], hT[:, s, 32 * q:32 * q + 32],
                                   w[:, s, T * j:T * j + T], q == 0 and s == 0, q == 3 and s == 3)
                    o.then_inc(e_unit, 1)
                pe.wait_ge(e_y, e + 1)
                pe.wait_ge(e_acc, e + 1)
                for t in range(TT):
                    for j in range(4):
                        o = mm(psum[:, 4 + j, t * T:t * T + T], selT[32 * j:32 * j + 32, t * P:t * P + P],
                               ysb[32 * j:32 * j + 32, :])
                o.then_inc(e_sc, 1)

            pe.wait_ge(n_xn, 3)
            turn_x(AT["n3_0"], xn3)

            def unit2(n):
                pe.wait_ge(w2_ready[n % RING], landed2(n))

            for h in range(2):
                cols3(AT[f"qa{h}"], 1, f"qa{h}", xs, first=AT["n3_0"] if h == 0 else None)
            cols3(AT["kc"], 1, "kc", xs)
            cols3(AT["ks"], 1, "ksvs", xs, ms=1)
            rows3(AT["vs"], 1, "ksvs", xs, c0=P, width=P)
            cols3(AT["kw"], 1, "kwvw", xs, ms=1)
            rows3(AT["vw"], 1, "kwvw", xs, c0=P, width=P)
            rows3(AT["gnsa"], 1, "gnsa", xs, width=24)
            rows3(AT["za0"], 1, "za0", xs)
            unit2(U2AT["w1"])
            i = AT["hk"]
            bank_free(pe, i)
            pe.wait_ge(kb_done, 1)
            for c in range(2):
                w = W(U2AT["w1"], 16, P, 2048 * c)
                for l in range(16):
                    o = mm(G(i)[:, 32 * c:32 * c + 2 * NCMP], w[:, l, :], kb2[:, c, l, 0:2 * NCMP], l == 0, l == 15)
            o.then_inc(g_ready, 1)
            rows3(AT["za1"], 1, "za1", xs)
            taken(pe, AT["hk"])
            i = AT["kcT"]
            bank_free(pe, i)
            w = slot(U2AT["kvwg"])[:, KT * 280:KT * 280 + 3 * HD]
            mm(G(i)[:, 0:2 * NCMP], w[:, 0:P], hk[:, 0, 0:2 * NCMP]).then_inc(g_ready, 1)
            i = AT["vcn"]
            bank_free(pe, i)
            for g in range(2):
                o = mm(G(i)[0:NCMP, g * HD:g * HD + HD], hk[:, 1, g * NCMP:g * NCMP + NCMP], w[:, P:P + HD])
            o.then_inc(g_ready, 1)

            def scores(j, J, s_, m_, base=0):
                if j >= 2:
                    pe.wait_ge(m_, base + (j - 1))
                mm(psum[:, 4 + j % 2, 0:sum(J["widths"])], J["q"], J["k"]).then_inc(s_, 1)

            def turn(j, J, x_, p_, t_, base=0, sbuf=sbuf):
                pe.wait_ge(x_, base + (j + 1))
                if j >= 1:
                    pe.wait_ge(p_, base + j)
                at = 0
                for i, w in enumerate(J["widths"]):
                    c = i * P
                    o = nc.tensor.transpose(psum[0:w, 6, c:c + P], sbuf[:, j % 4, at:at + w], ident)
                    at += w
                o.then_inc(t_, 1)

            def values(j, J, p_, d_, o_, base=0, pbuf=pbuf):
                pe.wait_ge(p_, base + (j + 1))
                if j >= 1:
                    pe.wait_ge(d_, base + j)
                n = len(J["widths"])
                for i, w in enumerate(J["widths"]):
                    o = mm(psum[:, 7, 0:HD], pbuf[0:w, j % 2, i * P:i * P + P], J["v"][i], i == 0, i == n - 1)
                o.then_inc(o_, 1)

            NJ = len(JOBS2)
            taken(pe, *[AT[n] for n in ("qa0", "qa1", "ks", "kw", "vs", "vw", "kcT", "vcn")])
            for kind, n in PLAN2:
                if kind == "job":
                    if n == len(NSA_JOBS):
                        taken(pe, *[AT[m] for m in ("qb0", "qb1", "kb0", "kb1", "vb0", "vb1")])
                    scores(n, job2(n), j_s, j_min)
                    if n >= 2:
                        turn(n - 2, job2(n - 2), j_exp, j_p, j_t)
                    if n >= 3:
                        values(n - 3, job2(n - 3), j_p, j_done, j_o)
                    continue
                if kind == "piece":
                    (cols3 if n[0] in "mqk" else rows3)(AT[n], 1, n, xs)
            for j in (NJ - 2, NJ - 1):
                turn(j, job2(j), j_exp, j_p, j_t)
                values(j - 1, job2(j - 1), j_p, j_done, j_o)
            values(NJ - 1, job2(NJ - 1), j_p, j_done, j_o)
            for h in range(4):
                pe.wait_ge(y_done, h // 2 + 1)
                i = AT[f"yt{h}"]
                bank_free(pe, i)
                src = (oA, oB)[h // 2]
                for m in range(2):
                    for t in range(TT):
                        k = 2 * (h % 2) + m
                        o = nc.tensor.transpose(G(i)[:, m * T + t * P:m * T + t * P + P],
                                                src[:, t, k * P:k * P + P], ident)
                o.then_inc(g_ready, 1)
            for q in range(2):
                for b, nm in ((0, "wa"), (1, "wb")):
                    for h in (2 * q, 2 * q + 1):
                        cols3(AT[f"{nm}{h}"], 1, f"{nm}{h}", (yR[:, 0], yR[:, 1]), k0=4 * b,
                              first=AT[f"yt{2 * b}"] if h == 0 else None)
            for h in range(4):
                rows3(AT[f"wo2_{h}"], 1, f"wo2_{h}", xs, counted=m_done if h == 0 else None)

            with pe.Fori(0, LAYERS) as l:
                def unit3(n):
                    pe.wait_ge(w3_ready[n % RING], landed3(n, l))

                def W3(n, kt, c, at=0):
                    return slot(n)[:, at:at + kt * c].rearrange("p (k c) -> p k c", k=kt)

                pe.wait_ge(n3_xn, l * 2 + 1)
                turn_x(LAT["n4_0"], mix, l)
                win = ("qa0", "ka0", "va0", "qb0", "kb0", "vb0", "qc0", "kc0", "vc0", "cq")
                done = set()
                for kind, n in PLAN3:
                    if kind == "job":
                        br = JOBS3[n][0]
                        if br not in done:
                            done.add(br)
                            need = {"na": ("qa0", "ka0", "va0"), "diff": ("qb0", "kb0", "vb0"),
                                    "dil": ("qc0", "kc0", "vc0"), "mla": ("qm0", "qm1", "km0", "km1", "ukv0", "ukv1")}[br]
                            taken(pe, *[LAT[m] for m in need], l=l)
                        scores(n, job3(n, l), k_s, k_min, l * NJ3)
                        if n >= 2:
                            turn(n - 2, job3(n - 2, l), k_exp, k_p, k_t, l * NJ3, sbuf3)
                        if n >= 3:
                            values(n - 3, job3(n - 3, l), k_p, k_done, k_o, l * NJ3, pbuf3)
                        continue
                    if kind == "split":
                        continue
                    i = LAT[n]
                    if n in win:
                        (rows3 if n[0] == "v" or n == "cq" else cols3)(i, 2, n, xs, l,
                                                                       first=LAT["n4_0"] if n == "qa0" else None)
                    elif n == "ckv":
                        rows3(i, 2, "ckvkr", xs, l, width=P)
                    elif n == "kr":
                        rows3(i, 2, "ckvkr", xs, l, c0=P, width=32)
                    elif n in ("cqT", "ckvT"):
                        pe.wait_ge(lat_n, l + 1)
                        bank_free(pe, i, l)
                        for m in range(2 if n == "cqT" else 1):
                            for t in range(TT):
                                src = (cqn if n == "cqT" else ckvn)[:, t, m * P:m * P + P]
                                o = nc.tensor.transpose(G(i)[:, m * T + t * P:m * T + t * P + P], src, ident)
                        ready(o, l)
                    elif n[:2] == "uq":
                        t = int(n[-1])
                        taken(pe, LAT["cqT"], l=l)
                        bank_free(pe, i, l)
                        w = W3(4, 2, 384, KT * 160)
                        for k in range(2):
                            o = mm(G(i)[:, 0:384], cqT[:, k, t * P:t * P + P], w[:, k, :], k == 0, k == 1)
                        ready(o, l)
                    elif n[:3] == "ukv":
                        t = int(n[-1])
                        taken(pe, LAT["ckvT"], l=l)
                        bank_free(pe, i, l)
                        ready(mm(G(i), ckvT[:, 0, t * P:t * P + P], W3(4, 1, 512, KT * 160 + 768)[:, 0, :]), l)
                    else:
                        pe.wait_ge(rope_q if n[0] == "q" else rope_k, l + 1)
                        bank_free(pe, i, l)
                        for m in range(2):
                            for t in range(TT):
                                src = (qdn if n[0] == "q" else kcat)[:, t, 2 * int(n[-1]) + m, :]
                                o = nc.tensor.transpose(G(i)[0:96, m * T + t * P:m * T + t * P + P], src, ident)
                        ready(o, l)
                for j in (NJ3 - 2, NJ3 - 1):
                    turn(j, job3(j, l), k_exp, k_p, k_t, l * NJ3, sbuf3)
                    values(j - 1, job3(j - 1, l), k_p, k_done, k_o, l * NJ3, pbuf3)
                values(NJ3 - 1, job3(NJ3 - 1, l), k_p, k_done, k_o, l * NJ3, pbuf3)
                pe.wait_ge(mix_done, l + 1)
                turn_x(LAT["mix0"], mix, l)
                for h in range(4):
                    rows3(LAT[f"wo3_{h}"], 2, f"wo3_{h}", (mixR[:, 0], mixR[:, 1]), l,
                          first=LAT["mix0"] if h == 0 else None)
                pe.wait_ge(n3_xn, l * 2 + 2)
                turn_x(LAT["n5_0"], mix, l)
                for i in range(22):
                    cols3(LAT[f"gu{i}"], 2, f"gu{i}", xs, l, first=LAT["n5_0"] if i == 0 else None)
                for q in range(4):
                    bank_free(pe, LAT[f"down{q}"], l)
                for c in range(FT // 2):
                    wh, wl = split_ready(2, f"dn{c}", l)
                    pe.wait_ge(act_done, l * 11 + (c + 1))
                    for k in range(2):
                        kk = 2 * c + k
                        for q in range(4):
                            ts, hs = slice(q // 2 * P, q // 2 * P + P), slice(512 * (q % 2), 512 * (q % 2) + 512)
                            o = product(psum[:, q, :], (actR[:, 0, kk, ts], actR[:, 1, kk, ts]),
                                        (wh[:, k, hs], wl[:, k, hs]), kk == 0, kk == FT - 1)
                            if kk == FT - 1:
                                ready(o, l)
                    if c < FT // 2 - 1:
                        o.then_inc(w3_dn, 1)

        @block.vector
        def _(dve):
            v = nc.vector
            xs = (xR[:, 0], xR[:, 1])

            def temp(h, k=2):
                return mt2[:, 512 * (h % 2):512 * (h % 2) + 512].rearrange("p (k t) -> p k t", k=k)

            def parts(src, xs, ks):
                v.tensor_copy(xs[0][:, ks, :], src)
                v.drain()
                return v.tensor_tensor(xs[1][:, ks, :], src, xs[0][:, ks, :].bitcast(F32), ALU.subtract)

            def modulated(first, A, B, l=None, whole=None):
                for h in range(4):
                    i = first + h
                    piece(dve, i, l)
                    d = temp(h) if whole is None else whole[:, 2 * h:2 * h + 2, :]
                    for m in range(2):
                        k = 2 * h + m
                        if B is None:
                            o = v.tensor_scalar(d[:, m, :], G(i)[:, m * T:m * T + T], A[:, k:k + 1], None, ALU.mult)
                        else:
                            o = v.tensor_scalar(d[:, m, :], G(i)[:, m * T:m * T + T], A[:, k:k + 1], B[:, k:k + 1],
                                                ALU.mult, ALU.add)
                    if whole is None:
                        v.drain()
                        o = parts(d, xs, slice(2 * h, 2 * h + 2))
                    o.then_inc((g_free if l is None else g3_free)[i % 4], 1)

            def normed(k, xn):
                dve.wait_ge(n_rstd, k + 1)
                for t in range(TT):
                    o = v.tensor_scalar(xn[:, t, :], x[:, t, :], rstd[:, t:t + 1], None, ALU.mult)
                o.then_inc(n_xn, 1)

            def pair(ap):
                return ap.rearrange("p (k t) -> p k t", k=2)

            dve.wait_ge(v_used, 1)
            v.tensor_copy(vec1, psum[:, 5, 0:112])
            v.tensor_copy(vec2, psum[:, 5, 128:206]).then_inc(v_cols, 1)
            dve.wait_ge(v_used, 2)
            dve.wait_ge(in_rel, 48)
            v.scalar_tensor_tensor(t5vec[0:8, :], psum[0:8, 7, :], -1.0, diladd[0:8, :], ALU.mult,
                                   ALU.add).then_inc(rel_src, 1)
            dve.wait_ge(in_lam, 32)
            lr = lamraw.rearrange("p l (a b n) -> p l a b n", a=2, b=2)
            for l in range(LAYERS):
                v.tensor_tensor(lamprod[:, l, :, :], lr[:, l, :, 0, :], lr[:, l, :, 1, :], ALU.mult)
                v.tensor_scalar(subg[:, l, :], subg[:, l, :], 1.0 - LAM_INIT[l], None, ALU.mult)
            v.drain()
            v.tensor_reduce(lamsum, lamprod.rearrange("p l c n -> p (l c) n"), AX_X, ALU.add).then_inc(lam_s, 1)
            normed(0, xn1)
            dve.wait_ge(in_b1, 16 * 4)
            dve.wait_ge(lam_e, 1)
            for l in range(LAYERS):
                v.tensor_tensor(lamneg[:, l:l + 1], lamexp[:, 2 * l + 1:2 * l + 2], lamexp[:, 2 * l:2 * l + 1], ALU.subtract)
            v.drain()
            for l in range(LAYERS):
                v.tensor_scalar(lamneg[:, l:l + 1], lamneg[:, l:l + 1], -LAM_INIT[l], None, ALU.add)
            for r, u in enumerate(GATE_UNITS):
                if u == 10:
                    dve.wait_ge(mod_mm, 10)
                    v.tensor_tensor(mod[:, 0:16], psum[:, 4, 0:16], vec1[:, 0:16], ALU.add)
                    v.tensor_tensor(mod[:, 24:40], psum[:, 4, 24:40], vec1[:, 24:40], ALU.add)
                    v.drain()
                    v.scalar_tensor_tensor(Am, mod[:, 8:16], 1.0, vec1[:, 48:56], ALU.add, ALU.mult)
                    v.scalar_tensor_tensor(Af, mod[:, 32:40], 1.0, vec1[:, 56:64], ALU.add, ALU.mult)
                dve.wait_ge(mod_mm, u + 1)
                g = (gate_m, gate_f)[r // 2][:, 512 * (r % 2):512 * (r % 2) + 512]
                v.tensor_tensor(g, psum[:, 6 + r % 2, :], g, ALU.add).then_inc(mod_done, 1)
            v.drain()
            low = Low(dve, 0)
            for i in range(2):
                low.half(0, i)
            modulated(AT["n1_0"], Am, mod[:, 0:8])
            low.ahead(-1)
            for h in range(2):
                low.ahead(C1AT[f"uf{h}"])
            for h in range(2):
                i = AT[f"dftb{h}"]
                piece(dve, i)
                parts(pair(G(i)), (fmR[:, 0], fmR[:, 1]), slice(2 * h, 2 * h + 2)).then_inc(g_free[i % 4], 1)
            for nm in "vb":
                for h in range(4):
                    low.ahead(C1AT[f"{nm}{h}"])
            for h in range(4):
                i = AT[f"c{h}"]
                low.ahead(C1AT[f"c{h}"])
                piece(dve, i)
                if h == 0:
                    taken(dve, *[AT[f"v{j}"] for j in range(4)])
                    taken(dve, *[AT[f"b{j}"] for j in range(4)])
                    dve.wait_ge(consts_set, 3)
                v.tensor_tensor(cv[:, 2 * h:2 * h + 2, 1:T + 1], pair(G(i)), vT[:, 2 * h:2 * h + 2, :],
                                ALU.mult).then_inc(g_free[i % 4], 1)
                v.drain()
                w = [vec1[:, 72 + 8 * j + 2 * h:74 + 8 * j + 2 * h] for j in range(3)]
                for m in range(2):
                    v.tensor_scalar(mtmp[:, m * T:m * T + T], cv[:, 2 * h + m, 0:T], w[0][:, m:m + 1], None, ALU.mult)
                for j in (1, 2):
                    v.drain()
                    for m in range(2):
                        v.scalar_tensor_tensor(mtmp[:, m * T:m * T + T], cv[:, 2 * h + m, j:T + j], w[j][:, m:m + 1],
                                               mtmp[:, m * T:m * T + T], ALU.mult, ALU.add)
                v.drain()
                v.tensor_tensor(temp(h), bT[:, 2 * h:2 * h + 2, :], mtmp[:, 0:2 * T].rearrange("p (k t) -> p k t", k=2),
                                ALU.mult)
                v.drain()
                parts(temp(h), (convH, convL), slice(2 * h, 2 * h + 2)).then_inc(conv_done, 1)
            for nm in ("ga", "gb"):
                for h in range(4):
                    low.ahead(C1AT[f"{nm}{h}"])
            for nm, gate in (("wf", gaT), ("wc", gbT)):
                for h in range(4):
                    i = AT[f"{nm}{h}"]
                    piece(dve, i)
                    if h == 0:
                        for j in range(4):
                            taken(dve, AT[("ga" if nm == "wf" else "gb") + str(j)])
                    g = gate[:, 2 * h:2 * h + 2, :]
                    v.tensor_tensor(g, pair(G(i)), g, ALU.mult).then_inc(g_free[i % 4], 1)
                    if nm == "wc":
                        v.drain()
                        z = gaT[:, 2 * h:2 * h + 2, :]
                        v.tensor_tensor(temp(h), z, g, ALU.add)
                        v.drain()
                        parts(temp(h), xs, slice(2 * h, 2 * h + 2)).then_inc(z_done, 1)
                    low.ahead(C1AT[f"{nm}{h}"])
            for h in range(4):
                i = AT[f"wo{h}"]
                low.ahead(C1AT[f"wo{h}"])
                piece(dve, i)
                c = slice(256 * h, 256 * h + 256)
                mt = mtmp[:, 512 * (h % 2):512 * (h % 2) + 512].rearrange("p (t n) -> p t n", t=TT)
                v.tensor_tensor(mt, G(i).rearrange("p (t n) -> p t n", t=TT),
                                gate_m[:, c].unsqueeze(1).broadcast_to([P, TT, 256]), ALU.mult).then_inc(g_free[i % 4], 1)
                v.drain()
                v.tensor_tensor(x[:, :, c], x[:, :, c], mt, ALU.add).then_inc(x1_done, 1)

            normed(1, xn2)
            modulated(AT["n2_0"], Af, mod[:, 24:32], whole=xTm)
            i = AT["rt"]
            piece(dve, i)
            dve.wait_ge(in_moe, 16 * 2)
            dve.wait_ge(in_route, 16 * 2)
            v.tensor_tensor(lg, G(i)[:, 0:TT * NE].rearrange("p (t e) -> p t e", t=TT),
                            brow.unsqueeze(1).broadcast_to([P, TT, NE]), ALU.add).then_inc(g_free[i % 4], 1)
            v.drain()
            v.tensor_reduce(negmax, lg, AX_X, ALU.max, negate=True).then_inc(r_lg, 1)
            dve.wait_ge(r_exp, TT)
            v.reciprocal(rrec, rsum)
            v.drain()
            for t in range(TT):
                o = v.tensor_scalar(prob[:, t, :], ex[:, t, :], rrec[:, t:t + 1], None, ALU.mult)
            o.then_inc(r_prob, 1)
            i = AT["pt"]
            piece(dve, i)
            v.tensor_copy(work[0:NE, :], G(i)[0:NE, 0:T]).then_inc(g_free[i % 4], 1)
            for _ in range(CAP // 8):
                v.drain()
                v.max(top8[0:NE, :], work[0:NE, :])
                v.drain()
                v.match_replace(work[0:NE, :], top8[0:NE, :], work[0:NE, :], -1.0)
            v.drain()
            v.tensor_scalar(mk[0:NE, :], work[0:NE, :], 0.0, None, ALU.is_lt).then_inc(r_sel, 1)
            i = AT["mk"]
            piece(dve, i)
            v.tensor_copy(maskn, G(i)[:, 0:TT * NE].rearrange("p (t e) -> p t e", t=TT)).then_inc(g_free[i % 4], 1)
            v.drain()
            i = AT["pos"]
            piece(dve, i)
            v.scalar_tensor_tensor(posm, maskn, -1000.0, G(i)[:, 0:TT * NE].rearrange("p (t e) -> p t e", t=TT),
                                   ALU.mult, ALU.add).then_inc(g_free[i % 4], 1)
            v.drain()
            v.tensor_scalar(posm, posm, 1000.0, None, ALU.add)
            v.drain()
            for t in range(TT):
                s3 = sel[:, t, :].rearrange("p (e c) -> p e c", e=NE)
                o = v.tensor_tensor(s3, slot_id, posm[:, t, :].unsqueeze(2).broadcast_to([P, NE, CAP]), ALU.is_equal)
            o.then_inc(r_sel, 1)
            v.drain()
            for t in range(TT):
                s3 = sel[:, t, :].rearrange("p (e c) -> p e c", e=NE)
                w3 = selw[:, t, :].rearrange("p (e c) -> p e c", e=NE)
                v.tensor_tensor(w3, s3, prob[:, t, :].unsqueeze(2).broadcast_to([P, NE, CAP]), ALU.mult)
            v.drain()
            dve.wait_ge(e_acc, 1)
            with dve.Fori(0, NE) as e:
                for t in range(TT):
                    o = v.tensor_copy(rep[:, t, :, :],
                                      selw[:, t, bass.ds(e * CAP, CAP)].unsqueeze(1).broadcast_to([P, 4, CAP]))
                o.then_inc(e_rep, 1)
                dve.wait_ge(e_gath, e + 1)
                v.tensor_copy(xeT.rearrange("p k c -> p (k c)"), psum[:, 3, 0:KT * CAP]).then_inc(e_xe, 1)
                dve.wait_ge(e_selTp, e + 1)
                v.tensor_copy(selT, psum[:, 2, 0:T]).then_inc(e_selT, 1)
                dve.wait_ge(e_sil, e + 1)
                dve.wait_ge(e_unit, e * UPE + 8)
                v.tensor_tensor(gu, sil, psum[:, 1, :], ALU.mult).then_inc(e_gu, 1)
                dve.wait_ge(e_sc, e + 1)
                for t in range(TT):
                    a3 = acc[:, t, :].rearrange("p (j n) -> p j n", j=4)
                    o = v.tensor_tensor(a3, psum[:, 4:8, t * T:t * T + T], a3, ALU.add)
                o.then_inc(e_acc, 1)
                v.drain()
            for t in range(TT):
                v.tensor_tensor(acc[:, t, :], acc[:, t, :], gate_f, ALU.mult)
                v.drain()
                v.tensor_tensor(x[:, t, :], x[:, t, :], acc[:, t, :], ALU.add).then_inc(x2_done, 1)
            low = Low(dve, 1)
            for i in range(2):
                low.half(0, i)
            dve.wait_ge(n_rstd, 3)
            for t in range(TT):
                v.scalar_tensor_tensor(x[:, t, :], x[:, t, :], rstd[:, t:t + 1], gbc, ALU.mult,
                                       ALU.mult).then_inc(x3_done, 1)

            normed(3, xn3)
            modulated(AT["n3_0"], vec2[:, 0:8], None)
            low.ahead(-1)
            for c in ("qa0", "qa1", "kc"):
                low.ahead(C2AT[c])

            def doubled(name, d):
                i = AT[name]
                piece(dve, i)
                for g in range(2):
                    for hf in range(2):
                        o = v.tensor_copy(d[HD * hf:HD * hf + HD, g, :], G(i)[HD * g:HD * g + HD, 0:T])
                o.then_inc(g_free[i % 4], 1)

            i = AT["kc"]
            piece(dve, i)
            for c in range(2):
                for g in range(2):
                    v.tensor_copy(k2[0:HD, c, g, :], G(i)[HD * g:HD * g + HD, c * T:c * T + T])
                    o = v.tensor_copy(k2[HD:P, c, g, 0:T - 1], G(i)[HD * g:HD * g + HD, c * T + 1:c * T + T])
            o.then_inc(g_free[i % 4], 1)
            v.drain()
            for c in range(2):
                for g in range(2):
                    for u in range(2):
                        src = k2[:, c, g, 16 * u:16 * u + 16 * NCMP].rearrange("p (n r o) -> p r n o", r=8, o=2)[:, :, :, 0]
                        d = kb2[:, c, 8 * u:8 * u + 8, g * NCMP:g * NCMP + NCMP]
                        pe_ = vec2[:, 46 + 16 * c + 8 * u:54 + 16 * c + 8 * u].unsqueeze(2).broadcast_to([P, 8, NCMP])
                        o = v.tensor_tensor(d, src, pe_, ALU.add)
            o.then_inc(kb_done, 1)
            doubled("ks", ksT)
            low.ahead(C2AT["ksvs"])
            doubled("kw", kwT)
            low.ahead(C2AT["kwvw"])
            low.ahead(C2AT["gnsa"])
            low.ahead(C2AT["za0"])
            low.ahead(C2AT["za1"])
            taken(dve, AT["gnsa"])
            for t in range(TT):
                o = v.tensor_scalar(gn[:, t, 0:8], gn[:, t, 0:8], K("cmpvalid")[:, t:t + 1], None, ALU.mult)
            v.drain()

            def least(j, J, s_, t_, m_, base=0, sbuf=sbuf):
                b = j % 4
                nk = sum(J["widths"])
                scored = psum[:, 4 + j % 2, 0:nk]
                dve.wait_ge(s_, base + (j + 1))
                if j >= 4:
                    dve.wait_ge(t_, base + (j - 3))
                if "dist" in J:
                    v.scalar_tensor_tensor(sbuf[:, b, 0:nk], J["dist"], J["slope"], scored, ALU.mult, ALU.add)
                    v.drain()
                    v.tensor_reduce(jmin[:, b:b + 1], sbuf[:, b, 0:nk], AX_X, ALU.min).then_inc(m_, 1)
                elif J["bias"] is None:
                    v.tensor_copy(sbuf[:, b, 0:nk], scored)
                    v.tensor_reduce(jmin[:, b:b + 1], scored, AX_X, ALU.min).then_inc(m_, 1)
                else:
                    v.memset(spare[:, j:j + 1], 0.0)
                    v.tensor_tensor_reduce(sbuf[:, b, 0:nk], scored, J["bias"], 1.0, 3e38,
                                           ALU.add, ALU.min, jmin[:, b:b + 1]).then_inc(m_, 1)

            def finish(j, J, x_, o_, d_, base=0):
                b = j % 4
                dve.wait_ge(x_, base + (j + 1))
                v.reciprocal(jrec[:, b:b + 1], jsum[:, b:b + 1])
                v.drain()
                if J["coef"] is not None:
                    v.tensor_tensor(jrec[:, b:b + 1], jrec[:, b:b + 1], J["coef"], ALU.mult)
                    v.drain()
                dve.wait_ge(o_, base + (j + 1))
                if J["first"]:
                    v.tensor_scalar(J["out"], psum[:, 7, 0:HD], jrec[:, b:b + 1], None, ALU.mult).then_inc(d_, 1)
                else:
                    v.scalar_tensor_tensor(J["out"], psum[:, 7, 0:HD], jrec[:, b:b + 1], J["out"],
                                           ALU.mult, ALU.add).then_inc(d_, 1)

            for kind, n in PLAN2:
                if kind == "job":
                    least(n, job2(n), j_s, j_t, j_min)
                    if n >= 3:
                        finish(n - 3, job2(n - 3), j_exp, j_o, j_done)
                    if n == len(NSA_JOBS) + 4:
                        v.drain()
                        taken(dve, AT["za0"], AT["za1"])
                        v.tensor_tensor(oA, oA, zA, ALU.mult).then_inc(y_done, 1)
                elif kind == "split":
                    low.half(*n)
            for j in range(NJ2 - 3, NJ2):
                finish(j, job2(j), j_exp, j_o, j_done)
            v.drain()
            taken(dve, AT["zb0"], AT["zb1"])
            v.tensor_tensor(oB, oB, zB, ALU.mult).then_inc(y_done, 1)
            for h in range(4):
                i = AT[f"yt{h}"]
                piece(dve, i)
                parts(pair(G(i)), (yR[:, 0], yR[:, 1]), slice(2 * h, 2 * h + 2)).then_inc(g_free[i % 4], 1)
            low.ahead(C2AT["mB3"])
            for q in range(2):
                for nm, gate in (("wa", mAT), ("wb", mBT)):
                    for h in (2 * q, 2 * q + 1):
                        i = AT[f"{nm}{h}"]
                        piece(dve, i)
                        if h == 0:
                            dve.wait_ge(merge_done, 1 if nm == "wa" else 2)
                        g = gate[:, 2 * h:2 * h + 2, :]
                        v.tensor_tensor(g, pair(G(i)), g, ALU.mult).then_inc(g_free[i % 4], 1)
                        if nm == "wb":
                            v.drain()
                            m = mAT[:, 2 * h:2 * h + 2, :]
                            v.tensor_tensor(temp(h), m, g, ALU.add)
                            v.drain()
                            parts(temp(h), xs, slice(2 * h, 2 * h + 2)).then_inc(m_done, 1)
                        low.ahead(C2AT[f"{nm}{h}"])
            for h in range(4):
                low.ahead(C2AT[f"wo2_{h}"])
            dve.wait_ge(in_post, 16)
            dve.wait_ge(n_rstd, 5)
            for t in range(TT):
                v.scalar_tensor_tensor(mixn[:, t, :], mixn[:, t, :], rstd[:, t:t + 1], gbc, ALU.mult, ALU.mult)
            v.drain()
            v.tensor_tensor(x, x, mixn, ALU.add).then_inc(x4_done, 1)

            def biases(l):
                dve.wait_ge(in_na, l * (16 * 16) + 16 * 16)
                for h in range(4):
                    for t in range(TT):
                        v.scalar_tensor_tensor(nab[:, h, t, :], nab[:, h, t, :], -1.0, K("nawin"), ALU.mult, ALU.add)
                v.drain()

            mb = mix[:, :, 256:512].rearrange("p t (h n) -> p t h n", h=4)

            def head_squares():
                v.drain()
                v.tensor_tensor(hsq, mb, mb, ALU.mult)
                v.drain()
                v.tensor_reduce(hstat[:, 0:8], hsq.rearrange("p t h n -> p (t h) n"), AX_X, ALU.add).then_inc(d_sq, 1)

            def head_norms(l):
                dve.wait_ge(d_rstd, l + 1)
                hr = hrstd.rearrange("p (t h) -> p t h", t=TT).unsqueeze(3).broadcast_to([P, TT, 4, HD])
                v.tensor_tensor(mb, mb, hr, ALU.mult)
                v.drain()
                for t in range(TT):
                    v.tensor_tensor(mb[:, t, :, :], mb[:, t, :, :], subl.unsqueeze(1).broadcast_to([P, 4, HD]), ALU.mult)

            cos = K("cos").rearrange("p (t n) -> p t n", t=TT)
            sin = K("sin").rearrange("p (t n) -> p t n", t=TT)
            with dve.Fori(0, LAYERS) as l:
                v.drain()
                v.tensor_copy(Am, vec2[:, bass.ds(l * KT + 8, KT)])
                v.tensor_copy(Af, vec2[:, bass.ds(l * KT + 24, KT)])
                v.tensor_copy(Bm[:, 0:2], vec2[:, bass.ds(l * 2 + 40, 2)])
                v.tensor_copy(Bm[:, 2:3], vec2[:, bass.ds(l + 44, 1)])
                v.tensor_copy(subl, subg.rearrange("p l n -> p (l n)")[:, bass.ds(l * HD, HD)])

                def normed3(need):
                    dve.wait_ge(n3_rstd, need)
                    for t in range(TT):
                        o = v.tensor_scalar(mix[:, t, :], x[:, t, :], rstd[:, t:t + 1], None, ALU.mult)
                    o.then_inc(n3_xn, 1)

                normed3(l * 2 + 1)
                low = Low(dve, 2, l)
                for i in range(2):
                    low.half(0, i)
                modulated(LAT["n4_0"], Am, None, l)
                low.ahead(-1)
                for kind, n in PLAN3:
                    if kind == "job":
                        if n == 8:
                            dve.wait_ge(in_t5, 16 * 16)
                        if n == 0:
                            biases(l)
                        least(n, job3(n, l), k_s, k_t, k_min, l * NJ3, sbuf3)
                        if n >= 3:
                            finish(n - 3, job3(n - 3, l), k_exp, k_o, k_done, l * NJ3)
                        if n == 28:
                            head_squares()
                        elif n == 31:
                            head_norms(l)
                        continue
                    if kind == "split":
                        low.half(*n)
                        continue
                    if n == "kr":
                        dve.wait_ge(h_rstd, l + 1)
                        taken(dve, LAT["cq"], LAT["ckv"], l=l)
                        for t in range(TT):
                            v.tensor_scalar(cqn[:, t, :], cqn[:, t, :], hrstd[:, t:t + 1], None, ALU.mult)
                            o = v.tensor_scalar(ckvn[:, t, :], ckvn[:, t, :], hrstd[:, 2 + t:3 + t], None, ALU.mult)
                        o.then_inc(lat_n, 1)
                    elif n in ("cqT", "ckvT"):
                        i = LAT[n]
                        piece(dve, i, l)
                        if n == "cqT":
                            for m in range(2):
                                o = v.tensor_scalar(cqT[:, m, :], G(i)[:, m * T:m * T + T], Bm[:, m:m + 1], None, ALU.mult)
                        else:
                            o = v.tensor_scalar(ckvT[:, 0, :], G(i)[:, 0:T], Bm[:, 2:3], None, ALU.mult)
                        o.then_inc(g3_free[i % 4], 1)
                    elif n == "uq1":
                        taken(dve, LAT["uq0"], LAT["uq1"], l=l)
                        x1, x2 = qdn[:, :, :, 64:80], qdn[:, :, :, 80:96]
                        cb = cos.unsqueeze(2).broadcast_to([P, TT, 4, 16])
                        sb_ = sin.unsqueeze(2).broadcast_to([P, TT, 4, 16])
                        for c, (u, f) in enumerate(((x1, cb), (x2, sb_), (x1, sb_), (x2, cb))):
                            v.tensor_tensor(rp[:, c, :, :, :], u, f, ALU.mult)
                        v.drain()
                        v.tensor_tensor(x1, rp[:, 0, :, :, :], rp[:, 1, :, :, :], ALU.subtract)
                        v.tensor_tensor(x2, rp[:, 2, :, :, :], rp[:, 3, :, :, :], ALU.add).then_inc(rope_q, 1)
                    elif n == "ukv1":
                        taken(dve, LAT["kr"], LAT["ukv0"], LAT["ukv1"], l=l)
                        x1, x2 = krn[:, :, 0:16], krn[:, :, 16:32]
                        for c, (u, f) in enumerate(((x1, cos), (x2, sin), (x1, sin), (x2, cos))):
                            v.tensor_tensor(rk[:, c, :, :], u, f, ALU.mult)
                        v.drain()
                        wide = [rk[:, c, :, :].unsqueeze(2).broadcast_to([P, TT, 4, 16]) for c in range(4)]
                        v.tensor_tensor(kcat[:, :, :, 64:80], wide[0], wide[1], ALU.subtract)
                        v.tensor_tensor(kcat[:, :, :, 80:96], wide[2], wide[3], ALU.add).then_inc(rope_k, 1)
                for j in range(NJ3 - 3, NJ3):
                    finish(j, job3(j, l), k_exp, k_o, k_done, l * NJ3)
                v.drain().then_inc(mix_done, 1)
                for h in range(4):
                    i = LAT[f"mix{h}"]
                    piece(dve, i, l)
                    parts(pair(G(i)), (mixR[:, 0], mixR[:, 1]), slice(2 * h, 2 * h + 2)).then_inc(g3_free[i % 4], 1)
                for h in range(4):
                    i = LAT[f"wo3_{h}"]
                    piece(dve, i, l)
                    c = slice(256 * h, 256 * h + 256)
                    v.tensor_tensor(x[:, :, c], G(i).rearrange("p (t n) -> p t n", t=TT), x[:, :, c],
                                    ALU.add).then_inc(g3_free[i % 4], 1)
                    v.drain().then_inc(xm_done, 1)
                    if h < 3:
                        low.ahead(C3AT[f"wo3_{h}"])
                normed3(l * 2 + 2)
                modulated(LAT["n5_0"], Af, None, l)
                low.ahead(C3AT["wo3_3"])
                for i in range(11):
                    n = LAT[f"gu{2 * i + 1}"]
                    low.ahead(C3AT[f"gu{2 * i}"])
                    piece(dve, n, l)
                    taken(dve, LAT[f"gu{2 * i}"], l=l)
                    v.tensor_tensor(temp(i), pair(G(n)), pair(silu[i % 2]), ALU.mult).then_inc(g3_free[n % 4], 1)
                    v.drain()
                    parts(temp(i), (actR[:, 0], actR[:, 1]), slice(2 * i, 2 * i + 2)).then_inc(act_done, 1)
                    low.ahead(C3AT[f"gu{2 * i + 1}"])
                for c in range(FT // 2):
                    low.ahead(C3AT[f"dn{c}"])
                for q in range(4):
                    i = LAT[f"down{q}"]
                    piece(dve, i, l)
                    xs = x[:, q // 2, 512 * (q % 2):512 * (q % 2) + 512]
                    v.tensor_tensor(xs, G(i), xs, ALU.add).then_inc(g3_free[i % 4], 1)
                v.drain().then_inc(x4_done, 1)
            dve.wait_ge(in_fin, 16)
            dve.wait_ge(n3_rstd, LAYERS * 2 + 1)
            for t in range(TT):
                v.scalar_tensor_tensor(x[:, t, :], x[:, t, :], rstd[:, t:t + 1], gbc, ALU.mult, ALU.mult).then_inc(y_out, 1)

    return nc


INPUTS = ["x", "c", "w_ada", "b_ada", "g_norm_mix", "w_in", "b_gate", "w_fourier", "w_conv", "w_conv_out", "w_o",
          "g_norm_moe", "w_router", "b_router", "w_gate_e", "w_up_e", "w_down_e", "g_final", "norm_pre_2", "w_in_2",
          "cmp_pe_k_2", "cmp_w1_k_2", "cmp_w2_k_2", "cmp_pe_v_2", "cmp_w1_v_2", "cmp_w2_v_2", "w_branch_a_2",
          "w_branch_b_2", "w_o_2", "norm_post_2", "attn_norm_3", "w_in_3", "na_rpb_3", "diff_lambda_3",
          "diff_subln_3", "mla_q_norm_3", "w_uq_3", "mla_kv_norm_3", "w_ukv_3", "t5_table_3", "w_o_3", "ffn_norm_3",
          "w_gate_3", "w_up_3", "w_down_3", "final_norm_3"]


def kernel(**inputs):
    import concourse.bacc as bacc
    from concourse.bass_utils import run_bass_kernel_spmd

    nc = bacc.Bacc("TRN2", target_bir_lowering=False, num_devices=1)
    kept, cst_at, dft, moe, rel = build_constants()
    arrays = {n: np.ascontiguousarray(inputs[n]) for n in INPUTS}
    arrays.update(c_kept=kept, c_dft=dft, c_moe=moe, c_rel=rel)
    handles = {n: nc.dram_tensor("in_" + n, v.shape, mybir.dt.from_np(v.dtype), kind="ExternalInput").ap()
               for n, v in arrays.items()}
    out = nc.dram_tensor("out", (1, T, D), F32, kind="ExternalOutput").ap()
    program(nc, handles, cst_at, out)
    r = run_bass_kernel_spmd(nc, [{"in_" + n: v for n, v in arrays.items()}], core_ids=[0])
    return r.results[0]["out"]
```
